# Optimizing a Trainium2 kernel written in Bass

```python
import math
import jax, jax.numpy as jnp
from jax import lax
import numpy as np

D_MODEL = 1024
BATCH = 1
SEQ = 256
DEPTH = 2

N_MIXERS = 4
D_FF = 2816
BLOCK = 128
LN_EPS = 1e-5
RMS_EPS = 1e-6
NEG = -1e30

SWA_HEADS = 16
SWA_KV_HEADS = 4
SWA_HEAD_DIM = 64
SWA_WINDOW = 128

MLA_HEADS = 16
MLA_Q_LORA = 768
MLA_KV_LORA = 256
MLA_NOPE = 64
MLA_ROPE = 32
MLA_V = 64
ROPE_THETA = 10000.0

DSA_HEADS = 16
DSA_KV_HEADS = 4
DSA_HEAD_DIM = 64
IDX_HEADS = 8
IDX_DIM = 64
IDX_TOPK = 256

SB_HEADS = 16
SB_HEAD_DIM = 64

ALPHA = (2.0 * DEPTH) ** 0.25
BETA = (8.0 * DEPTH) ** -0.25

kernel_name = "interleaved_hybrid_swa_mla_dsa_stickbreak_macaron"

def layer_norm(x, g, b):
    xf = x.astype(jnp.float32)
    mu = jnp.mean(xf, axis=-1, keepdims=True)
    var = jnp.mean(jnp.square(xf - mu), axis=-1, keepdims=True)
    return ((xf - mu) * lax.rsqrt(var + LN_EPS) * g.astype(jnp.float32) + b.astype(jnp.float32)).astype(x.dtype)

def rms_norm(x, g):
    xf = x.astype(jnp.float32)
    ms = jnp.mean(jnp.square(xf), axis=-1, keepdims=True)
    return (xf * lax.rsqrt(ms + RMS_EPS) * g.astype(jnp.float32)).astype(x.dtype)

def swiglu(x, w_gu, w_down):
    gate, up = jnp.split(x @ w_gu, 2, axis=-1)
    return (jax.nn.silu(gate) * up) @ w_down

def alibi_slopes(n_heads):
    return np.array([2.0 ** (-8.0 * (i + 1) / n_heads) for i in range(n_heads)], dtype=np.float32)

def rope(x, pos):
    d = x.shape[-1]
    inv = ROPE_THETA ** (-jnp.arange(0, d, 2, dtype=jnp.float32) / d)
    ang = pos.astype(jnp.float32)[:, None] * inv[None, :]
    cos = jnp.cos(ang)[None, :, None, :].astype(x.dtype)
    sin = jnp.sin(ang)[None, :, None, :].astype(x.dtype)
    x1, x2 = jnp.split(x, 2, axis=-1)
    return jnp.concatenate([x1 * cos - x2 * sin, x1 * sin + x2 * cos], axis=-1)

def to_blocks(a):
    b, s = a.shape[0], a.shape[1]
    return jnp.swapaxes(a.reshape(b, s // BLOCK, BLOCK, *a.shape[2:]), 0, 1)

def from_blocks(a):
    a = jnp.swapaxes(a, 0, 1)
    return a.reshape(a.shape[0], a.shape[1] * a.shape[2], *a.shape[3:])

def swa_sink_attention(x, w_in, sinks, w_o):
    B, S, _ = x.shape
    H, KV, dh = SWA_HEADS, SWA_KV_HEADS, SWA_HEAD_DIM
    G = H // KV
    nb = S // BLOCK
    q, k, v = jnp.split(x @ w_in, [H * dh, H * dh + KV * dh], axis=-1)
    q = q.reshape(B, nb, BLOCK, KV, G, dh)
    k = k.reshape(B, nb, BLOCK, KV, dh)
    v = v.reshape(B, nb, BLOCK, KV, dh)
    k_prev = jnp.concatenate([jnp.zeros_like(k[:, :1]), k[:, :-1]], axis=1)
    v_prev = jnp.concatenate([jnp.zeros_like(v[:, :1]), v[:, :-1]], axis=1)
    kb = jnp.concatenate([k_prev, k], axis=2)
    vb = jnp.concatenate([v_prev, v], axis=2)
    s = jnp.einsum('bnqgrd,bnkgd->bngrqk', q, kb).astype(jnp.float32) * (dh ** -0.5)
    qi = jnp.arange(BLOCK)[:, None]
    kj = jnp.arange(2 * BLOCK)[None, :]
    dist = qi + BLOCK - kj
    band = (dist >= 0) & (dist < SWA_WINDOW)
    valid = band[None] & ((jnp.arange(nb)[:, None, None] > 0) | (kj[None] >= BLOCK))
    slopes = alibi_slopes(H).reshape(KV, G)
    s = s - slopes[:, :, None, None] * dist.astype(jnp.float32)
    s = jnp.where(valid[None, :, None, None], s, NEG)
    sink = jnp.broadcast_to(sinks.astype(jnp.float32).reshape(KV, G)[None, None, :, :, None, None],
                            s.shape[:-1] + (1,))
    p = jax.nn.softmax(jnp.concatenate([s, sink], axis=-1), axis=-1)[..., :-1]
    o = jnp.einsum('bngrqk,bnkgd->bnqgrd', p.astype(vb.dtype), vb)
    return o.reshape(B, S, H * dh) @ w_o

def mla_attention(x, w_in, q_norm_g, w_uq, kv_norm_g, w_ukv, w_o):
    B, S, _ = x.shape
    H = MLA_HEADS
    c_q, c_kv, k_rope = jnp.split(x @ w_in, [MLA_Q_LORA, MLA_Q_LORA + MLA_KV_LORA], axis=-1)
    c_q = rms_norm(c_q, q_norm_g)
    c_kv = rms_norm(c_kv, kv_norm_g)
    pos = jnp.arange(S)
    q = (c_q @ w_uq).reshape(B, S, H, MLA_NOPE + MLA_ROPE)
    q_nope, q_rope = jnp.split(q, [MLA_NOPE], axis=-1)
    q_rope = rope(q_rope, pos)
    k_rope = rope(k_rope[:, :, None, :], pos)[:, :, 0, :]
    kv = (c_kv @ w_ukv).reshape(B, S, H, MLA_NOPE + MLA_V)
    k_nope, v = jnp.split(kv, [MLA_NOPE], axis=-1)
    scale = (MLA_NOPE + MLA_ROPE) ** -0.5
    nb = S // BLOCK
    key_pos = jnp.arange(S)

    def block_fn(args):
        qn, qr, bi = args
        s = (jnp.einsum('bqhd,bkhd->bhqk', qn, k_nope)
             + jnp.einsum('bqhd,bkd->bhqk', qr, k_rope)).astype(jnp.float32) * scale
        tq = bi * BLOCK + jnp.arange(BLOCK)
        s = jnp.where(tq[:, None] >= key_pos[None, :], s, NEG)
        p = jax.nn.softmax(s, axis=-1).astype(v.dtype)
        return jnp.einsum('bhqk,bkhd->bqhd', p, v)

    o = lax.map(block_fn, (to_blocks(q_nope), to_blocks(q_rope), jnp.arange(nb)))
    return from_blocks(o).reshape(B, S, H * MLA_V) @ w_o

def dsa_attention(x, w_in, w_o):
    B, S, _ = x.shape
    H, KV, dh = DSA_HEADS, DSA_KV_HEADS, DSA_HEAD_DIM
    G = H // KV
    topk = min(IDX_TOPK, S // 4)
    sizes = [H * dh, KV * dh, KV * dh, IDX_HEADS * IDX_DIM, IDX_DIM]
    cuts = np.cumsum(sizes).tolist()
    q, k, v, q_idx, k_idx, w_idx = jnp.split(x @ w_in, cuts, axis=-1)
    q = q.reshape(B, S, KV, G, dh)
    k = k.reshape(B, S, KV, dh)
    v = v.reshape(B, S, KV, dh)
    q_idx = q_idx.reshape(B, S, IDX_HEADS, IDX_DIM)
    w_idx = w_idx * (IDX_HEADS ** -0.5)
    slopes = alibi_slopes(H).reshape(KV, G)
    key_pos = jnp.arange(S)
    nb = S // BLOCK
    gather = jax.vmap(lambda kk, ii: kk[ii])

    def block_fn(args):
        qb, qib, wib, bi = args
        tq = bi * BLOCK + jnp.arange(BLOCK)
        dots = jnp.einsum('bqhd,bkd->bqhk', qib, k_idx).astype(jnp.float32) * (IDX_DIM ** -0.5)
        score = jnp.einsum('bqh,bqhk->bqk', wib.astype(jnp.float32), jax.nn.relu(dots))
        score = jnp.where(tq[None, :, None] >= key_pos[None, None, :], score, NEG)
        _, idx = lax.top_k(score, topk)
        sel_ok = idx <= tq[None, :, None]
        k_sel = gather(k, idx)
        v_sel = gather(v, idx)
        s = jnp.einsum('bqgrd,bqkgd->bgrqk', qb, k_sel).astype(jnp.float32) * (dh ** -0.5)
        dist = (tq[None, :, None] - idx).astype(jnp.float32)
        s = s - slopes[None, :, :, None, None] * dist[:, None, None]
        s = jnp.where(sel_ok[:, None, None], s, NEG)
        p = jax.nn.softmax(s, axis=-1).astype(v_sel.dtype)
        return jnp.einsum('bgrqk,bqkgd->bqgrd', p, v_sel)

    o = lax.map(block_fn, (to_blocks(q), to_blocks(q_idx), to_blocks(w_idx), jnp.arange(nb)))
    return from_blocks(o).reshape(B, S, H * dh) @ w_o

def stick_breaking_attention(x, w_in, w_o):
    B, S, _ = x.shape
    H, dh = SB_HEADS, SB_HEAD_DIM
    q, k, v = jnp.split(x @ w_in, 3, axis=-1)
    q = q.reshape(B, S, H, dh)
    k = k.reshape(B, S, H, dh)
    v = v.reshape(B, S, H, dh)
    key_pos = jnp.arange(S)
    nb = S // BLOCK

    def block_fn(args):
        qb, bi = args
        tq = bi * BLOCK + jnp.arange(BLOCK)
        z = jnp.einsum('bqhd,bkhd->bhqk', qb, k).astype(jnp.float32) * (dh ** -0.5)
        strict = key_pos[None, :] < tq[:, None]
        log_1m = jnp.where(strict, jax.nn.log_sigmoid(-z), 0.0)
        between = lax.cumsum(log_1m, axis=3, reverse=True) - log_1m
        a = jnp.where(strict, jnp.exp(jax.nn.log_sigmoid(z) + between), 0.0)
        return jnp.einsum('bhqk,bkhd->bqhd', a.astype(v.dtype), v)

    o = lax.map(block_fn, (to_blocks(q), jnp.arange(nb)))
    return from_blocks(o).reshape(B, S, H * dh) @ w_o

def _n_layers_of(m):
    return (DEPTH - m + N_MIXERS - 1) // N_MIXERS

def setup_inputs(seed: int = 0) -> dict:
    key = jax.random.key(seed)
    ks = iter(jax.random.split(key, 32))

    def dense(shape, fan_in, scale=1.0):
        return jax.random.normal(next(ks), shape, jnp.float32) * (scale * fan_in ** -0.5)

    def gain(shape):
        return 1.0 + 0.02 * jax.random.normal(next(ks), shape, jnp.float32)

    nA, nB, nC, nD = (_n_layers_of(m) for m in range(N_MIXERS))
    D = D_MODEL
    a_in = (SWA_HEADS + 2 * SWA_KV_HEADS) * SWA_HEAD_DIM
    b_in = MLA_Q_LORA + MLA_KV_LORA + MLA_ROPE
    c_in = (DSA_HEADS + 2 * DSA_KV_HEADS) * DSA_HEAD_DIM + IDX_HEADS * IDX_DIM + IDX_DIM + IDX_HEADS
    d_in = 3 * SB_HEADS * SB_HEAD_DIM
    return {
        "x": jax.random.normal(next(ks), (BATCH, SEQ, D), jnp.float32),
        "ffn1_w_gu": dense((DEPTH, D, 2 * D_FF), D),
        "ffn1_w_down": dense((DEPTH, D_FF, D), D_FF, BETA),
        "ffn2_w_gu": dense((DEPTH, D, 2 * D_FF), D),
        "ffn2_w_down": dense((DEPTH, D_FF, D), D_FF, BETA),
        "ln_g": gain((DEPTH, 3, D)),
        "ln_b": 0.02 * jax.random.normal(next(ks), (DEPTH, 3, D), jnp.float32),
        "a_w_in": dense((nA, D, a_in), D),
        "a_sinks": jax.random.normal(next(ks), (nA, SWA_HEADS), jnp.float32),
        "a_w_o": dense((nA, SWA_HEADS * SWA_HEAD_DIM, D), SWA_HEADS * SWA_HEAD_DIM, BETA),
        "b_w_in": dense((nB, D, b_in), D),
        "b_q_norm": gain((nB, MLA_Q_LORA)),
        "b_w_uq": dense((nB, MLA_Q_LORA, MLA_HEADS * (MLA_NOPE + MLA_ROPE)), MLA_Q_LORA),
        "b_kv_norm": gain((nB, MLA_KV_LORA)),
        "b_w_ukv": dense((nB, MLA_KV_LORA, MLA_HEADS * (MLA_NOPE + MLA_V)), MLA_KV_LORA),
        "b_w_o": dense((nB, MLA_HEADS * MLA_V, D), MLA_HEADS * MLA_V, BETA),
        "c_w_in": dense((nC, D, c_in), D),
        "c_w_o": dense((nC, DSA_HEADS * DSA_HEAD_DIM, D), DSA_HEADS * DSA_HEAD_DIM, BETA),
        "d_w_in": dense((nD, D, d_in), D),
        "d_w_o": dense((nD, SB_HEADS * SB_HEAD_DIM, D), SB_HEADS * SB_HEAD_DIM, BETA),
    }

def reference(x, ffn1_w_gu, ffn1_w_down, ffn2_w_gu, ffn2_w_down, ln_g, ln_b,
              a_w_in, a_sinks, a_w_o,
              b_w_in, b_q_norm, b_w_uq, b_kv_norm, b_w_ukv, b_w_o,
              c_w_in, c_w_o, d_w_in, d_w_o):
    for i in range(DEPTH):
        m, j = i % N_MIXERS, i // N_MIXERS
        x = layer_norm(ALPHA * x + 0.5 * swiglu(x, ffn1_w_gu[i], ffn1_w_down[i]), ln_g[i, 0], ln_b[i, 0])
        if m == 0:
            y = swa_sink_attention(x, a_w_in[j], a_sinks[j], a_w_o[j])
        elif m == 1:
            y = mla_attention(x, b_w_in[j], b_q_norm[j], b_w_uq[j], b_kv_norm[j], b_w_ukv[j], b_w_o[j])
        elif m == 2:
            y = dsa_attention(x, c_w_in[j], c_w_o[j])
        else:
            y = stick_breaking_attention(x, d_w_in[j], d_w_o[j])
        x = layer_norm(ALPHA * x + y, ln_g[i, 1], ln_b[i, 1])
        x = layer_norm(ALPHA * x + 0.5 * swiglu(x, ffn2_w_gu[i], ffn2_w_down[i]), ln_g[i, 2], ln_b[i, 2])
    return x


_drawn_inputs = setup_inputs


def setup_inputs(seed=0):
    import zlib

    import numpy as np

    out = dict(_drawn_inputs(seed))
    spreads = {}
    factors = {'a_sinks': 4.178, 'b_q_norm': 8.0, 'b_kv_norm': 8.0}
    for name, (base, spread) in spreads.items():
        noise = np.random.default_rng([zlib.crc32(name.encode()), seed]).standard_normal(out[name].shape)
        drawn = base * np.exp(spread * noise) if base else spread * noise
        out[name] = __import__('jax').numpy.asarray(drawn.astype(out[name].dtype))
    for name, factor in factors.items():
        out[name] = (out[name] * factor).astype(out[name].dtype)
    return out
```

```python
from contextlib import ExitStack

import numpy as np

import concourse.bass as bass
from concourse import mybir

F32 = mybir.dt.float32
F32R = mybir.dt.float32r
ALU = mybir.AluOpType
ACT = mybir.ActivationFunctionType

P = 128
D = 1024
S = 256
NT = S // P
KD = D // P
FF = 2816
NFT = FF // P
NFI = NFT // 2
ALPHA = (2.0 * 2) ** 0.25
LN_EPS, RMS_EPS, NEG = 1e-5, 1e-6, -1e30
HEADS, KV_HEADS, DH = 16, 4, 64
QLORA, KVLORA, NOPE, ROPE = 768, 256, 64, 32
HR = ROPE // 2
QW = NOPE + ROPE
QUADS = HEADS // 4
WIN_SCALE = DH ** -0.5
MLA_SCALE = QW ** -0.5

RAW_SLOTS, SPLIT_SLOTS, LOOKAHEAD, CH = 3, 6, 3, 2048

G_COL, B_COL, QN_COL, KVN_COL, N_COL = 0, 48, 96, 102, 104

FFN_CHUNKS = 3 * NFI
A_CHUNKS, B_CHUNKS, O_CHUNKS = 2 + QUADS, 5 + 2 + 2 * QUADS, KD // 2
FFN0 = 0
A0 = FFN0 + FFN_CHUNKS
AO = A0 + A_CHUNKS
FFN1 = AO + O_CHUNKS
FFN2 = FFN1 + FFN_CHUNKS
B0 = FFN2 + FFN_CHUNKS
BU = B0 + 5
BQ = BU + 2
BO = BQ + 2 * QUADS
FFN3 = BO + O_CHUNKS
CHUNKS = FFN3 + FFN_CHUNKS
FFN_BASE = [FFN0, FFN1, FFN2, FFN3]
assert BQ % 2 == 0

FFN_LN = [0, 2, 3, 5]
A_LN, B_LN = 1, 4
LNS = 6

T_X = 0
T_LN = {0: 4, 1: 12, 2: 16, 3: 20, 4: 32}
T_AO, T_CKV, T_CQ, T_BO = 8, 24, 25, 28
LN_BANKS, O_BANKS = [2, 3, 4, 5], [2, 3, 0, 1]
CQ_BANKS = [4, 5, 2]

NAT_ORDER = ["ckv", "cq0", "cq1", "kr", "cq2"]
NAT_BANK = {"ckv": 7, "cq0": 6, "cq1": 2, "kr": 3, "cq2": 1}


def trunk_kernel(nc, x, ffn1_w_gu, ffn1_w_down, ffn2_w_gu, ffn2_w_down, ln_g, ln_b,
                 a_w_in, a_sinks, a_w_o, b_w_in, b_q_norm, b_w_uq, b_kv_norm, b_w_ukv, b_w_o,
                 identity, window, causal, rope_tab, out):
    with ExitStack() as ctx:
        def sb(name, shape, dt=F32):
            return ctx.enter_context(nc.sbuf_tensor(name, shape, dt))

        def sem(name):
            return ctx.enter_context(nc.semaphore(name))

        raw = sb("raw", [P, RAW_SLOTS, CH])
        hi = sb("hi", [P, SPLIT_SLOTS, CH], F32R)
        lo = sb("lo", [P, SPLIT_SLOTS, CH], F32R)
        x_nat = sb("x_nat", [P, NT, D])
        r = sb("r", [P, NT, D])
        xT_hi = sb("xT_hi", [P, KD, S], F32R)
        xT_lo = sb("xT_lo", [P, KD, S], F32R)
        h_hi = sb("h_hi", [P, 2, S], F32R)
        h_lo = sb("h_lo", [P, 2, S], F32R)
        work = sb("work", [P, 5120])
        kv = sb("kv", [P, 6144])
        ident = sb("ident", [P, P])
        window_s = sb("window_s", [P, 2 * P])
        causal_s = sb("causal_s", [P, 2 * P])
        rope_s = sb("rope_s", [P, NT, 2, HR])
        cols = sb("cols", [P, N_COL])
        nsink = sb("nsink", [P, HEADS])
        bn = sb("bn", [P, NT, 2, 6])
        mv = sb("mv", [P, NT, 2])
        inv_v = sb("inv_v", [P, NT])
        inv_l = sb("inv_l", [P, NT])
        inv_e = sb("inv_e", [P, NT])
        inv_t = sb("inv_t", [P, NT])
        rstd = sb("rstd", [P, NT])
        smax = sb("smax", [P, NT, 4])
        negm = sb("negm", [P, NT, 4])
        rsum = sb("rsum", [P, NT, 4])
        esink = sb("esink", [P, NT, 4])
        rden = sb("rden", [P, NT, 4])
        msq = sb("msq", [P, 2, NT])
        rope_t = sb("rope_t", [P, 2, NT, 4, HR])
        qr_nat = sb("qr_nat", [P, NT, 4, ROPE])
        kr_nat = sb("kr_nat", [P, NT, ROPE])

        gb = work[:, 0:2 * D].rearrange("p (a d) -> p a d", a=2)
        sil = work[:, 2048:2560].rearrange("p (a n) -> p a n", a=2)
        hf = work[:, 2560:3072].rearrange("p (a n) -> p a n", a=2)
        xf = work[:, 4096:5120].rearrange("p (a k n) -> p a k n", a=2, k=2)
        prow = work[:, 0:P]
        qh = work[:, 0:2048].rearrange("p (a h n) -> p a h n", a=2, h=4)
        pT = work[:, 2048:3584].rearrange("p (i n) -> p i n", i=12)
        sc = work[:, 3584:5120].rearrange("p (h n) -> p h n", h=4)
        c_nat = work[:, 2048:4096].rearrange("p (t d) -> p t d", t=NT)
        alibi = kv[:, 0:4096].rearrange("p (h n) -> p h n", h=HEADS)
        khA = kv[:, 4096:5120].rearrange("p (h n) -> p h n", h=KV_HEADS)
        vA = kv[:, 5120:5632].rearrange("p (t d) -> p t d", t=NT)
        khB = kv[:, 0:4096].rearrange("p (h n) -> p h n", h=HEADS)
        junk = kv[:, 0:NT * QLORA].rearrange("p (t d) -> p t d", t=NT)
        vB = kv[:, 4096:6144].rearrange("p (t d) -> p t d", t=NT)

        W = ctx.enter_context(nc.psum_tensor("banks", [P, 8, 512], F32))

        raw_in = [sem(f"raw_in{i}") for i in range(RAW_SLOTS)]
        hi_done = sem("hi_done")
        lo_done = sem("lo_done")
        x_in = sem("x_in")
        rows_in = sem("rows_in")
        const_in = sem("const_in")
        gb_in = sem("gb_in")
        cols_tr = sem("cols_tr")
        cols_ready = sem("cols_ready")
        alibi_ready = sem("alibi_ready")
        sink_neg = sem("sink_neg")
        gu_ready = sem("gu_ready")
        sil_ready = sem("sil_ready")
        hf_ready = sem("hf_ready")
        hhi_ready = sem("hhi_ready")
        hlo_ready = sem("hlo_ready")
        d_done = sem("d_done")
        y_ready = sem("y_ready")
        ln_step = sem("ln_step")
        isq_dve = sem("isq_dve")
        isq_act = sem("isq_act")
        xhat_ready = sem("xhat_ready")
        pool_step = sem("pool_step")
        x_ready = sem("x_ready")
        fin_step = sem("fin_step")
        out_ready = sem("out_ready")
        out_done = sem("out_done")
        tr_ready = sem("tr_ready")
        xf_dve = sem("xf_dve")
        xf_act = sem("xf_act")
        thi_ready = sem("thi_ready")
        tlo_ready = sem("tlo_ready")
        k_psum, k_lower, k_upper = sem("k_psum"), sem("k_lower"), sem("k_upper")
        v_psum, v_out0, v_out1 = sem("v_psum"), sem("v_out0"), sem("v_out1")
        q_psum, q_lower, q_upper = sem("q_psum"), sem("q_lower"), sem("q_upper")
        s_psum = sem("s_psum")
        s_masked = sem("s_masked")
        negm_ready = sem("negm_ready")
        es_arg = sem("es_arg")
        es_ready = sem("es_ready")
        p_ready = sem("p_ready")
        pt_psum = sem("pt_psum")
        pt_dve, pt_act = sem("pt_dve"), sem("pt_act")
        den_step = sem("den_step")
        o_psum = sem("o_psum")
        o_out = sem("o_out")
        wo_done = sem("wo_done")
        nat_psum = sem("nat_psum")
        nat_out = sem("nat_out")
        msq_ready = sem("msq_ready")
        c_norm = sem("c_norm")
        rope_step = sem("rope_step")
        krt_psum = sem("krt_psum")
        kr_first = sem("kr_first")
        kr_all = sem("kr_all")
        qr_psum = sem("qr_psum")
        qr_ready = sem("qr_ready")
        qrt_psum = sem("qrt_psum")
        qr_act, qr_dve = sem("qr_act"), sem("qr_dve")

        def consumed(n):
            for f, base in enumerate(FFN_BASE):
                if base <= n < base + FFN_CHUNKS:
                    i, c = divmod(n - base, 3)
                    if c < 2:
                        return gu_ready, NFT * f + 2 * i + 2
                    if i < NFI - 1:
                        return d_done, (NFT - 1) * f + 2 * i + 2
                    return y_ready, NT * (FFN_LN[f] + 1)
            if n == A0:
                return k_psum, 1
            if n == A0 + 1:
                return v_psum, 1
            if n < AO:
                return q_psum, n - A0 - 1
            if n < FFN1:
                return (wo_done, n - AO + 1) if n < FFN1 - 1 else (y_ready, NT * (A_LN + 1))
            if n < BU:
                return nat_psum, n - B0 + 1
            if n < BQ:
                return v_psum, 1 + 2 * (n - BU + 1)
            if n < BO:
                return qr_psum, (n - BQ) // 2 + 1
            return (wo_done, O_CHUNKS - 1 + n - BO + 1) if n < FFN3 - 1 else (y_ready, NT * (B_LN + 1))

        def size(n):
            if n == B0 + NAT_ORDER.index("kr"):
                return KD * ROPE
            if BQ <= n < BO:
                return (QLORA // P) * 2 * QW
            return CH

        def parts(n, at):
            m, split = size(n), at[0] is not raw
            row = at[0][:, at[1], 0:m]
            if BU <= n < BQ:
                how = "p (k a h d) -> p k a h d" if split else "p (k h a d) -> p k a h d"
                v = row.rearrange(how, a=2, d=DH, k=KVLORA // P)
                return [v[:, k, :, :, :] for k in range(KVLORA // P)]
            if BQ <= n < BO:
                v = row.rearrange("p (k c) -> p k c", k=QLORA // P)
                if split:
                    return [v[:, :, 0:2 * NOPE].rearrange("p k (h d) -> p k h d", h=2),
                            v[:, :, 2 * NOPE:2 * QW].rearrange("p k (h d) -> p k h d", h=2)]
                v = v.rearrange("p k (h c) -> p k h c", h=2)
                return [v[:, :, :, 0:NOPE], v[:, :, :, NOPE:QW]]
            return [row]

        block = ctx.enter_context(nc.Block())

        @block.sync
        def _(sp):
            def place(n, sl):
                def cols_of(w, k, a, width):
                    return w.rearrange("(k p) f -> p k f", p=P)[:, :, a:a + width], "p (k f) -> p k f", k

                if n < AO:
                    w = a_w_in[0]
                    c = n - A0
                    a = {0: D, 1: D + KV_HEADS * DH}[c] if c < 2 else (c - 2) * 4 * DH
                    src, how, k = cols_of(w, KD, a, 4 * DH)
                elif n < FFN1 or BO <= n < FFN3:
                    w, c = (a_w_o, n - AO) if n < FFN1 else (b_w_o, n - BO)
                    src = w[0].rearrange("(k p) f -> p k f", p=P)[:, 2 * c:2 * c + 2, :]
                    how, k = "p (k f) -> p k f", 2
                elif n < BU:
                    part = NAT_ORDER[n - B0]
                    a, wd = {"ckv": (QLORA, KVLORA), "kr": (QLORA + KVLORA, ROPE)}.get(
                        part, (256 * int(part[2]) if part[0:2] == "cq" else 0, 256))
                    src, how, k = cols_of(b_w_in[0], KD, a, wd)
                elif n < BQ:
                    src, how, k = cols_of(b_w_ukv[0], KVLORA // P, (n - BU) * D, D)
                else:
                    src, how, k = cols_of(b_w_uq[0], QLORA // P, (n - BQ) * 2 * QW, 2 * QW)
                return src, raw[:, sl, 0:size(n)].rearrange(how, k=k)

            def load(n):
                if n >= RAW_SLOTS:
                    sp.wait_ge(lo_done, n - RAW_SLOTS + 1)
                src, dst = place(n, n % RAW_SLOTS)
                sp.dma_start(dst, src).then_inc(raw_in[n % RAW_SLOTS], 16)

            def load_ffn(f, i, n, p=None):
                w_gu = (ffn1_w_gu, ffn2_w_gu)[f % 2][f // 2].rearrange("(k p) f -> p k f", p=P)
                w_d = (ffn1_w_down, ffn2_w_down)[f % 2][f // 2].rearrange("(i j p) f -> i p j f", p=P, j=2)
                for c in range(3):
                    if n + c >= RAW_SLOTS:
                        more = 0 if p is None else 6 * p
                        sp.wait_ge(lo_done, n + c - RAW_SLOTS + 1 + more)
                    sl = (n + c) % RAW_SLOTS
                    if c < 2:
                        at = c * FF + 256 * i if p is None else 512 * p + (c * FF + 256 * i)
                        src = w_gu[:, :, bass.ds(at, 256)]
                        dst = raw[:, sl, :].rearrange("p (k f) -> p k f", k=KD)
                    else:
                        src = w_d[i] if p is None else w_d[bass.ds(2 * p + i, 1)].rearrange("a p j f -> (a p) j f")
                        dst = raw[:, sl, :].rearrange("p (k f) -> p k f", k=2)
                    sp.dma_start(dst, src).then_inc(raw_in[sl], 16)

            def load_gb(l):
                for a, w in enumerate((ln_g, ln_b)):
                    sp.dma_start(gb[:, a, :], w[l // 3, l % 3:l % 3 + 1, :].to_broadcast([P, D])).then_inc(gb_in, 16)

            def ffn_loads(f):
                base = FFN_BASE[f]
                load_ffn(f, 0, base)
                with sp.Fori(0, NFI // 2) as p:
                    load_ffn(f, 1, base + 3, p)
                    load_ffn(f, 2, base + 6, p)

            sp.dma_start(ident[:, :], identity).then_inc(const_in, 16)
            sp.dma_start(x_nat[:, :, :], x[0].rearrange("(t p) d -> p t d", p=P)).then_inc(x_in, 16)
            for w, at, n in ((ln_g, G_COL, 48), (ln_b, B_COL, 48)):
                sp.dma_start(prow[at:at + n, :], w.rearrange("a b (k p) -> (a b k) p", p=P)).then_inc(rows_in, 16)
            sp.dma_start(prow[QN_COL:QN_COL + 6, :], b_q_norm.rearrange("a (k p) -> (a k) p", p=P)).then_inc(rows_in, 16)
            sp.dma_start(prow[KVN_COL:KVN_COL + 2, :], b_kv_norm.rearrange("a (k p) -> (a k) p", p=P)).then_inc(rows_in, 16)
            load_ffn(0, 0, 0)
            sp.dma_start(window_s[:, :], window).then_inc(const_in, 16)
            sp.dma_start(causal_s[:, :], causal).then_inc(const_in, 16)
            sp.dma_start(rope_s[:, :, :, :], rope_tab.rearrange("(t p) a c -> p t a c", p=P)).then_inc(const_in, 16)
            sp.dma_start(nsink[:, :], a_sinks.to_broadcast([P, HEADS])).then_inc(const_in, 16)
            sp.wait_ge(cols_ready, 1)
            load_gb(0)
            with sp.Fori(0, NFI // 2) as p:
                load_ffn(0, 1, 3, p)
                load_ffn(0, 2, 6, p)
            for n in range(A0, AO + 3):
                load(n)
            sp.wait_ge(s_psum, 3 * QUADS)
            load_gb(A_LN)
            for n in range(AO + 3, FFN1):
                load(n)
            load_ffn(1, 0, FFN1)
            sp.wait_ge(x_ready, NT * (A_LN + 1))
            load_gb(FFN_LN[1])
            with sp.Fori(0, NFI // 2) as p:
                load_ffn(1, 1, FFN1 + 3, p)
                load_ffn(1, 2, FFN1 + 6, p)
            load_ffn(2, 0, FFN2)
            sp.wait_ge(x_ready, NT * (FFN_LN[1] + 1))
            load_gb(FFN_LN[2])
            with sp.Fori(0, NFI // 2) as p:
                load_ffn(2, 1, FFN2 + 3, p)
                load_ffn(2, 2, FFN2 + 6, p)
            for n in range(B0, BO + 3):
                load(n)
            sp.wait_ge(s_psum, 6 * QUADS)
            load_gb(B_LN)
            for n in range(BO + 3, FFN3):
                load(n)
            load_ffn(3, 0, FFN3)
            sp.wait_ge(x_ready, NT * (B_LN + 1))
            load_gb(FFN_LN[3])
            with sp.Fori(0, NFI // 2) as p:
                load_ffn(3, 1, FFN3 + 3, p)
                load_ffn(3, 2, FFN3 + 6, p)
            out_v = out[0].rearrange("(t p) d -> p t d", p=P)
            for t in range(NT):
                sp.wait_ge(out_ready, t + 1)
                sp.dma_start(out_v[:, t, :], r[:, t, :]).then_inc(out_done, 16)
            sp.wait_ge(out_done, 16 * NT)

        @block.gpsimd
        def _(pool):
            pool.wait_ge(const_in, 16 * 5)
            for h in range(HEADS):
                slope = 2.0 ** (-8.0 * (h + 1) / HEADS) / WIN_SCALE
                a = nc.gpsimd.tensor_scalar(alibi[:, h, :], window_s[:, :], slope, None, ALU.mult)
            a.then_inc(alibi_ready, 1)
            nc.gpsimd.tensor_scalar(nsink[:, :], nsink[:, :], -1.0, None, ALU.mult).then_inc(sink_neg, 1)

            def rebuild_x(l):
                pool.wait_ge(gb_in, 32 * (l + 1))
                for t in range(NT):
                    pool.wait_ge(xhat_ready, NT * l + t + 1)
                    nc.gpsimd.tensor_tensor(x_nat[:, t, :], r[:, t, :], gb[:, 0, :], ALU.mult).then_inc(pool_step, 1)
                    pool.wait_ge(pool_step, NT * l + t + 1)
                    nc.gpsimd.tensor_tensor(x_nat[:, t, :], x_nat[:, t, :], gb[:, 1, :], ALU.add).then_inc(x_ready, 1)

            for l in range(B_LN):
                rebuild_x(l)
            pool.wait_ge(x_ready, NT * B_LN)
            pool.wait_ge(kr_first, 1)
            src = khB[NOPE:QW, 0:1, :].to_broadcast([ROPE, HEADS - 1, S])
            nc.gpsimd.tensor_copy(khB[NOPE:QW, 1:HEADS, :], src).then_inc(kr_all, 1)
            pool.wait_ge(kr_all, 1)
            rebuild_x(B_LN)

        @block.tensor
        def _(pe):
            def mm3(dst, a_hi, a_lo, b_hi, b_lo, first, last):
                pe.matmul(dst, a_hi, b_hi, start=first, stop=False)
                pe.matmul(dst, a_hi, b_lo, start=False, stop=False)
                return pe.matmul(dst, a_lo, b_hi, start=False, stop=last)

            def weights(sl, a, n):
                return hi[:, sl, a:a + n], lo[:, sl, a:a + n]

            def transpose_pairs(src, tiles, banks, waits):
                for t in range(NT):
                    waits(t)
                    for k in range(tiles):
                        tr = pe.transpose(W[:, banks[k // 2], (k % 2) * S + t * P:(k % 2) * S + (t + 1) * P],
                                          src(t, k), ident[:, :])
                        if t == NT - 1 and k % 2:
                            tr.then_inc(tr_ready, 1)

            def after_ln(l):
                transpose_pairs(lambda t, k: r[:, t, k * P:(k + 1) * P], KD, LN_BANKS,
                                lambda t: pe.wait_ge(xhat_ready, NT * l + t + 1))

            def gate_up(f, t, sl, n, tp=0, np_=0, pairs=None):
                if isinstance(t, int) and t < 2:
                    pass
                else:
                    pe.wait_ge(hf_ready, NFT * f + t - 1 + tp)
                for half in range(2):
                    pe.wait_ge(lo_done, n + half + 1 + np_)
                    for k in range(KD):
                        if pairs is not None and half == 0 and k % 2 == 0:
                            pe.wait_ge(tlo_ready, pairs + k // 2 + 1)
                        wh, wl = weights(sl[half], k * 256 + (t % 2) * P, P)
                        mm = mm3(W[:, t % 2, half * S:(half + 1) * S], wh, wl, xT_hi[:, k, :], xT_lo[:, k, :],
                                 k == 0, k == KD - 1)
                mm.then_inc(gu_ready, 1)

            def down(f, t, sl, n, first, last, tp=0, np_=0):
                pe.wait_ge(hlo_ready, NFT * f + t + 1 + tp)
                pe.wait_ge(lo_done, n + 1 + np_)
                for tt in range(NT):
                    for c in range(2):
                        wh, wl = weights(sl, (t % 2) * D + c * 512, 512)
                        mm = mm3(W[:, 4 + 2 * tt + c, :], h_hi[:, t % 2, tt * P:(tt + 1) * P],
                                 h_lo[:, t % 2, tt * P:(tt + 1) * P], wh, wl, first, last)
                    if last:
                        mm.then_inc(y_ready, 1)
                if not last:
                    mm.then_inc(d_done, 1)

            def ffn(f, pairs):
                base = FFN_BASE[f]

                def step(i, p=None):
                    n = base + 3 * i
                    tp, np_ = (0, 0) if p is None else (4 * p, 6 * p)
                    s0 = [(n + c) % SPLIT_SLOTS for c in range(3)]
                    gate_up(f, 2 * i, s0, n, tp, np_, pairs if i == 0 else None)
                    if i:
                        down(f, 2 * i - 1, (n - 1) % SPLIT_SLOTS, n - 1, False, False, tp, np_)
                    gate_up(f, 2 * i + 1, s0, n, tp, np_)
                    down(f, 2 * i, s0[2], n + 2, i == 0, False, tp, np_)

                step(0)
                with pe.Fori(0, NFI // 2) as p:
                    step(1, p)
                    step(2, p)
                n = base + FFN_CHUNKS - 1
                down(f, NFT - 1, n % SPLIT_SLOTS, n, False, True)

            def two_tiles(n, width, at, kt, ah, al, bank, wait=None):
                for j in range(2):
                    for k in range(kt):
                        if wait is not None and j == 0 and k % 2 == 0:
                            wait(k)
                        wh, wl = at(j, k)
                        mm = mm3(W[:, bank, j * S:(j + 1) * S], wh, wl, ah[:, k, :], al[:, k, :], k == 0, k == kt - 1)
                return mm

            def plain_tiles(n):
                return lambda j, k: weights(n % SPLIT_SLOTS, k * 256 + j * P, P)

            def natural(n, width, kt, ah, al, bank):
                for t in range(NT):
                    for k in range(kt):
                        wh, wl = weights(n % SPLIT_SLOTS, k * width, width)
                        mm = mm3(W[:, bank, t * width:(t + 1) * width], ah[:, k, t * P:(t + 1) * P],
                                 al[:, k, t * P:(t + 1) * P], wh, wl, k == 0, k == kt - 1)
                return mm

            def scores(step, kh, head, rows):
                a = step % 2
                for j in range(4):
                    mm = pe.matmul(W[:, 4 + j // 2, (j % 2) * S:(j % 2 + 1) * S], qh[0:rows, a, j, P:S],
                                   kh[0:rows, head(j), :], start=True, stop=True)
                    if j % 2:
                        mm.then_inc(s_psum, 1)
                for j in range(4):
                    mm = pe.matmul(W[:, 6, j * P:(j + 1) * P], qh[0:rows, a, j, 0:P],
                                   kh[0:rows, head(j), 0:P], start=True, stop=True)
                mm.then_inc(s_psum, 1)

            def transpose_p(step, rotated=0):
                if step % QUADS:
                    pe.wait_ge(pt_dve, step)
                    pe.wait_ge(pt_act, 2 * step)
                pe.wait_ge(p_ready, 2 * step + 1)
                for j in range(4):
                    for kb in range(2):
                        tr = pe.transpose(W[:, 2 + j // 2, (j % 2) * S + kb * P:(j % 2) * S + (kb + 1) * P],
                                          sc[:, j, P + kb * P:P + (kb + 1) * P], ident[:, :])
                    if j % 2:
                        tr.then_inc(pt_psum, 1)
                pe.wait_ge(p_ready, 2 * step + 2)
                if rotated:
                    pe.wait_ge(qr_ready, rotated)
                for j in range(4):
                    tr = pe.transpose(W[:, 7, j * P:(j + 1) * P], sc[:, j, 0:P], ident[:, :])
                tr.then_inc(pt_psum, 1)

            def attend(step, v, col):
                pe.wait_ge(pt_dve, step + 1)
                pe.wait_ge(pt_act, 2 * step + 2)
                if step % QUADS:
                    pe.wait_ge(o_out, step)
                for j in range(4):
                    vj = v[:, :, col(j):col(j) + DH]
                    pe.matmul(W[:, 1, 256 + j * DH:256 + (j + 1) * DH], pT[:, 2 * j, :], vj[:, 0, :], start=True, stop=False)
                    pe.matmul(W[:, 1, 256 + j * DH:256 + (j + 1) * DH], pT[:, 2 * j + 1, :], vj[:, 1, :], start=False, stop=True)
                    mm = pe.matmul(W[:, 1, j * DH:(j + 1) * DH], pT[:, 8 + j, :], vj[:, 0, :], start=True, stop=True)
                mm.then_inc(o_psum, 1)

            def project_out(base, pairs, first_step):
                transpose_pairs(lambda t, k: r[:, t, k * P:(k + 1) * P], KD, O_BANKS,
                                lambda t: pe.wait_ge(o_out, first_step + QUADS))
                for c in range(O_CHUNKS):
                    n = base + c
                    pe.wait_ge(lo_done, n + 1)
                    pe.wait_ge(tlo_ready, pairs + c + 1)
                    last = c == O_CHUNKS - 1
                    for t in range(NT):
                        for k in range(2):
                            for half in range(2):
                                wh, wl = weights(n % SPLIT_SLOTS, k * D + half * 512, 512)
                                mm = mm3(W[:, 4 + 2 * t + half, :], xT_hi[:, 2 * c + k, t * P:(t + 1) * P],
                                         xT_lo[:, 2 * c + k, t * P:(t + 1) * P], wh, wl, c == 0 and k == 0, last and k == 1)
                        if last:
                            mm.then_inc(y_ready, 1)
                    if not last:
                        mm.then_inc(wo_done, 1)

            def mixer_a():
                pe.wait_ge(lo_done, A0 + 1)
                two_tiles(A0, 256, plain_tiles(A0), KD, xT_hi, xT_lo, 0,
                          lambda k: pe.wait_ge(tlo_ready, T_LN[0] + k // 2 + 1)).then_inc(k_psum, 1)
                pe.wait_ge(lo_done, A0 + 2)
                natural(A0 + 1, 256, KD, xT_hi, xT_lo, 1).then_inc(v_psum, 1)

                def project_q(c):
                    if c == 0:
                        pe.wait_ge(k_lower, 1)
                        pe.wait_ge(k_upper, 1)
                    else:
                        pe.wait_ge(q_lower, c)
                        pe.wait_ge(q_upper, c)
                    n = A0 + 2 + c
                    pe.wait_ge(lo_done, n + 1)
                    two_tiles(n, 256, plain_tiles(n), KD, xT_hi, xT_lo, 0).then_inc(q_psum, 1)

                def score(c):
                    pe.wait_ge(q_lower, c + 1)
                    pe.wait_ge(q_upper, c + 1)
                    if c:
                        pe.wait_ge(s_masked, c)
                    scores(c, khA, lambda j: c, DH)

                project_q(0)
                score(0)
                for c in range(QUADS):
                    if c + 1 < QUADS:
                        project_q(c + 1)
                    transpose_p(c)
                    if c + 1 < QUADS:
                        score(c + 1)
                    if c == 0:
                        pe.wait_ge(v_out0, 1)
                    attend(c, vA, lambda j: c * DH)
                project_out(AO, T_AO, 0)

            def mixer_b():
                kt_q, kt_kv = QLORA // P, KVLORA // P
                for c in range(2):
                    pe.wait_ge(lo_done, B0 + c + 1)
                    if c == 0:
                        for k in range(4):
                            pe.wait_ge(tlo_ready, T_LN[3] + k + 1)
                    natural(B0 + c, 256, KD, xT_hi, xT_lo, NAT_BANK[NAT_ORDER[c]]).then_inc(nat_psum, 1)
                transpose_pairs(lambda t, k: c_nat[:, t, QLORA + k * P:QLORA + (k + 1) * P], kt_kv, [0],
                                lambda t: pe.wait_ge(c_norm, t + 1))
                for c in range(2, 5):
                    part = NAT_ORDER[c]
                    pe.wait_ge(lo_done, B0 + c + 1)
                    natural(B0 + c, ROPE if part == "kr" else 256, KD, xT_hi, xT_lo, NAT_BANK[part]).then_inc(nat_psum, 1)
                for t in range(NT):
                    pe.wait_ge(nat_out, 4)
                    tr = pe.transpose(W[0:ROPE, 3, t * P:(t + 1) * P], kr_nat[:, t, :], ident[:, :])
                tr.then_inc(krt_psum, 1)
                pe.wait_ge(tlo_ready, T_CKV + 1)
                pe.wait_ge(nat_out, 5)
                for u in range(2):
                    n, sl = BU + u, (BU + u) % SPLIT_SLOTS
                    pe.wait_ge(lo_done, n + 1)

                    def head_cols(ring, k, h, part, count):
                        at = k * D + part * 8 * DH + h * DH
                        return ring[:, sl, at:at + count * DH]

                    for b in range(2):
                        if u:
                            pe.wait_ge(k_lower, 1 + b + 1)
                            pe.wait_ge(k_upper, 1 + b + 1)
                        mm = two_tiles(n, D, lambda j, k: (head_cols(hi, k, 4 * b + 2 * j, 0, 2), head_cols(lo, k, 4 * b + 2 * j, 0, 2)),
                                       kt_kv, h_hi, h_lo, b)
                        mm.then_inc(k_psum, 1)
                    for t in range(NT):
                        if u:
                            pe.wait_ge((v_out0, v_out1)[t], 2 - t)
                        for k in range(kt_kv):
                            mm = mm3(W[:, 6 + t, :], h_hi[:, k, t * P:(t + 1) * P], h_lo[:, k, t * P:(t + 1) * P],
                                     head_cols(hi, k, 0, 1, 8), head_cols(lo, k, 0, 1, 8), k == 0, k == kt_kv - 1)
                        mm.then_inc(v_psum, 1)
                transpose_pairs(lambda t, k: c_nat[:, t, k * P:(k + 1) * P], kt_q, CQ_BANKS,
                                lambda t: pe.wait_ge(c_norm, NT + t + 1))

                def project_q(c):
                    if c == 0:
                        pe.wait_ge(k_lower, 5)
                        pe.wait_ge(k_upper, 5)
                        pe.wait_ge(v_out0, 3)
                        pe.wait_ge(v_out1, 2)
                        pe.wait_ge(tlo_ready, T_CQ + 3)
                    else:
                        pe.wait_ge(qr_act, c)
                        pe.wait_ge(qr_dve, c)
                        pe.wait_ge(pt_act, 2 * (QUADS + c - 1))
                    for j in range(2):
                        n = BQ + 2 * c + j
                        pe.wait_ge(lo_done, n + 1)
                        for k in range(kt_q):
                            wh, wl = weights(n % SPLIT_SLOTS, k * 2 * QW, 2 * NOPE)
                            mm = mm3(W[:, 0, j * S:(j + 1) * S], wh, wl, xT_hi[:, k, :], xT_lo[:, k, :], k == 0, k == kt_q - 1)
                    mm.then_inc(q_psum, 1)
                    s0 = (BQ + 2 * c) % SPLIT_SLOTS
                    for t in range(NT):
                        for k in range(kt_q):
                            wh, wl = (ring[:, s0:s0 + 2, k * 2 * QW + 2 * NOPE:(k + 1) * 2 * QW] for ring in (hi, lo))
                            mm = mm3(W[:, 7, t * P:(t + 1) * P], xT_hi[:, k, t * P:(t + 1) * P], xT_lo[:, k, t * P:(t + 1) * P],
                                     wh, wl, k == 0, k == kt_q - 1)
                    mm.then_inc(qr_psum, 1)

                def transpose_qr(c):
                    pe.wait_ge(q_lower, QUADS + c + 1)
                    pe.wait_ge(q_upper, QUADS + c + 1)
                    pe.wait_ge(qr_ready, c + 1)
                    for t in range(NT):
                        tr = pe.transpose(W[:, 0, t * P:(t + 1) * P], qr_nat[:, t, :, :].rearrange("p h d -> p (h d)"), ident[:, :])
                    tr.then_inc(qrt_psum, 1)

                def score(c):
                    pe.wait_ge(qr_act, c + 1)
                    pe.wait_ge(qr_dve, c + 1)
                    if c:
                        pe.wait_ge(s_masked, QUADS + c)
                    else:
                        pe.wait_ge(kr_all, 1)
                    scores(QUADS + c, khB, lambda j: 4 * c + j, QW)

                project_q(0)
                transpose_qr(0)
                score(0)
                for c in range(QUADS):
                    if c + 1 < QUADS:
                        project_q(c + 1)
                    transpose_p(QUADS + c, min(c + 2, QUADS))
                    if c + 1 < QUADS:
                        transpose_qr(c + 1)
                    attend(QUADS + c, vB, lambda j: (4 * c + j) * DH)
                    if c + 1 < QUADS:
                        score(c + 1)
                project_out(BO, T_BO, QUADS)

            pe.wait_ge(const_in, 16)
            pe.wait_ge(rows_in, 64)
            pe.transpose(W[:, 7, 0:N_COL], prow[0:N_COL, :], ident[0:N_COL, 0:N_COL]).then_inc(cols_tr, 1)
            transpose_pairs(lambda t, k: x_nat[:, t, k * P:(k + 1) * P], KD, LN_BANKS, lambda t: pe.wait_ge(x_in, 16))
            ffn(0, T_X)
            after_ln(0)
            mixer_a()
            after_ln(A_LN)
            ffn(1, T_LN[1])
            after_ln(2)
            ffn(2, T_LN[2])
            after_ln(3)
            mixer_b()
            after_ln(B_LN)
            ffn(3, T_LN[4])

        @block.scalar
        def _(act):
            nxt = [0]

            def round_chunk(n, p=None, free=None):
                more = 0 if p is None else 2 * p
                act.wait_ge(raw_in[n % RAW_SLOTS], 16 * (n // RAW_SLOTS + 1) + 16 * more)
                if n >= SPLIT_SLOTS:
                    who, value = consumed(n - SPLIT_SLOTS)
                    act.wait_ge(who, value if p is None else value + 4 * p)
                for src, dst in zip(parts(n, (raw, n % RAW_SLOTS)), parts(n, (hi, n % SPLIT_SLOTS))):
                    op = nc.scalar.copy(dst, src)
                op.then_inc(hi_done, 1)

            def rounds_to(n):
                while nxt[0] <= min(n, CHUNKS - 1):
                    round_chunk(nxt[0])
                    nxt[0] += 1

            def hidden(f, t, tp=0):
                act.wait_ge(gu_ready, NFT * f + t + 1 + tp)
                nc.scalar.activation(sil[:, t % 2, :], W[:, t % 2, 0:S], ACT.Silu).then_inc(sil_ready, 1)
                act.wait_ge(hf_ready, NFT * f + t + 1 + tp)
                if t >= 2:
                    act.wait_ge(d_done, (NFT - 1) * f + t - 1 + tp)
                nc.scalar.copy(h_hi[:, t % 2, :], hf[:, t % 2, :]).then_inc(hhi_ready, 1)

            def ffn(f):
                base = FFN_BASE[f]

                def step(i, p=None, last=False):
                    n, tp = base + 3 * i, 0 if p is None else 4 * p
                    for c in range(3):
                        if n + LOOKAHEAD + c < CHUNKS:
                            round_chunk(n + LOOKAHEAD + c, p)
                        if c != 1:
                            hidden(f, 2 * i + c // 2, tp)

                step(0)
                with act.Fori(0, NFI // 2 - 1) as p:
                    step(1, p)
                    step(2, p)
                step(NFI - 2)
                step(NFI - 1)
                nxt[0] = base + FFN_CHUNKS + LOOKAHEAD

            def inverse_sqrt(e, at):
                act.wait_ge(isq_dve, 5 * e + 1)
                nc.scalar.activation(inv_l[:, at], inv_v[:, at], ACT.Ln).then_inc(isq_act, 1)
                act.wait_ge(isq_act, 2 * e + 1)
                nc.scalar.activation(inv_e[:, at], inv_l[:, at], ACT.Exp, scale=-0.5).then_inc(isq_act, 1)

            def deviations(l):
                for t in range(NT):
                    inverse_sqrt(ISQ_LN[l] + t, slice(t, t + 1))

            def pairs_affine(l):
                t0 = T_LN[l]
                deviations(l)

                def scale(p):
                    act.wait_ge(tr_ready, t0 + p + 1)
                    if p >= 2:
                        act.wait_ge(tlo_ready, t0 + p - 1)
                    for k in range(2):
                        c = l * KD + 2 * p + k
                        op = nc.scalar.activation(xf[:, p % 2, k, :], W[:, LN_BANKS[p], k * S:(k + 1) * S], ACT.Identity,
                                                  bias=cols[:, B_COL + c:B_COL + c + 1], scale=cols[:, G_COL + c:G_COL + c + 1])
                    op.then_inc(xf_act, 1)

                def rnd(p):
                    act.wait_ge((xf_dve, xf_act)[p % 2], 2 * LN_SEQ[l] + p // 2 + 1)
                    nc.scalar.copy(xT_hi[:, 2 * p:2 * p + 2, :], xf[:, p % 2, :, :]).then_inc(thi_ready, 1)

                scale(1)
                rnd(0)
                rnd(1)
                scale(3)
                rnd(2)
                rnd(3)

            def pairs_scaled(t0, n, banks, dst, col=None):
                for p in range(n):
                    act.wait_ge(tr_ready, t0 + p + 1)
                    if col is None:
                        op = nc.scalar.copy(dst[:, 2 * p:2 * p + 2, :], W[:, banks[p], :].rearrange("p (k n) -> p k n", k=2))
                    else:
                        for k in range(2):
                            c = col + 2 * p + k
                            op = nc.scalar.mul(dst[:, 2 * p + k, :], W[:, banks[p], k * S:(k + 1) * S], cols[:, c:c + 1])
                    op.then_inc(thi_ready, 1)

            def lower_heads(dst, bank, done):
                nc.scalar.copy(dst, W[0:DH, bank, :].rearrange("p (j n) -> p j n", j=2)).then_inc(done, 1)

            def exps(step, scale, sinks):
                act.wait_ge(negm_ready, step + 1)
                for t in (1, 0):
                    for j in range(4):
                        s = sc[:, j, P:3 * P] if t else sc[:, j, 0:P]
                        op = nc.scalar.activation(s, s, ACT.Exp, bias=negm[:, t, j:j + 1], scale=scale,
                                                  accum_out=rsum[:, t, j:j + 1])
                    op.then_inc(p_ready, 1)
                if sinks:
                    act.wait_ge(es_arg, step + 1)
                    nc.scalar.activation(esink[:, :, :], esink[:, :, :], ACT.Exp).then_inc(es_ready, 1)

            def copy_pt(step):
                if step:
                    act.wait_ge(o_psum, step)
                for b, (bank, at) in enumerate(((3, 4), (7, 8))):
                    act.wait_ge(pt_psum, 3 * step + 2 + b)
                    nc.scalar.copy(pT[:, at:at + 4, :], W[:, bank, :].rearrange("p (i n) -> p i n", i=4)).then_inc(pt_act, 1)

            def output_pairs(t0, base):
                pairs_scaled(t0, 4, O_BANKS, xT_hi)
                for c in range(O_CHUNKS):
                    rounds_to(base + c + LOOKAHEAD)

            def mixer_a():
                rounds_to(A0 + LOOKAHEAD)
                act.wait_ge(k_psum, 1)
                lower_heads(khA[0:DH, 0:KV_HEADS:2, :], 0, k_lower)
                rounds_to(A0 + 1 + LOOKAHEAD)
                rounds_to(A0 + 2 + LOOKAHEAD)
                for c in range(QUADS):
                    act.wait_ge(q_psum, c + 1)
                    if c == 0:
                        act.wait_ge(x_ready, NT * A_LN)
                    if c >= 2:
                        act.wait_ge(s_psum, 3 * (c - 1))
                    lower_heads(qh[0:DH, c % 2, 0:4:2, :], 0, q_lower)
                    if c:
                        copy_pt(c - 1)
                    exps(c, WIN_SCALE, True)
                    if c + 1 < QUADS:
                        rounds_to(A0 + 3 + c + LOOKAHEAD)
                copy_pt(QUADS - 1)
                output_pairs(T_AO, AO)

            def mixer_b():
                rounds_to(B0 + LOOKAHEAD)
                rounds_to(B0 + 1 + LOOKAHEAD)

                def squares(a, first, width, after):
                    act.wait_ge(nat_out, after)
                    for t in range(NT):
                        op = nc.scalar.activation(junk[:, t, 0:width], c_nat[:, t, first:first + width], ACT.Square,
                                                  scale=float(width) ** -0.5, accum_out=msq[:, a, t:t + 1])
                    op.then_inc(msq_ready, 1)
                    inverse_sqrt(ISQ_RMS[a], slice(0, NT))

                squares(0, QLORA, KVLORA, 1)
                rounds_to(B0 + 2 + LOOKAHEAD)
                pairs_scaled(T_CKV, 1, [0], h_hi, KVN_COL)
                rounds_to(B0 + 4 + LOOKAHEAD)
                squares(1, 0, QLORA, 5)
                act.wait_ge(krt_psum, 1)
                nc.scalar.copy(khB[NOPE:QW, 0, :], W[0:ROPE, 3, 0:S]).then_inc(kr_first, 1)
                for u in range(2):
                    rounds_to(BU + u + LOOKAHEAD)
                    for b in range(2):
                        act.wait_ge(k_psum, 1 + 2 * u + b + 1)
                        h = 8 * u + 4 * b
                        lower_heads(khB[0:DH, h:h + 4:2, :], b, k_lower)
                    act.wait_ge(v_psum, 1 + 2 * u + 1)
                    nc.scalar.copy(vB[:, 0, u * 512:(u + 1) * 512], W[:, 6, :]).then_inc(v_out0, 1)
                pairs_scaled(T_CQ, 3, CQ_BANKS, xT_hi, QN_COL)
                rounds_to(BQ + 1 + LOOKAHEAD)
                for c in range(QUADS):
                    act.wait_ge(q_psum, QUADS + c + 1)
                    if c == 0:
                        act.wait_ge(x_ready, NT * B_LN)
                    if c >= 2:
                        act.wait_ge(s_psum, 3 * (QUADS + c - 1))
                    lower_heads(qh[0:DH, c % 2, 0:4:2, :], 0, q_lower)
                    if c:
                        copy_pt(QUADS + c - 1)
                    act.wait_ge(qrt_psum, c + 1)
                    for j in range(2):
                        op = nc.scalar.copy(qh[NOPE:QW, c % 2, j, :], W[j * ROPE:(j + 1) * ROPE, 0, 0:S])
                    op.then_inc(qr_act, 1)
                    exps(QUADS + c, MLA_SCALE, False)
                    if c + 1 < QUADS:
                        rounds_to(BQ + 2 * c + 3 + LOOKAHEAD)
                copy_pt(2 * QUADS - 1)
                output_pairs(T_BO, BO)

            act.wait_ge(cols_tr, 1)
            nc.scalar.copy(cols[:, :], W[:, 7, 0:N_COL]).then_inc(cols_ready, 1)
            pairs_scaled(T_X, 4, LN_BANKS, xT_hi)
            rounds_to(LOOKAHEAD - 1)
            ffn(0)
            act.wait_ge(cols_ready, 1)
            pairs_affine(0)
            mixer_a()
            pairs_affine(A_LN)
            ffn(1)
            pairs_affine(2)
            ffn(2)
            pairs_affine(3)
            mixer_b()
            pairs_affine(B_LN)
            ffn(3)
            deviations(LNS - 1)

        @block.vector
        def _(dve):
            nxt = [0]

            def rest_of_chunk(n, p=None):
                dve.wait_ge(hi_done, n + 1 if p is None else n + 1 + 6 * p)
                sl = n % SPLIT_SLOTS
                for src, top, dst in zip(parts(n, (raw, n % RAW_SLOTS)), parts(n, (hi, sl)), parts(n, (lo, sl))):
                    op = nc.vector.tensor_tensor(dst, src, top, ALU.subtract)
                op.then_inc(lo_done, 1)

            def rests_to(n):
                while nxt[0] <= min(n, CHUNKS - 1):
                    rest_of_chunk(nxt[0])
                    nxt[0] += 1

            def hidden(f, t, tp=0):
                dve.wait_ge(sil_ready, NFT * f + t + 1 + tp)
                nc.vector.tensor_tensor(hf[:, t % 2, :], sil[:, t % 2, :], W[:, t % 2, S:2 * S], ALU.mult).then_inc(hf_ready, 1)

            def hidden_rest(f, t, tp=0):
                dve.wait_ge(hhi_ready, NFT * f + t + 1 + tp)
                nc.vector.tensor_tensor(h_lo[:, t % 2, :], hf[:, t % 2, :], h_hi[:, t % 2, :], ALU.subtract).then_inc(hlo_ready, 1)

            def ffn(f):
                base = FFN_BASE[f]

                def step(i, p=None):
                    n, tp = base + 3 * i + LOOKAHEAD, 0 if p is None else 4 * p
                    if n < CHUNKS:
                        rest_of_chunk(n, p)
                    hidden(f, 2 * i, tp)
                    if n < CHUNKS:
                        rest_of_chunk(n + 1, p)
                    hidden_rest(f, 2 * i, tp)
                    if n < CHUNKS:
                        rest_of_chunk(n + 2, p)
                    hidden(f, 2 * i + 1, tp)
                    hidden_rest(f, 2 * i + 1, tp)

                step(0)
                with dve.Fori(0, NFI // 2 - 1) as p:
                    step(1, p)
                    step(2, p)
                step(NFI - 2)
                step(NFI - 1)
                nxt[0] = base + FFN_CHUNKS + LOOKAHEAD

            def inverse_sqrt(e, v, eps, at):
                nc.vector.tensor_scalar(inv_v[:, at], v, eps, None, ALU.add).then_inc(isq_dve, 1)
                dve.wait_ge(isq_act, 2 * e + 2)
                nc.vector.tensor_tensor(inv_t[:, at], inv_e[:, at], inv_e[:, at], ALU.mult).then_inc(isq_dve, 1)
                dve.wait_ge(isq_dve, 5 * e + 2)
                nc.vector.tensor_tensor(inv_t[:, at], inv_t[:, at], inv_v[:, at], ALU.mult).then_inc(isq_dve, 1)
                dve.wait_ge(isq_dve, 5 * e + 3)
                nc.vector.tensor_scalar(inv_t[:, at], inv_t[:, at], -0.5, 1.5, ALU.mult, ALU.add).then_inc(isq_dve, 1)
                dve.wait_ge(isq_dve, 5 * e + 4)
                nc.vector.tensor_tensor(rstd[:, at], inv_e[:, at], inv_t[:, at], ALU.mult).then_inc(isq_dve, 1)
                dve.wait_ge(isq_dve, 5 * e + 5)

            def layer_norm(l, ffn_before):
                two = 2.0 if ffn_before else 1.0
                if l == 0:
                    dve.wait_ge(x_in, 16)
                for t in range(NT):
                    s0 = 3 * (NT * l + t)
                    dve.wait_ge(y_ready, NT * l + t + 1)
                    if l:
                        dve.wait_ge(x_ready, NT * (l - 1) + t + 1)
                    nc.vector.scalar_tensor_tensor(out=r[:, t, :], in0=x_nat[:, t, :], scalar=two * ALPHA,
                                                   in1=W[:, 4 + 2 * t:6 + 2 * t, :].rearrange("p b n -> p (b n)"),
                                                   op0=ALU.mult, op1=ALU.add).then_inc(ln_step, 1)
                    dve.wait_ge(ln_step, s0 + 1)
                    for a in range(2):
                        op = nc.vector.bn_stats(bn[:, t, a, :], r[:, t, a * 512:(a + 1) * 512])
                    op.then_inc(ln_step, 1)
                    dve.wait_ge(ln_step, s0 + 2)
                    nc.vector.bn_aggr(mv[:, t, :], bn[:, t, :, :].rearrange("p a s -> p (a s)")).then_inc(ln_step, 1)
                    dve.wait_ge(ln_step, s0 + 3)
                    inverse_sqrt(ISQ_LN[l] + t, mv[:, t, 1:2], two * two * LN_EPS, slice(t, t + 1))
                    nc.vector.tensor_scalar(r[:, t, :], r[:, t, :], mv[:, t, 0:1], rstd[:, t:t + 1],
                                            ALU.subtract, ALU.mult).then_inc(xhat_ready, 1)

            def pairs_affine(l):
                t0 = T_LN[l]

                def scale(p):
                    dve.wait_ge(tr_ready, t0 + p + 1)
                    if p >= 2:
                        dve.wait_ge(tlo_ready, t0 + p - 1)
                    for k in range(2):
                        c = l * KD + 2 * p + k
                        op = nc.vector.tensor_scalar(xf[:, p % 2, k, :], W[:, LN_BANKS[p], k * S:(k + 1) * S],
                                                     cols[:, G_COL + c:G_COL + c + 1], cols[:, B_COL + c:B_COL + c + 1],
                                                     ALU.mult, ALU.add)
                    op.then_inc(xf_dve, 1)

                def rest(p):
                    dve.wait_ge(thi_ready, t0 + p + 1)
                    nc.vector.tensor_tensor(xT_lo[:, 2 * p:2 * p + 2, :], xf[:, p % 2, :, :], xT_hi[:, 2 * p:2 * p + 2, :],
                                            ALU.subtract).then_inc(tlo_ready, 1)

                scale(0)
                rest(0)
                scale(2)
                rest(1)
                rest(2)
                rest(3)

            def pairs_scaled(t0, n, banks, dst, src, col=None):
                for p in range(n):
                    dve.wait_ge(thi_ready, t0 + p + 1)
                    if col is None:
                        op = nc.vector.tensor_tensor(dst[:, 2 * p:2 * p + 2, :], W[:, banks[p], :].rearrange("p (k n) -> p k n", k=2),
                                                     src[:, 2 * p:2 * p + 2, :], ALU.subtract)
                    else:
                        for k in range(2):
                            c = col + 2 * p + k
                            op = nc.vector.scalar_tensor_tensor(out=dst[:, 2 * p + k, :], in0=W[:, banks[p], k * S:(k + 1) * S],
                                                                scalar=cols[:, c:c + 1], in1=src[:, 2 * p + k, :],
                                                                op0=ALU.mult, op1=ALU.subtract)
                    op.then_inc(tlo_ready, 1)

            def upper_heads(dst, bank, done):
                nc.vector.tensor_copy(dst, W[DH:P, bank, :].rearrange("p (j n) -> p j n", j=2)).then_inc(done, 1)

            def maxima(step, bias):
                for t in (1, 0):
                    for j in range(4):
                        if t and j % 2 == 0:
                            dve.wait_ge(s_psum, 3 * step + j // 2 + 1)
                        if t == 0 and j == 0:
                            dve.wait_ge(s_psum, 3 * step + 3)
                        if t:
                            dst, src, b = sc[:, j, P:3 * P], W[:, 4 + j // 2, (j % 2) * S:(j % 2 + 1) * S], bias(j)
                        else:
                            dst, src, b = sc[:, j, 0:P], W[:, 6, j * P:(j + 1) * P], bias(j)[:, P:2 * P]
                        op = nc.vector.tensor_tensor_reduce(out=dst, in0=src, in1=b, scale=1.0, scalar=NEG, op0=ALU.add,
                                                            op1=ALU.max, accum_out=smax[:, t, j:j + 1])
                op.then_inc(s_masked, 1)

            def copy_pt(step):
                dve.wait_ge(pt_psum, 3 * step + 1)
                nc.vector.tensor_copy(pT[:, 0:4, :], W[:, 2, :].rearrange("p (i n) -> p i n", i=4)).then_inc(pt_dve, 1)

            def normalise(step, c):
                dve.wait_ge(o_psum, step + 1)
                dve.wait_ge(den_step, DEN[step])
                if c == 0:
                    dve.wait_ge(x_ready, NT * (A_LN if step == 0 else B_LN))
                nc.vector.tensor_tensor(
                    r[:, :, c * 4 * DH:(c + 1) * 4 * DH].rearrange("p t (j d) -> p t j d", j=4),
                    W[:, 1, :].rearrange("p (t j d) -> p t j d", t=NT, j=4),
                    rden[:, :, :].unsqueeze(3).to_broadcast([P, NT, 4, DH]), ALU.mult).then_inc(o_out, 1)

            def output_pairs(t0, base):
                pairs_scaled(t0, 4, O_BANKS, xT_lo, xT_hi)
                for c in range(O_CHUNKS):
                    rests_to(base + c + LOOKAHEAD)

            def mixer_a():
                rests_to(A0 + LOOKAHEAD)
                dve.wait_ge(k_psum, 1)
                upper_heads(khA[0:DH, 1:KV_HEADS:2, :], 0, k_upper)
                rests_to(A0 + 1 + LOOKAHEAD)
                dve.wait_ge(v_psum, 1)
                nc.vector.tensor_copy(vA[:, :, :], W[:, 1, :].rearrange("p (t d) -> p t d", t=NT)).then_inc(v_out0, 1)
                rests_to(A0 + 2 + LOOKAHEAD)
                dve.wait_ge(alibi_ready, 1)
                dve.wait_ge(sink_neg, 1)

                def finish(c):
                    dve.wait_ge(es_ready, c + 1)
                    nc.vector.tensor_tensor(rden[:, :, :], rsum[:, :, :], esink[:, :, :], ALU.add).then_inc(den_step, 1)
                    dve.wait_ge(den_step, 2 * c + 1)
                    nc.vector.reciprocal(rden[:, :, :], rden[:, :, :]).then_inc(den_step, 1)
                    copy_pt(c)
                    normalise(c, c)

                for c in range(QUADS):
                    dve.wait_ge(q_psum, c + 1)
                    if c == 0:
                        dve.wait_ge(x_ready, NT * A_LN)
                    if c >= 2:
                        dve.wait_ge(s_psum, 3 * (c - 1))
                    upper_heads(qh[0:DH, c % 2, 1:4:2, :], 0, q_upper)
                    if c:
                        finish(c - 1)
                    maxima(c, lambda j: alibi[:, 4 * c + j, :])
                    dve.wait_ge(s_masked, c + 1)
                    sinks = nsink[:, 4 * c:4 * c + 4].unsqueeze(1).to_broadcast([P, NT, 4])
                    nc.vector.scalar_tensor_tensor(out=negm[:, :, :], in0=smax[:, :, :], scalar=-WIN_SCALE, in1=sinks,
                                                   op0=ALU.mult, op1=ALU.min).then_inc(negm_ready, 1)
                    dve.wait_ge(negm_ready, c + 1)
                    nc.vector.tensor_tensor(esink[:, :, :], negm[:, :, :], sinks, ALU.subtract).then_inc(es_arg, 1)
                    if c + 1 < QUADS:
                        rests_to(A0 + 3 + c + LOOKAHEAD)
                finish(QUADS - 1)
                output_pairs(T_AO, AO)

            def rotate(x1, x2, o1, o2, shape, start):
                heads = shape[1]
                ta = rope_t[:, 0, :, 0:heads, :]
                tb = rope_t[:, 1, :, 0:heads, :]
                cos, sin = (rope_s[:, :, a:a + 1, :].to_broadcast([P, NT, heads, HR]) for a in range(2))
                for o, (fa, fb, op) in ((o1, (cos, sin, ALU.subtract)), (o2, (sin, cos, ALU.add))):
                    nc.vector.tensor_tensor(ta, x1, fa, ALU.mult)
                    nc.vector.tensor_tensor(tb, x2, fb, ALU.mult).then_inc(rope_step, 1)
                    start += 1
                    dve.wait_ge(rope_step, start)
                    last = nc.vector.tensor_tensor(o, ta, tb, op)
                    if o is o1:
                        last.then_inc(rope_step, 1)
                        start += 1
                        dve.wait_ge(rope_step, start)
                return last

            def mixer_b():
                rests_to(B0 + LOOKAHEAD)

                def nat_copy(c):
                    part = NAT_ORDER[c]
                    at = QLORA if part == "ckv" else 256 * int(part[2])
                    dve.wait_ge(nat_psum, c + 1)
                    nc.vector.tensor_copy(c_nat[:, :, at:at + 256],
                                          W[:, NAT_BANK[part], :].rearrange("p (t d) -> p t d", t=NT)).then_inc(nat_out, 1)

                def rms(a, first, width):
                    dve.wait_ge(msq_ready, a + 1)
                    inverse_sqrt(ISQ_RMS[a], msq[:, a, :], RMS_EPS, slice(0, NT))
                    for t in range(NT):
                        nc.vector.tensor_scalar(c_nat[:, t, first:first + width], c_nat[:, t, first:first + width],
                                                rstd[:, t:t + 1], None, ALU.mult).then_inc(c_norm, 1)

                nat_copy(0)
                rests_to(B0 + 1 + LOOKAHEAD)
                rms(0, QLORA, KVLORA)
                nat_copy(1)
                pairs_scaled(T_CKV, 1, [0], h_lo, h_hi, KVN_COL)
                rests_to(B0 + 2 + LOOKAHEAD)
                nat_copy(2)
                dve.wait_ge(nat_psum, 4)
                ps = W[:, NAT_BANK["kr"], 0:NT * ROPE].rearrange("p (t a c) -> p t a c", t=NT, a=2)
                rotate(ps[:, :, 0:1, :], ps[:, :, 1:2, :], kr_nat[:, :, 0:HR].unsqueeze(2), kr_nat[:, :, HR:ROPE].unsqueeze(2),
                       [NT, 1], 0).then_inc(nat_out, 1)
                rests_to(B0 + 4 + LOOKAHEAD)
                nat_copy(4)
                rms(1, 0, QLORA)
                for u in range(2):
                    rests_to(BU + u + LOOKAHEAD)
                    for b in range(2):
                        dve.wait_ge(k_psum, 1 + 2 * u + b + 1)
                        h = 8 * u + 4 * b
                        upper_heads(khB[0:DH, h + 1:h + 4:2, :], b, k_upper)
                    dve.wait_ge(v_psum, 1 + 2 * u + 2)
                    nc.vector.tensor_copy(vB[:, 1, u * 512:(u + 1) * 512], W[:, 7, :]).then_inc(v_out1, 1)
                pairs_scaled(T_CQ, 3, CQ_BANKS, xT_lo, xT_hi, QN_COL)
                rests_to(BQ + 1 + LOOKAHEAD)

                def finish(c):
                    step = QUADS + c
                    dve.wait_ge(p_ready, 2 * step + 2)
                    nc.vector.reciprocal(rden[:, :, :], rsum[:, :, :]).then_inc(den_step, 1)
                    normalise(step, c)

                for c in range(QUADS):
                    dve.wait_ge(q_psum, QUADS + c + 1)
                    if c == 0:
                        dve.wait_ge(x_ready, NT * B_LN)
                    if c >= 2:
                        dve.wait_ge(s_psum, 3 * (QUADS + c - 1))
                    upper_heads(qh[0:DH, c % 2, 1:4:2, :], 0, q_upper)
                    dve.wait_ge(qr_psum, c + 1)
                    if c:
                        dve.wait_ge(qrt_psum, c)
                    ps = W[:, 7, 0:NT * P].rearrange("p (t h a c) -> p t h a c", t=NT, h=4, a=2)
                    rotate(ps[:, :, :, 0, :], ps[:, :, :, 1, :], qr_nat[:, :, :, 0:HR], qr_nat[:, :, :, HR:ROPE],
                           [NT, 4], 3 * (c + 1)).then_inc(qr_ready, 1)
                    if c:
                        copy_pt(QUADS + c - 1)
                    dve.wait_ge(qrt_psum, c + 1)
                    for j in range(2, 4):
                        op = nc.vector.tensor_copy(qh[NOPE:QW, c % 2, j, :], W[j * ROPE:(j + 1) * ROPE, 0, 0:S])
                    op.then_inc(qr_dve, 1)
                    if c:
                        finish(c - 1)
                    maxima(QUADS + c, lambda j: causal_s[:, :])
                    dve.wait_ge(s_masked, QUADS + c + 1)
                    nc.vector.tensor_scalar(negm[:, :, :], smax[:, :, :], -MLA_SCALE, None, ALU.mult).then_inc(negm_ready, 1)
                    if c + 1 < QUADS:
                        rests_to(BQ + 2 * c + 3 + LOOKAHEAD)
                copy_pt(2 * QUADS - 1)
                finish(QUADS - 1)
                output_pairs(T_BO, BO)

            pairs_scaled(T_X, 4, LN_BANKS, xT_lo, xT_hi)
            rests_to(LOOKAHEAD - 1)
            ffn(0)
            layer_norm(0, True)
            dve.wait_ge(cols_ready, 1)
            pairs_affine(0)
            mixer_a()
            layer_norm(A_LN, False)
            pairs_affine(A_LN)
            ffn(1)
            layer_norm(2, True)
            pairs_affine(2)
            ffn(2)
            layer_norm(3, True)
            pairs_affine(3)
            mixer_b()
            layer_norm(B_LN, False)
            pairs_affine(B_LN)
            ffn(3)
            layer_norm(LNS - 1, True)
            dve.wait_ge(gb_in, 32 * LNS)
            for t in range(NT):
                dve.wait_ge(xhat_ready, NT * (LNS - 1) + t + 1)
                nc.vector.tensor_tensor(r[:, t, :], r[:, t, :], gb[:, 0, :], ALU.mult).then_inc(fin_step, 1)
                dve.wait_ge(fin_step, t + 1)
                nc.vector.tensor_tensor(r[:, t, :], r[:, t, :], gb[:, 1, :], ALU.add).then_inc(out_ready, 1)


DEN = [2 * (s + 1) for s in range(QUADS)] + [2 * QUADS + s + 1 for s in range(QUADS)]
ISQ_LN = [2 * l if l < B_LN else 2 * l + 2 for l in range(LNS)]
ISQ_RMS = [2 * B_LN, 2 * B_LN + 1]
LN_SEQ = {l: i for i, l in enumerate(sorted(T_LN))}

_INS = ["x", "ffn1_w_gu", "ffn1_w_down", "ffn2_w_gu", "ffn2_w_down", "ln_g", "ln_b",
        "a_w_in", "a_sinks", "a_w_o", "b_w_in", "b_q_norm", "b_w_uq", "b_kv_norm", "b_w_ukv", "b_w_o"]


def shape_constants():
    q = np.arange(P)[:, None]
    k = np.arange(2 * P)[None, :]
    dist = q + P - k
    window = np.where((dist >= 0) & (dist < P), -dist, NEG).astype(np.float32)
    causal = np.where(dist >= 0, 0.0, NEG).astype(np.float32)
    inv = np.float32(10000.0) ** (-np.arange(0, ROPE, 2, dtype=np.float32) / np.float32(ROPE))
    ang = np.arange(S, dtype=np.float32)[:, None] * inv[None, :].astype(np.float32)
    table = np.stack([np.cos(ang), np.sin(ang)], axis=1).astype(np.float32)
    return {"identity": np.eye(P, dtype=np.float32), "window": window, "causal": causal, "rope_tab": table}


def kernel(**inputs):
    import concourse.bacc as _bacc
    from concourse.bass_utils import run_bass_kernel_spmd as _run

    nc = _bacc.Bacc("TRN2", target_bir_lowering=False, num_devices=1)
    arrays, args = {}, []
    given = {name: np.ascontiguousarray(inputs[name]) for name in _INS}
    for name, a in {**given, **shape_constants()}.items():
        arrays[f"in_{name}_dram"] = a
        args.append(nc.dram_tensor(f"in_{name}_dram", a.shape, mybir.dt.from_np(a.dtype), kind="ExternalInput").ap())
    args.append(nc.dram_tensor("out_0_dram", (1, S, D), F32, kind="ExternalOutput").ap())
    trunk_kernel(nc, *args)
    r = _run(nc, [arrays], core_ids=[0])
    return r.results[0]["out_0_dram"]
```

```python
from contextlib import ExitStack

import numpy as np

import concourse.bass as bass
from concourse import mybir

F32 = mybir.dt.float32
F32R = mybir.dt.float32r
ALU = mybir.AluOpType
ACT = mybir.ActivationFunctionType

P = 128
D = 1024
S = 256
NT = S // P
KD = D // P
FF = 2816
NFT = FF // P
NFI = NFT // 2
ALPHA = (2.0 * 2) ** 0.25
LN_EPS, RMS_EPS, NEG = 1e-5, 1e-6, -1e30
HEADS, KV_HEADS, DH = 16, 4, 64
QLORA, KVLORA, NOPE, ROPE = 768, 256, 64, 32
HR = ROPE // 2
QW = NOPE + ROPE
QUADS = HEADS // 4
WIN_SCALE = DH ** -0.5
MLA_SCALE = QW ** -0.5

RAW_SLOTS, SPLIT_SLOTS, LOOKAHEAD, CH = 3, 6, 3, 2048

G_COL, B_COL, QN_COL, KVN_COL, N_COL = 0, 48, 96, 102, 104

FFN_CHUNKS = 3 * NFI
A_CHUNKS, B_CHUNKS, O_CHUNKS = 2 + QUADS, 5 + 2 + 2 * QUADS, KD // 2
FFN0 = 0
A0 = FFN0 + FFN_CHUNKS
AO = A0 + A_CHUNKS
FFN1 = AO + O_CHUNKS
FFN2 = FFN1 + FFN_CHUNKS
B0 = FFN2 + FFN_CHUNKS
BU = B0 + 5
BQ = BU + 2
BO = BQ + 2 * QUADS
FFN3 = BO + O_CHUNKS
CHUNKS = FFN3 + FFN_CHUNKS
FFN_BASE = [FFN0, FFN1, FFN2, FFN3]
assert BQ % 2 == 0

FFN_LN = [0, 2, 3, 5]
A_LN, B_LN = 1, 4
LNS = 6

T_X = 0
T_LN = {0: 4, 1: 12, 2: 16, 3: 20, 4: 32}
T_AO, T_CKV, T_CQ, T_BO = 8, 24, 25, 28
LN_BANKS, O_BANKS = [2, 3, 4, 5], [2, 3, 0, 1]
CKV_BANKS, CQ_BANKS = [2], [4, 5, 2]
HRING = 4
D_DONE = NFT - 3

NAT_ORDER = ["ckv", "cq0", "cq1", "kr", "cq2"]
NAT_BANK = {"ckv": 0, "cq0": 1, "cq1": 6, "kr": 3, "cq2": 7}


def trunk_kernel(nc, x, ffn1_w_gu, ffn1_w_down, ffn2_w_gu, ffn2_w_down, ln_g, ln_b,
                 a_w_in, a_sinks, a_w_o, b_w_in, b_q_norm, b_w_uq, b_kv_norm, b_w_ukv, b_w_o,
                 identity, window, causal, rope_tab, out):
    with ExitStack() as ctx:
        def sb(name, shape, dt=F32):
            return ctx.enter_context(nc.sbuf_tensor(name, shape, dt))

        def sem(name):
            return ctx.enter_context(nc.semaphore(name))

        raw = sb("raw", [P, RAW_SLOTS, CH])
        hi = sb("hi", [P, SPLIT_SLOTS, CH], F32R)
        lo = sb("lo", [P, SPLIT_SLOTS, CH], F32R)
        x_nat = sb("x_nat", [P, NT, D])
        r = sb("r", [P, NT, D])
        xT_hi = sb("xT_hi", [P, KD, S], F32R)
        xT_lo = sb("xT_lo", [P, KD, S], F32R)
        h_hi = sb("h_hi", [P, HRING, S], F32R)
        h_lo = sb("h_lo", [P, HRING, S], F32R)
        work = sb("work", [P, 5120])
        kv = sb("kv", [P, 6144])
        ident = sb("ident", [P, P])
        window_s = sb("window_s", [P, 2 * P])
        causal_s = sb("causal_s", [P, 2 * P])
        rope_s = sb("rope_s", [P, NT, 2, HR])
        cols = sb("cols", [P, N_COL])
        nsink = sb("nsink", [P, HEADS])
        bn = sb("bn", [P, NT, 2, 6])
        mv = sb("mv", [P, NT, 2])
        inv_v = sb("inv_v", [P, NT])
        inv_s = sb("inv_s", [P, NT])
        inv_e = sb("inv_e", [P, NT])
        inv_t = sb("inv_t", [P, NT])
        rstd = sb("rstd", [P, NT])
        eps_col = sb("eps_col", [P, 3])
        warm = sb("warm", [P, 1])
        smax = sb("smax", [P, NT, 4])
        negm = sb("negm", [P, NT, 4])
        rsum = sb("rsum", [P, NT, 4])
        esink = sb("esink", [P, NT, 4])
        rden = sb("rden", [P, NT, 4])
        msq = sb("msq", [P, 2, NT])

        gb = work[:, 0:2 * D].rearrange("p (a d) -> p a d", a=2)
        sil = work[:, 2048:2560].rearrange("p (a n) -> p a n", a=2)
        hf = work[:, 2560:3072].rearrange("p (a n) -> p a n", a=2)
        xf = work[:, 4096:5120].rearrange("p (a k n) -> p a k n", a=2, k=4)
        prow = work[:, 0:P]
        qh = work[:, 0:2048].rearrange("p (a h n) -> p a h n", a=2, h=4)
        pT = work[:, 2048:3584].rearrange("p (i n) -> p i n", i=12)
        sc = work[:, 3584:5120].rearrange("p (h n) -> p h n", h=4)
        c_nat = work[:, 2048:4096].rearrange("p (t d) -> p t d", t=NT)
        rope_t = r[:, 0, 768:1024].rearrange("p (a t h c) -> p a t h c", a=2, t=NT, h=4)
        qr_nat = r[:, 1, 768:1024].rearrange("p (t h c) -> p t h c", t=NT, h=4)
        kr_nat = r[:, 0, 512:512 + NT * ROPE].rearrange("p (t c) -> p t c", t=NT)
        alibi = kv[:, 0:4096].rearrange("p (h n) -> p h n", h=HEADS)
        khA = kv[:, 4096:5120].rearrange("p (h n) -> p h n", h=KV_HEADS)
        vA = kv[:, 5120:5632].rearrange("p (t d) -> p t d", t=NT)
        khB = kv[:, 0:4096].rearrange("p (h n) -> p h n", h=HEADS)
        junk = kv[:, 0:NT * QLORA].rearrange("p (t d) -> p t d", t=NT)
        vB = kv[:, 4096:6144].rearrange("p (t d) -> p t d", t=NT)

        W = ctx.enter_context(nc.psum_tensor("banks", [P, 8, 512], F32))

        raw_in = [sem(f"raw_in{i}") for i in range(RAW_SLOTS)]
        hi_done = sem("hi_done")
        lo_done = sem("lo_done")
        x_in = [sem(f"x_in{t}") for t in range(NT)]
        ident_in = sem("ident_in")
        rows_in = sem("rows_in")
        const_in = sem("const_in")
        gb_in = sem("gb_in")
        cols_tr = sem("cols_tr")
        cols_ready = sem("cols_ready")
        alibi_ready = sem("alibi_ready")
        sink_neg = sem("sink_neg")
        gu_ready = sem("gu_ready")
        sil_ready = sem("sil_ready")
        hidden_tr = sem("hidden_tr")
        hf_ready = sem("hf_ready")
        hhi_ready = sem("hhi_ready")
        hlo_ready = sem("hlo_ready")
        d_done = sem("d_done")
        y_ready = sem("y_ready")
        ln_step = sem("ln_step")
        isq_dve = sem("isq_dve")
        isq_act = sem("isq_act")
        eps_ready = sem("eps_ready")
        rstd_ready = sem("rstd_ready")
        xhat_ready = sem("xhat_ready")
        pool_step = sem("pool_step")
        x_ready = sem("x_ready")
        fin_step = sem("fin_step")
        out_ready = sem("out_ready")
        out_done = sem("out_done")
        tr_ready = sem("tr_ready")
        xf_ready = sem("xf_ready")
        xf_last = sem("xf_last")
        thi_ready = sem("thi_ready")
        tlo_ready = sem("tlo_ready")
        k_psum, k_lower, k_upper = sem("k_psum"), sem("k_lower"), sem("k_upper")
        v_psum, v_out0, v_out1 = sem("v_psum"), sem("v_out0"), sem("v_out1")
        q_psum, q_lower, q_upper = sem("q_psum"), sem("q_lower"), sem("q_upper")
        s_psum = sem("s_psum")
        s_masked = sem("s_masked")
        negm_ready = sem("negm_ready")
        es_arg = sem("es_arg")
        es_ready = sem("es_ready")
        p_ready = sem("p_ready")
        pt_psum = sem("pt_psum")
        pt_dve, pt_act = sem("pt_dve"), sem("pt_act")
        den_step = sem("den_step")
        o_psum = sem("o_psum")
        o_out = sem("o_out")
        wo_done = sem("wo_done")
        nat_psum = sem("nat_psum")
        nat_out = sem("nat_out")
        msq_ready = sem("msq_ready")
        c_norm = sem("c_norm")
        rope_step = sem("rope_step")
        krt_psum = sem("krt_psum")
        kr_first = sem("kr_first")
        kr_all = sem("kr_all")
        qr_psum = sem("qr_psum")
        qr_ready = sem("qr_ready")
        qrt_psum = sem("qrt_psum")
        qr_act, qr_dve = sem("qr_act"), sem("qr_dve")

        def consumed(n):
            for f, base in enumerate(FFN_BASE):
                if base <= n < base + FFN_CHUNKS:
                    i, c = divmod(n - base, 3)
                    if c < 2:
                        return gu_ready, NFT * f + 2 * i + 2
                    if i < NFI - 2:
                        return d_done, D_DONE * f + 2 * i + 2
                    return y_ready, NT * (FFN_LN[f] + 1)
            if n == A0:
                return k_psum, 1
            if n == A0 + 1:
                return v_psum, 1
            if n < AO:
                return q_psum, n - A0 - 1
            if n < FFN1:
                return (wo_done, n - AO + 1) if n < AO + 2 else (y_ready, NT * (A_LN + 1))
            if n < BU:
                return nat_psum, n - B0 + 1
            if n < BQ:
                return v_psum, 1 + 2 * (n - BU + 1)
            if n < BO:
                return q_psum, QUADS + (n - BQ) // 2 + 1
            return (wo_done, 2 + n - BO + 1) if n < BO + 2 else (y_ready, NT * (B_LN + 1))

        def size(n):
            if n == B0 + NAT_ORDER.index("kr"):
                return KD * ROPE
            if BQ <= n < BO:
                return (QLORA // P) * 2 * QW
            return CH

        def parts(n, at):
            m, split = size(n), at[0] is not raw
            row = at[0][:, at[1], 0:m]
            if BU <= n < BQ:
                how = "p (k a h d) -> p k a h d" if split else "p (k h a d) -> p k a h d"
                v = row.rearrange(how, a=2, d=DH, k=KVLORA // P)
                return [v[:, k, :, :, :] for k in range(KVLORA // P)]
            if BQ <= n < BO:
                v = row.rearrange("p (k c) -> p k c", k=QLORA // P)
                if split:
                    return [v[:, :, 0:2 * NOPE].rearrange("p k (h d) -> p k h d", h=2),
                            v[:, :, 2 * NOPE:2 * QW].rearrange("p k (h d) -> p k h d", h=2)]
                v = v.rearrange("p k (h c) -> p k h c", h=2)
                return [v[:, :, :, 0:NOPE], v[:, :, :, NOPE:QW]]
            return [row]

        block = ctx.enter_context(nc.Block())

        @block.sync
        def _(sp):
            def place(n, sl):
                def cols_of(w, k, a, width):
                    return w.rearrange("(k p) f -> p k f", p=P)[:, :, a:a + width], "p (k f) -> p k f", k

                if n < AO:
                    w = a_w_in[0]
                    c = n - A0
                    a = {0: D, 1: D + KV_HEADS * DH}[c] if c < 2 else (c - 2) * 4 * DH
                    src, how, k = cols_of(w, KD, a, 4 * DH)
                elif n < FFN1 or BO <= n < FFN3:
                    w, c = (a_w_o, n - AO) if n < FFN1 else (b_w_o, n - BO)
                    src = w[0].rearrange("(k p) f -> p k f", p=P)[:, 2 * c:2 * c + 2, :]
                    how, k = "p (k f) -> p k f", 2
                elif n < BU:
                    part = NAT_ORDER[n - B0]
                    a, wd = {"ckv": (QLORA, KVLORA), "kr": (QLORA + KVLORA, ROPE)}.get(
                        part, (256 * int(part[2]) if part[0:2] == "cq" else 0, 256))
                    src, how, k = cols_of(b_w_in[0], KD, a, wd)
                elif n < BQ:
                    src, how, k = cols_of(b_w_ukv[0], KVLORA // P, (n - BU) * D, D)
                else:
                    src, how, k = cols_of(b_w_uq[0], QLORA // P, (n - BQ) * 2 * QW, 2 * QW)
                return src, raw[:, sl, 0:size(n)].rearrange(how, k=k)

            def load(n):
                if n >= RAW_SLOTS:
                    sp.wait_ge(lo_done, n - RAW_SLOTS + 1)
                src, dst = place(n, n % RAW_SLOTS)
                sp.dma_start(dst, src).then_inc(raw_in[n % RAW_SLOTS], 16)

            def load_ffn(f, i, n, p=None):
                w_gu = (ffn1_w_gu, ffn2_w_gu)[f % 2][f // 2].rearrange("(k p) f -> p k f", p=P)
                w_d = (ffn1_w_down, ffn2_w_down)[f % 2][f // 2].rearrange("(i j p) f -> i p j f", p=P, j=2)
                for c in range(3):
                    if n + c >= RAW_SLOTS:
                        more = 0 if p is None else 6 * p
                        sp.wait_ge(lo_done, n + c - RAW_SLOTS + 1 + more)
                    sl = (n + c) % RAW_SLOTS
                    if c < 2:
                        at = c * FF + 256 * i if p is None else 512 * p + (c * FF + 256 * i)
                        src = w_gu[:, :, bass.ds(at, 256)]
                        dst = raw[:, sl, :].rearrange("p (k f) -> p k f", k=KD)
                    else:
                        src = w_d[i] if p is None else w_d[bass.ds(2 * p + i, 1)].rearrange("a p j f -> (a p) j f")
                        dst = raw[:, sl, :].rearrange("p (k f) -> p k f", k=2)
                    sp.dma_start(dst, src).then_inc(raw_in[sl], 16)

            def load_first(c):
                dst = raw[:, c, :].rearrange("p (k f) -> p k f", k=KD if c < 2 else 2)
                src = (ffn1_w_gu[0].rearrange("(k p) f -> p k f", p=P)[:, :, c * FF:c * FF + 256] if c < 2 else
                       ffn1_w_down[0].rearrange("(i j p) f -> i p j f", p=P, j=2)[0])
                sp.dma_start(dst, src).then_inc(raw_in[c], 16)

            def load_gb(l):
                for a, w in enumerate((ln_g, ln_b)):
                    sp.dma_start(gb[:, a, :], w[l // 3, l % 3:l % 3 + 1, :].to_broadcast([P, D])).then_inc(gb_in, 16)

            def ffn_loads(f):
                base = FFN_BASE[f]
                load_ffn(f, 0, base)
                with sp.Fori(0, NFI // 2) as p:
                    load_ffn(f, 1, base + 3, p)
                    load_ffn(f, 2, base + 6, p)

            sp.dma_start(ident[:, :], identity).then_inc(ident_in, 16)
            load_first(0)
            for t in range(NT):
                sp.dma_start(x_nat[:, t, :], x[0, t * P:(t + 1) * P, :]).then_inc(x_in[t], 16)
            load_first(1)
            for w, at, n in ((ln_g, G_COL, 48), (ln_b, B_COL, 48)):
                sp.dma_start(prow[at:at + n, :], w.rearrange("a b (k p) -> (a b k) p", p=P)).then_inc(rows_in, 16)
            sp.dma_start(prow[QN_COL:QN_COL + 6, :], b_q_norm.rearrange("a (k p) -> (a k) p", p=P)).then_inc(rows_in, 16)
            sp.dma_start(prow[KVN_COL:KVN_COL + 2, :], b_kv_norm.rearrange("a (k p) -> (a k) p", p=P)).then_inc(rows_in, 16)
            load_first(2)
            with sp.Fori(0, NFI // 2) as p:
                load_ffn(0, 1, 3, p)
                load_ffn(0, 2, 6, p)
            sp.wait_ge(cols_ready, 1)
            load_gb(0)
            sp.dma_start(window_s[:, :], window).then_inc(const_in, 16)
            sp.dma_start(causal_s[:, :], causal).then_inc(const_in, 16)
            sp.dma_start(rope_s[:, :, :, :], rope_tab.rearrange("(t p) a c -> p t a c", p=P)).then_inc(const_in, 16)
            sp.dma_start(nsink[:, :], a_sinks.to_broadcast([P, HEADS])).then_inc(const_in, 16)
            for n in range(A0, AO + 3):
                load(n)
            for n in range(AO + 3, FFN1):
                load(n)
            sp.wait_ge(s_psum, 3 * QUADS)
            load_gb(A_LN)
            for f in (1, 2):
                ffn_loads(f)
                sp.wait_ge(x_ready, NT * FFN_LN[f])
                load_gb(FFN_LN[f])
            for n in range(B0, BO + 3):
                load(n)
            for n in range(BO + 3, FFN3):
                load(n)
            sp.wait_ge(s_psum, 6 * QUADS)
            load_gb(B_LN)
            ffn_loads(3)
            sp.wait_ge(x_ready, NT * (B_LN + 1))
            load_gb(FFN_LN[3])
            out_v = out[0].rearrange("(t p) d -> p t d", p=P)
            for t in range(NT):
                sp.wait_ge(out_ready, t + 1)
                sp.dma_start(out_v[:, t, :], r[:, t, :]).then_inc(out_done, 16)
            sp.wait_ge(out_done, 16 * NT)

        @block.gpsimd
        def _(pool):
            for a, eps in enumerate((LN_EPS, 4 * LN_EPS, RMS_EPS)):
                e = nc.gpsimd.memset(eps_col[:, a:a + 1], eps)
            e.then_inc(eps_ready, 1)
            pool.wait_ge(const_in, 16 * 4)
            for h in range(HEADS):
                slope = 2.0 ** (-8.0 * (h + 1) / HEADS) / WIN_SCALE
                a = nc.gpsimd.tensor_scalar(alibi[:, h, :], window_s[:, :], slope, None, ALU.mult)
            a.then_inc(alibi_ready, 1)
            nc.gpsimd.tensor_scalar(nsink[:, :], nsink[:, :], -1.0, None, ALU.mult).then_inc(sink_neg, 1)

            def rebuild_x(l):
                u = T_LN[l] + 2
                pool.wait_ge(thi_ready, u)
                pool.wait_ge(tlo_ready, u - 1)
                nc.gpsimd.tensor_tensor(xT_lo[:, 4:8, 0:P], xf[:, 1, :, :], xT_hi[:, 4:8, 0:P],
                                        ALU.subtract).then_inc(tlo_ready, 1)
                pool.wait_ge(tlo_ready, u)
                pool.wait_ge(gb_in, 32 * (l + 1))
                for t in range(NT):
                    pool.wait_ge(xhat_ready, 2 * (NT * l + t + 1))
                    nc.gpsimd.tensor_tensor(x_nat[:, t, :], r[:, t, :], gb[:, 0, :], ALU.mult).then_inc(pool_step, 1)
                    pool.wait_ge(pool_step, NT * l + t + 1)
                    nc.gpsimd.tensor_tensor(x_nat[:, t, :], x_nat[:, t, :], gb[:, 1, :], ALU.add).then_inc(x_ready, 1)

            for l in range(B_LN):
                rebuild_x(l)
            pool.wait_ge(x_ready, NT * B_LN)
            pool.wait_ge(kr_first, 1)
            src = khB[NOPE:QW, 0:1, :].to_broadcast([ROPE, HEADS - 1, S])
            nc.gpsimd.tensor_copy(khB[NOPE:QW, 1:HEADS, :], src).then_inc(kr_all, 1)
            pool.wait_ge(kr_all, 1)
            rebuild_x(B_LN)

        @block.tensor
        def _(pe):
            def mm3(dst, a_hi, a_lo, b_hi, b_lo, first, last):
                pe.matmul(dst, a_hi, b_hi, start=first, stop=False)
                pe.matmul(dst, a_hi, b_lo, start=False, stop=False)
                return pe.matmul(dst, a_lo, b_hi, start=False, stop=last)

            def weights(sl, a, n):
                return hi[:, sl, a:a + n], lo[:, sl, a:a + n]

            def transpose_units(src, banks, waits, tiles=range(NT)):
                for t in tiles:
                    for q in range(2):
                        waits(t, q)
                        for k in range(4):
                            tr = pe.transpose(W[:, banks[2 * t + q], k * P:(k + 1) * P],
                                              src[:, t, (4 * q + k) * P:(4 * q + k + 1) * P], ident[:, :])
                        tr.then_inc(tr_ready, 1)

            def transpose_outputs(q):
                for t in range(NT):
                    for k in range(4):
                        tr = pe.transpose(W[:, O_BANKS[NT * q + t], k * P:(k + 1) * P],
                                          r[:, t, (4 * q + k) * P:(4 * q + k + 1) * P], ident[:, :])
                    tr.then_inc(tr_ready, 1)

            def transpose_pairs(src, tiles, banks, waits):
                for t in range(NT):
                    waits(t)
                    for k in range(tiles):
                        tr = pe.transpose(W[:, banks[k // 2], (k % 2) * S + t * P:(k % 2) * S + (t + 1) * P],
                                          src(t, k), ident[:, :])
                        if t == NT - 1 and k % 2:
                            tr.then_inc(tr_ready, 1)

            def after_ln(l, t):
                transpose_units(r, LN_BANKS, lambda t, q: pe.wait_ge(xhat_ready, 2 * (NT * l + t) + q + 1), [t])

            def unit_wait(units, t, k):
                if k % 4 == 0:
                    pe.wait_ge(tlo_ready, units + 2 * t + k // 4 + 1)

            def natural_part(f, half, t, units):
                n = FFN_BASE[f] + half
                pe.wait_ge(lo_done, n + 1)
                for k in range(KD):
                    if half == 0:
                        unit_wait(units, t, k)
                    wh, wl = weights(n % SPLIT_SLOTS, k * 256, 256)
                    mm = mm3(W[:, t, half * S:(half + 1) * S], xT_hi[:, k, t * P:(t + 1) * P], xT_lo[:, k, t * P:(t + 1) * P],
                             wh, wl, k == 0, k == KD - 1)
                if half:
                    mm.then_inc(gu_ready, 1)

            def transpose_hidden(f):
                for t in range(NT):
                    pe.wait_ge(hf_ready, NFT * f + t + 1)
                    for j in range(2):
                        tr = pe.transpose(W[:, 2, j * S + t * P:j * S + (t + 1) * P], hf[:, t, j * P:(j + 1) * P], ident[:, :])
                tr.then_inc(hidden_tr, 1)

            def gate_up(f, t, sl, n, tp=0, np_=0):
                pe.wait_ge(hf_ready, NFT * f + t - 1 + tp)
                for half in range(2):
                    pe.wait_ge(lo_done, n + half + 1 + np_)
                    for k in range(KD):
                        wh, wl = weights(sl[half], k * 256 + (t % 2) * P, P)
                        mm = mm3(W[:, t % 2, half * S:(half + 1) * S], wh, wl, xT_hi[:, k, :], xT_lo[:, k, :],
                                 k == 0, k == KD - 1)
                mm.then_inc(gu_ready, 1)

            def down(t, sl, tt, first, last):
                for c in range(2):
                    wh, wl = weights(sl, (t % 2) * D + c * 512, 512)
                    mm = mm3(W[:, 4 + 2 * tt + c, :], h_hi[:, t % HRING, tt * P:(tt + 1) * P],
                             h_lo[:, t % HRING, tt * P:(tt + 1) * P], wh, wl, first, last)
                return mm

            def down_both(f, t, sl, n, first, tp=0, np_=0):
                pe.wait_ge(hlo_ready, NFT * f + t + 1 + tp)
                pe.wait_ge(lo_done, n + 1 + np_)
                for tt in range(NT):
                    mm = down(t, sl, tt, first, False)
                mm.then_inc(d_done, 1)

            def ffn(f, units, transposes):
                base = FFN_BASE[f]

                def step(i, p=None):
                    n = base + 3 * i
                    tp, np_ = (0, 0) if p is None else (4 * p, 6 * p)
                    s0 = [(n + c) % SPLIT_SLOTS for c in range(3)]
                    gate_up(f, 2 * i, s0, n, tp, np_)
                    if i > 1 and i < NFI - 1:
                        down_both(f, 2 * i - 1, (n - 1) % SPLIT_SLOTS, n - 1, False, tp, np_)
                    if i == 1:
                        transpose_hidden(f)
                    gate_up(f, 2 * i + 1, s0, n, tp, np_)
                    if i == 1:
                        for t in range(2):
                            down_both(f, t, (n - 1) % SPLIT_SLOTS, n - 1, t == 0)
                    if i < NFI - 1:
                        down_both(f, 2 * i, s0[2], n + 2, False, tp, np_)

                transposes(0)
                natural_part(f, 0, 0, units)
                transposes(1)
                natural_part(f, 1, 0, units)
                natural_part(f, 0, 1, units)
                natural_part(f, 1, 1, units)
                step(1)
                with pe.Fori(0, NFI // 2 - 1) as p:
                    step(2, p)
                    step(3, p)
                step(NFI - 1)
                n = base + FFN_CHUNKS - 1
                for tt in range(NT):
                    for t in range(NFT - 3, NFT):
                        m = n - 3 if t == NFT - 3 else n
                        if tt == 0:
                            pe.wait_ge(hlo_ready, NFT * f + t + 1)
                            pe.wait_ge(lo_done, m + 1)
                        mm = down(t, m % SPLIT_SLOTS, tt, False, t == NFT - 1)
                    mm.then_inc(y_ready, 1)

            def two_tiles(at, kt, ah, al, bank):
                for j in range(2):
                    for k in range(kt):
                        wh, wl = at(j, k)
                        mm = mm3(W[:, bank, j * S:(j + 1) * S], wh, wl, ah[:, k, :], al[:, k, :], k == 0, k == kt - 1)
                return mm

            def plain_tiles(n):
                return lambda j, k: weights(n % SPLIT_SLOTS, k * 256 + j * P, P)

            def natural(n, width, kt, ah, al, bank, tiles=range(NT), wait=None):
                for t in tiles:
                    for k in range(kt):
                        if wait is not None:
                            wait(k)
                        wh, wl = weights(n % SPLIT_SLOTS, k * width, width)
                        mm = mm3(W[:, bank, t * width:(t + 1) * width], ah[:, k, t * P:(t + 1) * P],
                                 al[:, k, t * P:(t + 1) * P], wh, wl, k == 0, k == kt - 1)
                return mm

            def scores(step, kh, head, rows):
                a = step % 2
                for j in range(4):
                    mm = pe.matmul(W[:, 4 + j // 2, (j % 2) * S:(j % 2 + 1) * S], qh[0:rows, a, j, P:S],
                                   kh[0:rows, head(j), :], start=True, stop=True)
                    if j % 2:
                        mm.then_inc(s_psum, 1)
                for j in range(4):
                    mm = pe.matmul(W[:, 6, j * P:(j + 1) * P], qh[0:rows, a, j, 0:P],
                                   kh[0:rows, head(j), 0:P], start=True, stop=True)
                mm.then_inc(s_psum, 1)

            def transpose_p(step, rotated=0):
                if step % QUADS:
                    pe.wait_ge(pt_dve, step)
                    pe.wait_ge(pt_act, 2 * step)
                pe.wait_ge(p_ready, 2 * step + 1)
                for j in range(4):
                    for kb in range(2):
                        tr = pe.transpose(W[:, 2 + j // 2, (j % 2) * S + kb * P:(j % 2) * S + (kb + 1) * P],
                                          sc[:, j, P + kb * P:P + (kb + 1) * P], ident[:, :])
                    if j % 2:
                        tr.then_inc(pt_psum, 1)
                pe.wait_ge(p_ready, 2 * step + 2)
                if rotated:
                    pe.wait_ge(qr_act, rotated)
                    pe.wait_ge(qr_dve, rotated)
                for j in range(4):
                    tr = pe.transpose(W[:, p_bank(step), j * P:(j + 1) * P], sc[:, j, 0:P], ident[:, :])
                tr.then_inc(pt_psum, 1)

            def attend(step, v, col):
                pe.wait_ge(pt_dve, step + 1)
                pe.wait_ge(pt_act, 2 * step + 2)
                if step % QUADS:
                    pe.wait_ge(o_out, step)
                for j in range(4):
                    vj = v[:, :, col(j):col(j) + DH]
                    pe.matmul(W[:, 1, 256 + j * DH:256 + (j + 1) * DH], pT[:, 2 * j, :], vj[:, 0, :], start=True, stop=False)
                    pe.matmul(W[:, 1, 256 + j * DH:256 + (j + 1) * DH], pT[:, 2 * j + 1, :], vj[:, 1, :], start=False, stop=True)
                    mm = pe.matmul(W[:, 1, j * DH:(j + 1) * DH], pT[:, 8 + j, :], vj[:, 0, :], start=True, stop=True)
                mm.then_inc(o_psum, 1)

            def last_quad(base, units, first_step, attend_last):
                def part(c, t):
                    n = base + c
                    pe.wait_ge(lo_done, n + 1)
                    pe.wait_ge(tlo_ready, units + NT * (c // 2) + t + 1)
                    for k in range(2):
                        for half in range(2):
                            wh, wl = weights(n % SPLIT_SLOTS, k * D + half * 512, 512)
                            mm = mm3(W[:, 4 + 2 * t + half, :], xT_hi[:, 2 * c + k, t * P:(t + 1) * P],
                                     xT_lo[:, 2 * c + k, t * P:(t + 1) * P], wh, wl,
                                     c == 0 and k == 0, c == O_CHUNKS - 1 and k == 1)
                    return mm

                last = first_step + QUADS - 1
                pe.wait_ge(o_out, last)
                transpose_outputs(0)
                pe.wait_ge(s_masked, last + 1)
                part(0, 0)
                pe.wait_ge(tlo_ready, units + 2)
                transpose_p(last)
                part(0, 1).then_inc(wo_done, 1)
                attend_last()
                part(1, 0)
                pe.wait_ge(o_out, last + 1)
                transpose_outputs(1)
                part(1, 1).then_inc(wo_done, 1)
                for t in range(NT):
                    for c in range(2, O_CHUNKS):
                        mm = part(c, t)
                    mm.then_inc(y_ready, 1)

            def mixer_a():
                for t in range(NT):
                    if t == 0:
                        after_ln(0, 0)
                    pe.wait_ge(lo_done, A0 + 2)
                    mm = natural(A0 + 1, 256, KD, xT_hi, xT_lo, 1, [t], lambda k: unit_wait(T_LN[0], t, k))
                    if t == 0:
                        after_ln(0, 1)
                mm.then_inc(v_psum, 1)
                pe.wait_ge(lo_done, A0 + 1)
                two_tiles(plain_tiles(A0), KD, xT_hi, xT_lo, 7).then_inc(k_psum, 1)

                def project_q(c):
                    if c:
                        pe.wait_ge(q_lower, c)
                        pe.wait_ge(q_upper, c)
                    n = A0 + 2 + c
                    pe.wait_ge(lo_done, n + 1)
                    two_tiles(plain_tiles(n), KD, xT_hi, xT_lo, 0).then_inc(q_psum, 1)

                def score(c):
                    pe.wait_ge(q_lower, c + 1)
                    pe.wait_ge(q_upper, c + 1)
                    if c:
                        pe.wait_ge(s_masked, c)
                    else:
                        pe.wait_ge(k_lower, 1)
                        pe.wait_ge(k_upper, 1)
                    scores(c, khA, lambda j: c, DH)

                project_q(0)
                score(0)
                for c in range(QUADS - 1):
                    project_q(c + 1)
                    transpose_p(c)
                    score(c + 1)
                    if c == 0:
                        pe.wait_ge(v_out0, 1)
                    attend(c, vA, lambda j: c * DH)
                last_quad(AO, T_AO, 0, lambda: attend(QUADS - 1, vA, lambda j: (QUADS - 1) * DH))

            def mixer_b():
                kt_q, kt_kv = QLORA // P, KVLORA // P
                after_ln(3, 0)
                for t in range(NT):
                    for c in range(2):
                        if t == 0 and c == 1:
                            after_ln(3, 1)
                        pe.wait_ge(lo_done, B0 + c + 1)
                        mm = natural(B0 + c, 256, KD, xT_hi, xT_lo, NAT_BANK[NAT_ORDER[c]], [t],
                                     lambda k: unit_wait(T_LN[3], t, k))
                        if t == NT - 1:
                            mm.then_inc(nat_psum, 1)
                for c in range(2, 5):
                    part = NAT_ORDER[c]
                    pe.wait_ge(lo_done, B0 + c + 1)
                    natural(B0 + c, ROPE if part == "kr" else 256, KD, xT_hi, xT_lo, NAT_BANK[part]).then_inc(nat_psum, 1)
                    if c == 2:
                        transpose_pairs(lambda t, k: c_nat[:, t, QLORA + k * P:QLORA + (k + 1) * P], kt_kv, CKV_BANKS,
                                        lambda t: pe.wait_ge(c_norm, t + 1))
                for t in range(NT):
                    pe.wait_ge(nat_out, 4)
                    tr = pe.transpose(W[0:ROPE, 3, t * P:(t + 1) * P], kr_nat[:, t, :], ident[:, :])
                tr.then_inc(krt_psum, 1)
                pe.wait_ge(tlo_ready, T_CKV + 1)
                for u in range(2):
                    n, sl = BU + u, (BU + u) % SPLIT_SLOTS
                    pe.wait_ge(lo_done, n + 1)

                    def head_cols(ring, k, h, part, count):
                        at = k * D + part * 8 * DH + h * DH
                        return ring[:, sl, at:at + count * DH]

                    for b in range(2):
                        if u:
                            pe.wait_ge(k_lower, 1 + b + 1)
                            pe.wait_ge(k_upper, 1 + b + 1)
                        else:
                            pe.wait_ge(nat_out, b + 1)
                        mm = two_tiles(lambda j, k: (head_cols(hi, k, 4 * b + 2 * j, 0, 2), head_cols(lo, k, 4 * b + 2 * j, 0, 2)),
                                       kt_kv, h_hi, h_lo, b)
                        mm.then_inc(k_psum, 1)
                    for t in range(NT):
                        if u:
                            pe.wait_ge((v_out0, v_out1)[t], 2 - t)
                        else:
                            pe.wait_ge(nat_out, (3, 5)[t])
                        for k in range(kt_kv):
                            mm = mm3(W[:, 6 + t, :], h_hi[:, k, t * P:(t + 1) * P], h_lo[:, k, t * P:(t + 1) * P],
                                     head_cols(hi, k, 0, 1, 8), head_cols(lo, k, 0, 1, 8), k == 0, k == kt_kv - 1)
                        mm.then_inc(v_psum, 1)
                    if u == 0:
                        transpose_pairs(lambda t, k: c_nat[:, t, k * P:(k + 1) * P], kt_q, CQ_BANKS,
                                        lambda t: pe.wait_ge(c_norm, NT + t + 1))

                def project_q(c):
                    if c == 0:
                        pe.wait_ge(tlo_ready, T_CQ + 3)
                        pe.wait_ge(v_out1, 2)
                    else:
                        pe.wait_ge(pt_act, 2 * (QUADS + c - 1))
                    s0 = (BQ + 2 * c) % SPLIT_SLOTS
                    pe.wait_ge(lo_done, BQ + 2 * c + 2)
                    for t in range(NT):
                        for k in range(kt_q):
                            wh, wl = (ring[:, s0:s0 + 2, k * 2 * QW + 2 * NOPE:(k + 1) * 2 * QW] for ring in (hi, lo))
                            mm = mm3(W[:, 7, t * P:(t + 1) * P], xT_hi[:, k, t * P:(t + 1) * P], xT_lo[:, k, t * P:(t + 1) * P],
                                     wh, wl, k == 0, k == kt_q - 1)
                    mm.then_inc(qr_psum, 1)
                    if c == 0:
                        pe.wait_ge(k_lower, 4)
                        pe.wait_ge(k_upper, 4)
                    else:
                        pe.wait_ge(q_lower, QUADS + c)
                        pe.wait_ge(q_upper, QUADS + c)
                    for j in range(2):
                        for k in range(kt_q):
                            wh, wl = weights((BQ + 2 * c + j) % SPLIT_SLOTS, k * 2 * QW, 2 * NOPE)
                            mm = mm3(W[:, 0, j * S:(j + 1) * S], wh, wl, xT_hi[:, k, :], xT_lo[:, k, :], k == 0, k == kt_q - 1)
                    mm.then_inc(q_psum, 1)
                    pe.wait_ge(qr_ready, c + 1)
                    for t in range(NT):
                        tr = pe.transpose(W[:, 7, S + t * P:S + (t + 1) * P], qr_nat[:, t, :, :].rearrange("p h d -> p (h d)"), ident[:, :])
                    tr.then_inc(qrt_psum, 1)

                def score(c):
                    pe.wait_ge(q_lower, QUADS + c + 1)
                    pe.wait_ge(q_upper, QUADS + c + 1)
                    pe.wait_ge(qr_act, c + 1)
                    pe.wait_ge(qr_dve, c + 1)
                    if c:
                        pe.wait_ge(s_masked, QUADS + c)
                    else:
                        pe.wait_ge(k_lower, 5)
                        pe.wait_ge(k_upper, 5)
                        pe.wait_ge(kr_all, 1)
                    scores(QUADS + c, khB, lambda j: 4 * c + j, QW)

                project_q(0)
                score(0)
                for c in range(QUADS - 1):
                    project_q(c + 1)
                    transpose_p(QUADS + c, c + 2)
                    if c == 0:
                        pe.wait_ge(v_out0, 3)
                    attend(QUADS + c, vB, lambda j: (4 * c + j) * DH)
                    score(c + 1)
                last_quad(BO, T_BO, QUADS, lambda: attend(2 * QUADS - 1, vB, lambda j: (4 * QUADS - 4 + j) * DH))

            def first_transposes(t):
                if t == 0:
                    pe.wait_ge(ident_in, 16)
                    transpose_units(x_nat, LN_BANKS, lambda t, q: pe.wait_ge(x_in[t], 16))
                else:
                    pe.wait_ge(rows_in, 64)
                    pe.transpose(W[:, 7, 0:N_COL], prow[0:N_COL, :], ident[0:N_COL, 0:N_COL]).then_inc(cols_tr, 1)

            ffn(0, T_X, first_transposes)
            mixer_a()
            ffn(1, T_LN[1], lambda t: after_ln(A_LN, t))
            ffn(2, T_LN[2], lambda t: after_ln(2, t))
            mixer_b()
            ffn(3, T_LN[4], lambda t: after_ln(B_LN, t))

        @block.scalar
        def _(act):
            nxt = [0]

            def round_chunk(n, p=None, free=None):
                more = 0 if p is None else 2 * p
                act.wait_ge(raw_in[n % RAW_SLOTS], 16 * (n // RAW_SLOTS + 1) + 16 * more)
                if n >= SPLIT_SLOTS:
                    who, value = consumed(n - SPLIT_SLOTS)
                    act.wait_ge(who, value if p is None else value + 4 * p)
                for src, dst in zip(parts(n, (raw, n % RAW_SLOTS)), parts(n, (hi, n % SPLIT_SLOTS))):
                    op = nc.scalar.copy(dst, src)
                op.then_inc(hi_done, 1)

            def rounds_to(n):
                while nxt[0] <= min(n, CHUNKS - 1):
                    round_chunk(nxt[0])
                    nxt[0] += 1

            def hidden(f, t, tp=0):
                act.wait_ge(gu_ready, NFT * f + t + 1 + tp)
                nc.scalar.activation(sil[:, t % 2, :], W[:, t % 2, 0:S], ACT.Silu).then_inc(sil_ready, 1)
                act.wait_ge(hf_ready, NFT * f + t + 1 + tp)
                if t >= HRING:
                    act.wait_ge(d_done, D_DONE * f + t - HRING + 1 + tp)
                nc.scalar.copy(h_hi[:, t % HRING, :], hf[:, t % 2, :]).then_inc(hhi_ready, 1)

            def hidden_natural(f, t):
                act.wait_ge(gu_ready, NFT * f + t + 1)
                nc.scalar.activation(sil[:, t, :], W[:, t, 0:S], ACT.Silu).then_inc(sil_ready, 1)

            def ffn(f):
                base = FFN_BASE[f]

                def step(i, p=None):
                    n, tp = base + 3 * i, 0 if p is None else 4 * p
                    if i == 0:
                        hidden_natural(f, 0)
                    for c in range(3):
                        if n + LOOKAHEAD + c < min(base + FFN_CHUNKS + 2, CHUNKS):
                            round_chunk(n + LOOKAHEAD + c, p)
                        if i == 0 and c == 1:
                            hidden_natural(f, 1)
                        if i == 1 and c == 0:
                            act.wait_ge(hidden_tr, f + 1)
                            nc.scalar.copy(h_hi[:, 0:2, :], W[:, 2, :].rearrange("p (j n) -> p j n", j=2)).then_inc(hhi_ready, 2)
                        if i and c != 1:
                            hidden(f, 2 * i + c // 2, tp)

                load_table(ACT.Silu)
                step(0)
                step(1)
                with act.Fori(0, NFI // 2 - 1) as p:
                    step(2, p)
                    step(3, p)
                step(NFI - 1)
                nxt[0] = base + FFN_CHUNKS + 2

            def load_table(func):
                nc.scalar.activation(warm[:, :], eps_col[:, 0:1], func)

            def square_root(e, v, at, eps):
                nc.scalar.activation(inv_s[:, at], v, ACT.Sqrt, bias=eps_col[:, eps:eps + 1]).then_inc(isq_act, 1)

            def layer_norm(l):
                load_table(ACT.Sqrt)

                def root(t):
                    act.wait_ge(ln_step, 4 * (NT * l + t) + 4)
                    square_root(ISQ_LN[l] + t, mv[:, t, 1:2], slice(t, t + 1), 1 if l in FFN_LN else 0)

                def affine(t, q):
                    act.wait_ge(tr_ready, T_LN[l] + 2 * t + q + 1)
                    if t:
                        act.wait_ge(tlo_ready, T_LN[l] + 1)
                    for k in range(4):
                        c = l * KD + 4 * q + k
                        op = nc.scalar.activation(xf[:, q, k, :], W[:, LN_BANKS[2 * t + q], k * P:(k + 1) * P], ACT.Identity,
                                                  bias=cols[:, B_COL + c:B_COL + c + 1], scale=cols[:, G_COL + c:G_COL + c + 1])
                    op.then_inc(xf_ready, 1)

                def round_unit(t, q):
                    if t and q:
                        act.wait_ge(xf_last, LN_SEQ[l] + 1)
                    else:
                        act.wait_ge(xf_ready, 3 * LN_SEQ[l] + 2 * t + q + 1)
                    nc.scalar.copy(xT_hi[:, 4 * q:4 * q + 4, t * P:(t + 1) * P], xf[:, q, :, :]).then_inc(thi_ready, 1)

                root(0)
                if l not in T_LN:
                    root(1)
                    return
                affine(0, 0)
                round_unit(0, 0)
                affine(0, 1)
                if l in FFN_LN:
                    root(1)
                round_unit(0, 1)
                if l not in FFN_LN:
                    root(1)
                affine(1, 0)
                round_unit(1, 0)
                round_unit(1, 1)

            def units_plain(t0, banks):
                for u in range(4):
                    t, q = divmod(u, 2)
                    act.wait_ge(tr_ready, t0 + u + 1)
                    nc.scalar.copy(xT_hi[:, 4 * q:4 * q + 4, t * P:(t + 1) * P],
                                   W[:, banks[u], :].rearrange("p (k n) -> p k n", k=4)).then_inc(thi_ready, 1)

            def pairs_scaled(t0, n, banks, dst, col):
                for p in range(n):
                    act.wait_ge(tr_ready, t0 + p + 1)
                    for k in range(2):
                        c = col + 2 * p + k
                        op = nc.scalar.mul(dst[:, 2 * p + k, :], W[:, banks[p], k * S:(k + 1) * S], cols[:, c:c + 1])
                    op.then_inc(thi_ready, 1)

            def lower_heads(dst, bank, done):
                nc.scalar.copy(dst, W[0:DH, bank, :].rearrange("p (j n) -> p j n", j=2)).then_inc(done, 1)

            def exps(step, scale, sinks):
                act.wait_ge(negm_ready, step + 1)
                for t in (1, 0):
                    for j in range(4):
                        s = sc[:, j, P:3 * P] if t else sc[:, j, 0:P]
                        op = nc.scalar.activation(s, s, ACT.Exp, bias=negm[:, t, j:j + 1], scale=scale,
                                                  accum_out=rsum[:, t, j:j + 1])
                    op.then_inc(p_ready, 1)
                if sinks:
                    act.wait_ge(es_arg, step + 1)
                    nc.scalar.activation(esink[:, :, :], esink[:, :, :], ACT.Exp).then_inc(es_ready, 1)

            def copy_pt(step):
                if step:
                    act.wait_ge(o_psum, step)
                for b, (bank, at) in enumerate(((3, 4), (p_bank(step), 8))):
                    act.wait_ge(pt_psum, 3 * step + 2 + b)
                    nc.scalar.copy(pT[:, at:at + 4, :], W[:, bank, :].rearrange("p (i n) -> p i n", i=4)).then_inc(pt_act, 1)

            def output_units(t0, q):
                for t in range(NT):
                    u = NT * q + t
                    act.wait_ge(tr_ready, t0 + u + 1)
                    nc.scalar.copy(xT_hi[:, 4 * q:4 * q + 4, t * P:(t + 1) * P],
                                   W[:, O_BANKS[u], :].rearrange("p (k n) -> p k n", k=4)).then_inc(thi_ready, 1)

            def last_quad(t0, base, step):
                copy_pt(step)
                rounds_to(base + LOOKAHEAD)
                output_units(t0, 1)
                for c in range(1, O_CHUNKS):
                    rounds_to(base + c + LOOKAHEAD)

            def mixer_a():
                rounds_to(A0 + LOOKAHEAD)
                act.wait_ge(k_psum, 1)
                lower_heads(khA[0:DH, 0:KV_HEADS:2, :], 7, k_lower)
                rounds_to(A0 + 1 + LOOKAHEAD)
                for c in range(QUADS):
                    act.wait_ge(q_psum, c + 1)
                    if c == 0:
                        act.wait_ge(x_ready, NT * A_LN)
                    if c >= 2:
                        act.wait_ge(s_psum, 3 * (c - 1))
                    lower_heads(qh[0:DH, c % 2, 0:4:2, :], 0, q_lower)
                    if c:
                        copy_pt(c - 1)
                    else:
                        load_table(ACT.Exp)
                    rounds_to(A0 + 2 + c + LOOKAHEAD)
                    if c == QUADS - 1:
                        output_units(T_AO, 0)
                    exps(c, WIN_SCALE, True)
                last_quad(T_AO, AO, QUADS - 1)

            def mixer_b():
                rounds_to(B0 + LOOKAHEAD)
                rounds_to(B0 + 1 + LOOKAHEAD)

                def squares(a, first, width, after):
                    act.wait_ge(nat_out, after)
                    for t in range(NT):
                        op = nc.scalar.activation(junk[:, t, 0:width], c_nat[:, t, first:first + width], ACT.Square,
                                                  scale=float(width) ** -0.5, accum_out=msq[:, a, t:t + 1])
                    op.then_inc(msq_ready, 1)
                    act.wait_ge(msq_ready, a + 1)
                    square_root(ISQ_RMS[a], msq[:, a, :], slice(0, NT), 2)

                squares(0, QLORA, KVLORA, 1)
                rounds_to(B0 + 2 + LOOKAHEAD)
                pairs_scaled(T_CKV, 1, CKV_BANKS, h_hi, KVN_COL)
                rounds_to(B0 + 4 + LOOKAHEAD)
                squares(1, 0, QLORA, 5)
                act.wait_ge(krt_psum, 1)
                nc.scalar.copy(khB[NOPE:QW, 0, :], W[0:ROPE, 3, 0:S]).then_inc(kr_first, 1)
                for u in range(2):
                    rounds_to(BU + u + LOOKAHEAD)
                    for b in range(2):
                        act.wait_ge(k_psum, 1 + 2 * u + b + 1)
                        h = 8 * u + 4 * b
                        lower_heads(khB[0:DH, h:h + 4:2, :], b, k_lower)
                    act.wait_ge(v_psum, 1 + 2 * u + 1)
                    nc.scalar.copy(vB[:, 0, u * 512:(u + 1) * 512], W[:, 6, :]).then_inc(v_out0, 1)
                    if u == 0:
                        pairs_scaled(T_CQ, 3, CQ_BANKS, xT_hi, QN_COL)
                rounds_to(BQ + 1 + LOOKAHEAD)
                for c in range(QUADS):
                    act.wait_ge(q_psum, QUADS + c + 1)
                    if c == 0:
                        act.wait_ge(x_ready, NT * B_LN)
                    if c >= 2:
                        act.wait_ge(s_psum, 3 * (QUADS + c - 1))
                    lower_heads(qh[0:DH, c % 2, 0:4:2, :], 0, q_lower)
                    act.wait_ge(qrt_psum, c + 1)
                    for j in range(2):
                        op = nc.scalar.copy(qh[NOPE:QW, c % 2, j, :], W[j * ROPE:(j + 1) * ROPE, 7, S:2 * S])
                    op.then_inc(qr_act, 1)
                    if c:
                        copy_pt(QUADS + c - 1)
                    if c:
                        rounds_to(BQ + 2 * c + 1 + LOOKAHEAD)
                    else:
                        load_table(ACT.Exp)
                    if c == QUADS - 1:
                        output_units(T_BO, 0)
                    exps(QUADS + c, MLA_SCALE, False)
                last_quad(T_BO, BO, 2 * QUADS - 1)

            act.wait_ge(eps_ready, 1)
            load_table(ACT.Silu)
            rounds_to(0)
            units_plain(T_X, LN_BANKS)
            rounds_to(LOOKAHEAD - 1)
            act.wait_ge(cols_tr, 1)
            nc.scalar.copy(cols[:, :], W[:, 7, 0:N_COL]).then_inc(cols_ready, 1)
            ffn(0)
            act.wait_ge(cols_ready, 1)
            layer_norm(0)
            mixer_a()
            layer_norm(A_LN)
            ffn(1)
            layer_norm(2)
            rounds_to(FFN2 + 2)
            ffn(2)
            layer_norm(3)
            mixer_b()
            layer_norm(B_LN)
            ffn(3)
            layer_norm(LNS - 1)

        @block.vector
        def _(dve):
            nxt = [0]

            def rest_of_chunk(n, p=None):
                dve.wait_ge(hi_done, n + 1 if p is None else n + 1 + 6 * p)
                sl = n % SPLIT_SLOTS
                for src, top, dst in zip(parts(n, (raw, n % RAW_SLOTS)), parts(n, (hi, sl)), parts(n, (lo, sl))):
                    op = nc.vector.tensor_tensor(dst, src, top, ALU.subtract)
                op.then_inc(lo_done, 1)

            def rests_to(n):
                while nxt[0] <= min(n, CHUNKS - 1):
                    rest_of_chunk(nxt[0])
                    nxt[0] += 1

            def hidden(f, t, tp=0):
                dve.wait_ge(sil_ready, NFT * f + t + 1 + tp)
                nc.vector.tensor_tensor(hf[:, t % 2, :], sil[:, t % 2, :], W[:, t % 2, S:2 * S], ALU.mult).then_inc(hf_ready, 1)

            def hidden_rest(f, t, tp=0):
                dve.wait_ge(hhi_ready, NFT * f + t + 1 + tp)
                nc.vector.tensor_tensor(h_lo[:, t % HRING, :], hf[:, t % 2, :], h_hi[:, t % HRING, :], ALU.subtract).then_inc(hlo_ready, 1)

            def ffn(f):
                base = FFN_BASE[f]

                def step(i, p=None):
                    n, tp = base + 3 * i + LOOKAHEAD, 0 if p is None else 4 * p
                    if i == 0:
                        hidden(f, 0)
                        rest_of_chunk(n)
                        rest_of_chunk(n + 1)
                        hidden(f, 1)
                        rest_of_chunk(n + 2)
                        return
                    if n < CHUNKS:
                        rest_of_chunk(n, p)
                    if i == 1:
                        dve.wait_ge(hhi_ready, NFT * f + 2)
                        nc.vector.tensor_tensor(h_lo[:, 0:2, :], W[:, 2, :].rearrange("p (j n) -> p j n", j=2),
                                                h_hi[:, 0:2, :], ALU.subtract).then_inc(hlo_ready, 2)
                    hidden(f, 2 * i, tp)
                    if n < CHUNKS:
                        rest_of_chunk(n + 1, p)
                    hidden_rest(f, 2 * i, tp)
                    if i < NFI - 1:
                        rest_of_chunk(n + 2, p)
                    hidden(f, 2 * i + 1, tp)
                    hidden_rest(f, 2 * i + 1, tp)

                step(0)
                step(1)
                with dve.Fori(0, NFI // 2 - 1) as p:
                    step(2, p)
                    step(3, p)
                step(NFI - 1)
                nxt[0] = base + FFN_CHUNKS + 2

            def inverse_sqrt(e, v, eps, at):
                nc.vector.tensor_scalar(inv_v[:, at], v, eps, None, ALU.add).then_inc(isq_dve, 1)
                dve.wait_ge(isq_act, e + 1)
                nc.vector.reciprocal(inv_e[:, at], inv_s[:, at]).then_inc(isq_dve, 1)
                dve.wait_ge(isq_dve, 4 * e + 2)
                for t in range(at.start, at.stop):
                    op = nc.vector.scalar_tensor_tensor(out=inv_t[:, t:t + 1], in0=inv_e[:, t:t + 1], scalar=inv_v[:, t:t + 1],
                                                        in1=inv_e[:, t:t + 1], op0=ALU.mult, op1=ALU.mult)
                op.then_inc(isq_dve, 1)
                dve.wait_ge(isq_dve, 4 * e + 3)
                nc.vector.tensor_scalar(inv_t[:, at], inv_t[:, at], -0.5, 1.5, ALU.mult, ALU.add).then_inc(isq_dve, 1)
                dve.wait_ge(isq_dve, 4 * e + 4)
                nc.vector.tensor_tensor(rstd[:, at], inv_e[:, at], inv_t[:, at], ALU.mult).then_inc(rstd_ready, 1)
                dve.wait_ge(rstd_ready, e + 1)

            def layer_norm(l, ffn_before):
                two = 2.0 if ffn_before else 1.0
                for t in range(NT):
                    s0 = 4 * (NT * l + t)
                    dve.wait_ge(y_ready, NT * l + t + 1)
                    if l:
                        dve.wait_ge(x_ready, NT * (l - 1) + t + 1)
                    else:
                        dve.wait_ge(x_in[t], 16)
                    for a in range(2):
                        half = slice(a * 512, (a + 1) * 512)
                        nc.vector.scalar_tensor_tensor(out=r[:, t, half], in0=x_nat[:, t, half], scalar=two * ALPHA,
                                                       in1=W[:, 4 + 2 * t + a, :], op0=ALU.mult, op1=ALU.add).then_inc(ln_step, 1)
                    for a in range(2):
                        dve.wait_ge(ln_step, s0 + a + 1)
                        op = nc.vector.bn_stats(bn[:, t, a, :], r[:, t, a * 512:(a + 1) * 512])
                    op.then_inc(ln_step, 1)
                    if t and l in T_LN:
                        rest_of_unit(l, 0)
                    dve.wait_ge(ln_step, s0 + 3)
                    nc.vector.bn_aggr(mv[:, t, :], bn[:, t, :, :].rearrange("p a s -> p (a s)")).then_inc(ln_step, 1)
                    dve.wait_ge(ln_step, s0 + 4)
                    inverse_sqrt(ISQ_LN[l] + t, mv[:, t, 1:2], two * two * LN_EPS, slice(t, t + 1))
                    for a in range(2):
                        half = slice(a * 512, (a + 1) * 512)
                        nc.vector.tensor_scalar(r[:, t, half], r[:, t, half], mv[:, t, 0:1], rstd[:, t:t + 1],
                                                ALU.subtract, ALU.mult).then_inc(xhat_ready, 1)
                if l in T_LN:
                    dve.wait_ge(tr_ready, T_LN[l] + 4)
                    dve.wait_ge(tlo_ready, T_LN[l] + 2)
                    for k in range(4):
                        c = l * KD + 4 + k
                        op = nc.vector.tensor_scalar(xf[:, 1, k, :], W[:, LN_BANKS[3], k * P:(k + 1) * P],
                                                     cols[:, G_COL + c:G_COL + c + 1], cols[:, B_COL + c:B_COL + c + 1],
                                                     ALU.mult, ALU.add)
                    op.then_inc(xf_last, 1)
                    rest_of_unit(l, 2)
                    rest_of_unit(l, 3)

            def rest_of_unit(l, u):
                t, q = divmod(u, 2)
                dve.wait_ge(thi_ready, T_LN[l] + u + 1)
                at = xT_lo[:, 4 * q:4 * q + 4, t * P:(t + 1) * P]
                nc.vector.tensor_tensor(at, xf[:, q, :, :], xT_hi[:, 4 * q:4 * q + 4, t * P:(t + 1) * P],
                                        ALU.subtract).then_inc(tlo_ready, 1)

            def units_plain(t0, banks):
                for u in range(4):
                    t, q = divmod(u, 2)
                    dve.wait_ge(thi_ready, t0 + u + 1)
                    nc.vector.tensor_tensor(xT_lo[:, 4 * q:4 * q + 4, t * P:(t + 1) * P],
                                            W[:, banks[u], :].rearrange("p (k n) -> p k n", k=4),
                                            xT_hi[:, 4 * q:4 * q + 4, t * P:(t + 1) * P], ALU.subtract).then_inc(tlo_ready, 1)

            def pairs_scaled(t0, n, banks, dst, src, col):
                for p in range(n):
                    dve.wait_ge(thi_ready, t0 + p + 1)
                    for k in range(2):
                        c = col + 2 * p + k
                        op = nc.vector.scalar_tensor_tensor(out=dst[:, 2 * p + k, :], in0=W[:, banks[p], k * S:(k + 1) * S],
                                                            scalar=cols[:, c:c + 1], in1=src[:, 2 * p + k, :],
                                                            op0=ALU.mult, op1=ALU.subtract)
                    op.then_inc(tlo_ready, 1)

            def upper_heads(dst, bank, done):
                nc.vector.tensor_copy(dst, W[DH:P, bank, :].rearrange("p (j n) -> p j n", j=2)).then_inc(done, 1)

            def maxima(step, bias):
                for t in (1, 0):
                    for j in range(4):
                        if t and j % 2 == 0:
                            dve.wait_ge(s_psum, 3 * step + j // 2 + 1)
                        if t == 0 and j == 0:
                            dve.wait_ge(s_psum, 3 * step + 3)
                        if t:
                            dst, src, b = sc[:, j, P:3 * P], W[:, 4 + j // 2, (j % 2) * S:(j % 2 + 1) * S], bias(j)
                        else:
                            dst, src, b = sc[:, j, 0:P], W[:, 6, j * P:(j + 1) * P], bias(j)[:, P:2 * P]
                        op = nc.vector.tensor_tensor_reduce(out=dst, in0=src, in1=b, scale=1.0, scalar=NEG, op0=ALU.add,
                                                            op1=ALU.max, accum_out=smax[:, t, j:j + 1])
                op.then_inc(s_masked, 1)

            def copy_pt(step):
                dve.wait_ge(pt_psum, 3 * step + 1)
                nc.vector.tensor_copy(pT[:, 0:4, :], W[:, 2, :].rearrange("p (i n) -> p i n", i=4)).then_inc(pt_dve, 1)

            def normalise(step, c):
                dve.wait_ge(o_psum, step + 1)
                dve.wait_ge(den_step, DEN[step])
                if c == 0:
                    dve.wait_ge(x_ready, NT * (A_LN if step == 0 else B_LN))
                nc.vector.tensor_tensor(
                    r[:, :, c * 4 * DH:(c + 1) * 4 * DH].rearrange("p t (j d) -> p t j d", j=4),
                    W[:, 1, :].rearrange("p (t j d) -> p t j d", t=NT, j=4),
                    rden[:, :, :].unsqueeze(3).to_broadcast([P, NT, 4, DH]), ALU.mult).then_inc(o_out, 1)

            def output_units(t0, q):
                for t in range(NT):
                    u = NT * q + t
                    dve.wait_ge(thi_ready, t0 + u + 1)
                    nc.vector.tensor_tensor(xT_lo[:, 4 * q:4 * q + 4, t * P:(t + 1) * P],
                                            W[:, O_BANKS[u], :].rearrange("p (k n) -> p k n", k=4),
                                            xT_hi[:, 4 * q:4 * q + 4, t * P:(t + 1) * P], ALU.subtract).then_inc(tlo_ready, 1)

            def last_quad(t0, base, finish):
                output_units(t0, 0)
                finish()
                output_units(t0, 1)
                for c in range(O_CHUNKS):
                    rests_to(base + c + LOOKAHEAD)

            def mixer_a():
                rests_to(A0 + LOOKAHEAD)
                dve.wait_ge(v_psum, 1)
                nc.vector.tensor_copy(vA[:, :, :], W[:, 1, :].rearrange("p (t d) -> p t d", t=NT)).then_inc(v_out0, 1)
                dve.wait_ge(k_psum, 1)
                upper_heads(khA[0:DH, 1:KV_HEADS:2, :], 7, k_upper)
                rests_to(A0 + 1 + LOOKAHEAD)
                dve.wait_ge(alibi_ready, 1)
                dve.wait_ge(sink_neg, 1)

                def finish(c, n):
                    dve.wait_ge(es_ready, c + 1)
                    nc.vector.tensor_tensor(rden[:, :, :], rsum[:, :, :], esink[:, :, :], ALU.add).then_inc(den_step, 1)
                    dve.wait_ge(den_step, 2 * c + 1)
                    nc.vector.reciprocal(rden[:, :, :], rden[:, :, :]).then_inc(den_step, 1)
                    copy_pt(c)
                    rests_to(n)
                    normalise(c, c)

                for c in range(QUADS):
                    dve.wait_ge(q_psum, c + 1)
                    if c == 0:
                        dve.wait_ge(x_ready, NT * A_LN)
                    if c >= 2:
                        dve.wait_ge(s_psum, 3 * (c - 1))
                    upper_heads(qh[0:DH, c % 2, 1:4:2, :], 0, q_upper)
                    if c:
                        finish(c - 1, A0 + 2 + c + LOOKAHEAD)
                    else:
                        rests_to(A0 + 2 + LOOKAHEAD)
                    maxima(c, lambda j: alibi[:, 4 * c + j, :])
                    dve.wait_ge(s_masked, c + 1)
                    sinks = nsink[:, 4 * c:4 * c + 4].unsqueeze(1).to_broadcast([P, NT, 4])
                    nc.vector.scalar_tensor_tensor(out=negm[:, :, :], in0=smax[:, :, :], scalar=-WIN_SCALE, in1=sinks,
                                                   op0=ALU.mult, op1=ALU.min).then_inc(negm_ready, 1)
                    dve.wait_ge(negm_ready, c + 1)
                    nc.vector.tensor_tensor(esink[:, :, :], negm[:, :, :], sinks, ALU.subtract).then_inc(es_arg, 1)
                last_quad(T_AO, AO, lambda: finish(QUADS - 1, AO + LOOKAHEAD))

            def rotate(x1, x2, o1, o2, shape, start):
                heads = shape[1]
                ta = rope_t[:, 0, :, 0:heads, :]
                tb = rope_t[:, 1, :, 0:heads, :]
                cos, sin = (rope_s[:, :, a:a + 1, :].to_broadcast([P, NT, heads, HR]) for a in range(2))
                for o, (fa, fb, op) in ((o1, (cos, sin, ALU.subtract)), (o2, (sin, cos, ALU.add))):
                    nc.vector.tensor_tensor(ta, x1, fa, ALU.mult)
                    nc.vector.tensor_tensor(tb, x2, fb, ALU.mult).then_inc(rope_step, 1)
                    start += 1
                    dve.wait_ge(rope_step, start)
                    last = nc.vector.tensor_tensor(o, ta, tb, op)
                    if o is o1:
                        last.then_inc(rope_step, 1)
                        start += 1
                        dve.wait_ge(rope_step, start)
                return last

            def mixer_b():
                rests_to(B0 + LOOKAHEAD)

                def nat_copy(c):
                    part = NAT_ORDER[c]
                    at = QLORA if part == "ckv" else 256 * int(part[2])
                    dve.wait_ge(nat_psum, c + 1)
                    nc.vector.tensor_copy(c_nat[:, :, at:at + 256],
                                          W[:, NAT_BANK[part], :].rearrange("p (t d) -> p t d", t=NT)).then_inc(nat_out, 1)

                def rms(a, first, width):
                    dve.wait_ge(msq_ready, a + 1)
                    inverse_sqrt(ISQ_RMS[a], msq[:, a, :], RMS_EPS, slice(0, NT))
                    for t in range(NT):
                        nc.vector.tensor_scalar(c_nat[:, t, first:first + width], c_nat[:, t, first:first + width],
                                                rstd[:, t:t + 1], None, ALU.mult).then_inc(c_norm, 1)

                nat_copy(0)
                rms(0, QLORA, KVLORA)
                nat_copy(1)
                rests_to(B0 + 1 + LOOKAHEAD)
                nat_copy(2)
                pairs_scaled(T_CKV, 1, CKV_BANKS, h_lo, h_hi, KVN_COL)
                rests_to(B0 + 2 + LOOKAHEAD)
                dve.wait_ge(nat_psum, 4)
                dve.wait_ge(x_ready, NT * B_LN)
                ps = W[:, NAT_BANK["kr"], 0:NT * ROPE].rearrange("p (t a c) -> p t a c", t=NT, a=2)
                rotate(ps[:, :, 0:1, :], ps[:, :, 1:2, :], kr_nat[:, :, 0:HR].unsqueeze(2), kr_nat[:, :, HR:ROPE].unsqueeze(2),
                       [NT, 1], 0).then_inc(nat_out, 1)
                rests_to(B0 + 4 + LOOKAHEAD)
                nat_copy(4)
                rms(1, 0, QLORA)
                for u in range(2):
                    rests_to(BU + u + LOOKAHEAD)
                    for b in range(2):
                        dve.wait_ge(k_psum, 1 + 2 * u + b + 1)
                        h = 8 * u + 4 * b
                        upper_heads(khB[0:DH, h + 1:h + 4:2, :], b, k_upper)
                    dve.wait_ge(v_psum, 1 + 2 * u + 2)
                    nc.vector.tensor_copy(vB[:, 1, u * 512:(u + 1) * 512], W[:, 7, :]).then_inc(v_out1, 1)
                    if u == 0:
                        pairs_scaled(T_CQ, 3, CQ_BANKS, xT_lo, xT_hi, QN_COL)
                rests_to(BQ + 1 + LOOKAHEAD)

                def finish(c, n):
                    step = QUADS + c
                    dve.wait_ge(p_ready, 2 * step + 2)
                    nc.vector.reciprocal(rden[:, :, :], rsum[:, :, :]).then_inc(den_step, 1)
                    rests_to(n)
                    normalise(step, c)

                for c in range(QUADS):
                    dve.wait_ge(qr_psum, c + 1)
                    if c:
                        dve.wait_ge(qrt_psum, c)
                    ps = W[:, 7, 0:NT * P].rearrange("p (t h a c) -> p t h a c", t=NT, h=4, a=2)
                    rotate(ps[:, :, :, 0, :], ps[:, :, :, 1, :], qr_nat[:, :, :, 0:HR], qr_nat[:, :, :, HR:ROPE],
                           [NT, 4], 3 * (c + 1)).then_inc(qr_ready, 1)
                    dve.wait_ge(q_psum, QUADS + c + 1)
                    if c == 0:
                        dve.wait_ge(x_ready, NT * B_LN)
                    if c >= 2:
                        dve.wait_ge(s_psum, 3 * (QUADS + c - 1))
                    upper_heads(qh[0:DH, c % 2, 1:4:2, :], 0, q_upper)
                    dve.wait_ge(qrt_psum, c + 1)
                    for j in range(2, 4):
                        op = nc.vector.tensor_copy(qh[NOPE:QW, c % 2, j, :], W[j * ROPE:(j + 1) * ROPE, 7, S:2 * S])
                    op.then_inc(qr_dve, 1)
                    if c:
                        copy_pt(QUADS + c - 1)
                    if c:
                        finish(c - 1, BQ + 2 * c + 1 + LOOKAHEAD)
                    maxima(QUADS + c, lambda j: causal_s[:, :])
                    dve.wait_ge(s_masked, QUADS + c + 1)
                    nc.vector.tensor_scalar(negm[:, :, :], smax[:, :, :], -MLA_SCALE, None, ALU.mult).then_inc(negm_ready, 1)

                def finish_last():
                    copy_pt(2 * QUADS - 1)
                    finish(QUADS - 1, BO + LOOKAHEAD)

                last_quad(T_BO, BO, finish_last)

            rests_to(0)
            units_plain(T_X, LN_BANKS)
            rests_to(LOOKAHEAD - 1)
            ffn(0)
            layer_norm(0, True)
            mixer_a()
            layer_norm(A_LN, False)
            ffn(1)
            layer_norm(2, True)
            rests_to(FFN2 + 2)
            ffn(2)
            layer_norm(3, True)
            mixer_b()
            layer_norm(B_LN, False)
            ffn(3)
            layer_norm(LNS - 1, True)
            dve.wait_ge(gb_in, 32 * LNS)
            for t in range(NT):
                dve.wait_ge(xhat_ready, 2 * (NT * (LNS - 1) + t + 1))
                nc.vector.tensor_tensor(r[:, t, :], r[:, t, :], gb[:, 0, :], ALU.mult).then_inc(fin_step, 1)
                dve.wait_ge(fin_step, t + 1)
                nc.vector.tensor_tensor(r[:, t, :], r[:, t, :], gb[:, 1, :], ALU.add).then_inc(out_ready, 1)


def p_bank(step):
    return 0 if step % QUADS == QUADS - 1 else 7


DEN = [2 * (s + 1) for s in range(QUADS)] + [2 * QUADS + s + 1 for s in range(QUADS)]
ISQ_LN = [2 * l if l < B_LN else 2 * l + 2 for l in range(LNS)]
ISQ_RMS = [2 * B_LN, 2 * B_LN + 1]
LN_SEQ = {l: i for i, l in enumerate(sorted(T_LN))}

_INS = ["x", "ffn1_w_gu", "ffn1_w_down", "ffn2_w_gu", "ffn2_w_down", "ln_g", "ln_b",
        "a_w_in", "a_sinks", "a_w_o", "b_w_in", "b_q_norm", "b_w_uq", "b_kv_norm", "b_w_ukv", "b_w_o"]


def shape_constants():
    q = np.arange(P)[:, None]
    k = np.arange(2 * P)[None, :]
    dist = q + P - k
    window = np.where((dist >= 0) & (dist < P), -dist, NEG).astype(np.float32)
    causal = np.where(dist >= 0, 0.0, NEG).astype(np.float32)
    inv = np.float32(10000.0) ** (-np.arange(0, ROPE, 2, dtype=np.float32) / np.float32(ROPE))
    ang = np.arange(S, dtype=np.float32)[:, None] * inv[None, :].astype(np.float32)
    table = np.stack([np.cos(ang), np.sin(ang)], axis=1).astype(np.float32)
    return {"identity": np.eye(P, dtype=np.float32), "window": window, "causal": causal, "rope_tab": table}


def kernel(**inputs):
    import concourse.bacc as _bacc
    from concourse.bass_utils import run_bass_kernel_spmd as _run

    nc = _bacc.Bacc("TRN2", target_bir_lowering=False, num_devices=1)
    arrays, args = {}, []
    given = {name: np.ascontiguousarray(inputs[name]) for name in _INS}
    for name, a in {**given, **shape_constants()}.items():
        arrays[f"in_{name}_dram"] = a
        args.append(nc.dram_tensor(f"in_{name}_dram", a.shape, mybir.dt.from_np(a.dtype), kind="ExternalInput").ap())
    args.append(nc.dram_tensor("out_0_dram", (1, S, D), F32, kind="ExternalOutput").ap())
    trunk_kernel(nc, *args)
    r = _run(nc, [arrays], core_ids=[0])
    return r.results[0]["out_0_dram"]
```

```python
from contextlib import ExitStack

import numpy as np

import concourse.bass as bass
from concourse import mybir

F32 = mybir.dt.float32
F32R = mybir.dt.float32r
ALU = mybir.AluOpType
ACT = mybir.ActivationFunctionType

P = 128
D = 1024
S = 256
NT = S // P
KD = D // P
FF = 2816
NFT = FF // P
NFI = NFT // 2
ALPHA = (2.0 * 2) ** 0.25
LN_EPS, RMS_EPS, NEG = 1e-5, 1e-6, -1e30
HEADS, KV_HEADS, DH = 16, 4, 64
QLORA, KVLORA, NOPE, ROPE = 768, 256, 64, 32
HR = ROPE // 2
QW = NOPE + ROPE
QUADS = HEADS // 4
WIN_SCALE = DH ** -0.5
MLA_SCALE = QW ** -0.5

RAW_SLOTS, SPLIT_SLOTS, LOOKAHEAD, CH = 3, 6, 3, 2048

G_COL, B_COL, QN_COL, KVN_COL, N_COL = 0, 48, 96, 102, 104

FFN_CHUNKS = 3 * NFI
A_CHUNKS, B_CHUNKS, O_CHUNKS = 2 + QUADS, 5 + 2 + 2 * QUADS, KD // 2
FFN0 = 0
A0 = FFN0 + FFN_CHUNKS
AO = A0 + A_CHUNKS
FFN1 = AO + O_CHUNKS
FFN2 = FFN1 + FFN_CHUNKS
B0 = FFN2 + FFN_CHUNKS
BU = B0 + 5
BQ = BU + 2
BO = BQ + 2 * QUADS
FFN3 = BO + O_CHUNKS
CHUNKS = FFN3 + FFN_CHUNKS
FFN_BASE = [FFN0, FFN1, FFN2, FFN3]
assert BQ % 2 == 0

FFN_LN = [0, 2, 3, 5]
A_LN, B_LN = 1, 4
LNS = 6

T_X = 0
T_LN = {0: 4, 1: 12, 2: 16, 3: 20, 4: 32}
T_AO, T_CKV, T_CQ, T_BO = 8, 24, 25, 28
LN_BANKS, O_BANKS = [2, 3, 4, 5], [6, 7, 0, 1]
CKV_BANKS, CQ_BANKS = [2], [4, 5, 2]
HRING = 4
LAST = HRING
D_DONE = NFT - LAST

NAT_ORDER = ["ckv", "cq0", "cq1", "kr", "cq2"]
NAT_BANK = {"ckv": 0, "cq0": 1, "cq1": 6, "kr": 3, "cq2": 7}


def trunk_kernel(nc, x, ffn1_w_gu, ffn1_w_down, ffn2_w_gu, ffn2_w_down, ln_g, ln_b,
                 a_w_in, a_sinks, a_w_o, b_w_in, b_q_norm, b_w_uq, b_kv_norm, b_w_ukv, b_w_o,
                 identity, window, causal, rope_tab, out):
    with ExitStack() as ctx:
        def sb(name, shape, dt=F32):
            return ctx.enter_context(nc.sbuf_tensor(name, shape, dt))

        def sem(name):
            return ctx.enter_context(nc.semaphore(name))

        raw = sb("raw", [P, RAW_SLOTS, CH])
        hi = sb("hi", [P, SPLIT_SLOTS, CH], F32R)
        lo = sb("lo", [P, SPLIT_SLOTS, CH], F32R)
        x_nat = sb("x_nat", [P, NT, D])
        r = sb("r", [P, NT, D])
        xT_hi = sb("xT_hi", [P, KD, S], F32R)
        xT_lo = sb("xT_lo", [P, KD, S], F32R)
        h_hi = sb("h_hi", [P, HRING, S], F32R)
        h_lo = sb("h_lo", [P, HRING, S], F32R)
        work = sb("work", [P, 5120])
        kv = sb("kv", [P, 6144])
        ident = sb("ident", [P, P])
        window_s = sb("window_s", [P, 2 * P])
        causal_s = sb("causal_s", [P, 2 * P])
        rope_s = sb("rope_s", [P, NT, 2, HR])
        cols = sb("cols", [P, N_COL])
        nsink = sb("nsink", [P, HEADS])
        bn = sb("bn", [P, NT, 2, 6])
        mv = sb("mv", [P, NT, 2])
        inv_v = sb("inv_v", [P, NT])
        inv_s = sb("inv_s", [P, NT])
        inv_e = sb("inv_e", [P, NT])
        inv_t = sb("inv_t", [P, NT])
        rstd = sb("rstd", [P, NT])
        eps_col = sb("eps_col", [P, 3])
        warm = sb("warm", [P, 1])
        smax = sb("smax", [P, NT, 4])
        negm = sb("negm", [P, NT, 4])
        rsum = sb("rsum", [P, NT, 4])
        esink = sb("esink", [P, NT, 4])
        rden = sb("rden", [P, NT, 4])
        msq = sb("msq", [P, 2, NT])

        gb = work[:, 0:2 * D].rearrange("p (a d) -> p a d", a=2)
        sil = work[:, 2048:2560].rearrange("p (a n) -> p a n", a=2)
        hf = work[:, 2560:3072].rearrange("p (a n) -> p a n", a=2)
        xf = work[:, 4096:5120].rearrange("p (a k n) -> p a k n", a=2, k=4)
        prow = work[:, 0:P]
        qh = work[:, 0:2048].rearrange("p (a h n) -> p a h n", a=2, h=4)
        pT = work[:, 2048:3584].rearrange("p (i n) -> p i n", i=12)
        sc = work[:, 3584:5120].rearrange("p (h n) -> p h n", h=4)
        c_nat = work[:, 2048:4096].rearrange("p (t d) -> p t d", t=NT)
        rope_t = r[:, 0, 512:1024].rearrange("p (a t h c) -> p a t h c", a=2, t=NT, h=8)
        qr_nat = r[:, 1, 512:1024].rearrange("p (t h c) -> p t h c", t=NT, h=8)
        kr_nat = r[:, 0, 0:NT * ROPE].rearrange("p (t c) -> p t c", t=NT)
        kr_T = r[0:ROPE, 1, 0:S]
        alibi = kv[:, 0:4096].rearrange("p (h n) -> p h n", h=HEADS)
        khA = kv[:, 4096:5120].rearrange("p (h n) -> p h n", h=KV_HEADS)
        vA = kv[:, 5120:5632].rearrange("p (t d) -> p t d", t=NT)
        khB = kv[:, 0:4096].rearrange("p (h n) -> p h n", h=HEADS)
        junk = kv[:, 0:NT * QLORA].rearrange("p (t d) -> p t d", t=NT)
        vB = kv[:, 4096:6144].rearrange("p (t d) -> p t d", t=NT)

        W = ctx.enter_context(nc.psum_tensor("banks", [P, 8, 512], F32))

        raw_in = [sem(f"raw_in{i}") for i in range(RAW_SLOTS)]
        half_in = sem("half_in")
        half_hi = sem("half_hi")
        half_lo = sem("half_lo")
        hi_done = sem("hi_done")
        lo_done = sem("lo_done")
        x_in = [sem(f"x_in{t}") for t in range(NT)]
        ident_in = sem("ident_in")
        rows_in = sem("rows_in")
        const_in = sem("const_in")
        gb_in = sem("gb_in")
        cols_tr = sem("cols_tr")
        cols_ready = sem("cols_ready")
        alibi_ready = sem("alibi_ready")
        sink_neg = sem("sink_neg")
        gu_ready = sem("gu_ready")
        sil_ready = sem("sil_ready")
        hidden_tr = sem("hidden_tr")
        hf_ready = sem("hf_ready")
        hhi_ready = sem("hhi_ready")
        hlo_ready = sem("hlo_ready")
        d_done = sem("d_done")
        y_ready = sem("y_ready")
        ln_step = sem("ln_step")
        isq_dve = sem("isq_dve")
        isq_act = sem("isq_act")
        eps_ready = sem("eps_ready")
        rstd_ready = sem("rstd_ready")
        xhat_ready = sem("xhat_ready")
        pool_step = sem("pool_step")
        x_ready = sem("x_ready")
        fin_step = sem("fin_step")
        fin_pool = sem("fin_pool")
        out_pool = sem("out_pool")
        out_dve = sem("out_dve")
        out_done = sem("out_done")
        tr_ready = sem("tr_ready")
        xf_ready = sem("xf_ready")
        xf_last = sem("xf_last")
        thi_ready = sem("thi_ready")
        tlo_ready = sem("tlo_ready")
        k_psum, k_lower, k_upper = sem("k_psum"), sem("k_lower"), sem("k_upper")
        v_psum, v_out0, v_out1 = sem("v_psum"), sem("v_out0"), sem("v_out1")
        q_psum, q_lower, q_upper = sem("q_psum"), sem("q_lower"), sem("q_upper")
        s_psum = sem("s_psum")
        s_masked = sem("s_masked")
        negm_ready = sem("negm_ready")
        es_arg = sem("es_arg")
        es_ready = sem("es_ready")
        p_ready = sem("p_ready")
        pt_psum = sem("pt_psum")
        pt_dve, pt_act = sem("pt_dve"), sem("pt_act")
        den_step = sem("den_step")
        o_psum = sem("o_psum")
        o_out = sem("o_out")
        wo_done = sem("wo_done")
        nat_psum = sem("nat_psum")
        nat_out = sem("nat_out")
        msq_ready = sem("msq_ready")
        c_norm = sem("c_norm")
        rope_step = sem("rope_step")
        kr_out = sem("kr_out")
        krn_psum = sem("krn_psum")
        kr_rotated = sem("kr_rotated")
        krt_psum = sem("krt_psum")
        kr_first = sem("kr_first")
        kr_all = sem("kr_all")
        qr_psum = sem("qr_psum")
        qr_ready = sem("qr_ready")
        qrt_psum = sem("qrt_psum")
        qr_act, qr_dve = sem("qr_act"), sem("qr_dve")

        def consumed(n):
            for f, base in enumerate(FFN_BASE):
                if base <= n < base + FFN_CHUNKS:
                    i, c = divmod(n - base, 3)
                    if c < 2:
                        return gu_ready, NFT * f + 2 * i + 2
                    if i < NFI - 2:
                        return d_done, D_DONE * f + 2 * i + 2
                    return y_ready, 2 * NT * (FFN_LN[f] + 1)
            if n == A0:
                return k_psum, 1
            if n == A0 + 1:
                return v_psum, 1
            if n < AO:
                return q_psum, n - A0 - 1
            if n < FFN1:
                return (wo_done, 1) if n == AO else (y_ready, 2 * NT * (A_LN + 1))
            if n < BU:
                return nat_psum, n - B0 + 1
            if n < BQ:
                return v_psum, 1 + 2 * (n - BU + 1)
            if n < BO:
                return q_psum, QUADS + (n - BQ) // 2 + 1
            return (wo_done, 2) if n == BO else (y_ready, 2 * NT * (B_LN + 1))

        def size(n):
            if n == B0 + NAT_ORDER.index("kr"):
                return KD * ROPE
            if BQ <= n < BO:
                return (QLORA // P) * 2 * QW
            return CH

        def parts(n, at):
            m, split = size(n), at[0] is not raw
            row = at[0][:, at[1], 0:m]
            if BU <= n < BQ:
                how = "p (k a h d) -> p k a h d" if split else "p (k h a d) -> p k a h d"
                v = row.rearrange(how, a=2, d=DH, k=KVLORA // P)
                return [v[:, k, :, :, :] for k in range(KVLORA // P)]
            if BQ <= n < BO:
                v = row.rearrange("p (k c) -> p k c", k=QLORA // P)
                if split:
                    return [v[:, :, 0:2 * NOPE].rearrange("p k (h d) -> p k h d", h=2),
                            v[:, :, 2 * NOPE:2 * QW].rearrange("p k (h d) -> p k h d", h=2)]
                v = v.rearrange("p k (h c) -> p k h c", h=2)
                return [v[:, :, :, 0:NOPE], v[:, :, :, NOPE:QW]]
            return [row]

        block = ctx.enter_context(nc.Block())

        @block.sync
        def _(sp):
            def place(n, sl):
                def cols_of(w, k, a, width):
                    return w.rearrange("(k p) f -> p k f", p=P)[:, :, a:a + width], "p (k f) -> p k f", k

                if n < AO:
                    w = a_w_in[0]
                    c = n - A0
                    a = {0: D, 1: D + KV_HEADS * DH}[c] if c < 2 else (c - 2) * 4 * DH
                    src, how, k = cols_of(w, KD, a, 4 * DH)
                elif n < FFN1 or BO <= n < FFN3:
                    w, c = (a_w_o, n - AO) if n < FFN1 else (b_w_o, n - BO)
                    src = w[0].rearrange("(k p) f -> p k f", p=P)[:, 2 * c:2 * c + 2, :]
                    how, k = "p (k f) -> p k f", 2
                elif n < BU:
                    part = NAT_ORDER[n - B0]
                    a, wd = {"ckv": (QLORA, KVLORA), "kr": (QLORA + KVLORA, ROPE)}.get(
                        part, (256 * int(part[2]) if part[0:2] == "cq" else 0, 256))
                    src, how, k = cols_of(b_w_in[0], KD, a, wd)
                elif n < BQ:
                    src, how, k = cols_of(b_w_ukv[0], KVLORA // P, (n - BU) * D, D)
                else:
                    src, how, k = cols_of(b_w_uq[0], QLORA // P, (n - BQ) * 2 * QW, 2 * QW)
                return src, raw[:, sl, 0:size(n)].rearrange(how, k=k)

            def load(n):
                if n >= RAW_SLOTS:
                    sp.wait_ge(lo_done, n - RAW_SLOTS + 1)
                src, dst = place(n, n % RAW_SLOTS)
                sp.dma_start(dst, src).then_inc(raw_in[n % RAW_SLOTS], 16)

            def load_ffn(f, i, n, p=None):
                w_gu = (ffn1_w_gu, ffn2_w_gu)[f % 2][f // 2].rearrange("(k p) f -> p k f", p=P)
                w_d = (ffn1_w_down, ffn2_w_down)[f % 2][f // 2].rearrange("(i j p) f -> i p j f", p=P, j=2)
                for c in range(3):
                    if n + c >= RAW_SLOTS:
                        more = 0 if p is None else 6 * p
                        sp.wait_ge(lo_done, n + c - RAW_SLOTS + 1 + more)
                    sl = (n + c) % RAW_SLOTS
                    if c < 2:
                        at = c * FF + 256 * i if p is None else 512 * p + (c * FF + 256 * i)
                        src = w_gu[:, :, bass.ds(at, 256)]
                        dst = raw[:, sl, :].rearrange("p (k f) -> p k f", k=KD)
                    else:
                        src = w_d[i] if p is None else w_d[bass.ds(2 * p + i, 1)].rearrange("a p j f -> (a p) j f")
                        dst = raw[:, sl, :].rearrange("p (k f) -> p k f", k=2)
                    sp.dma_start(dst, src).then_inc(raw_in[sl], 16)

            def load_first(c, ks=slice(None), signal=None):
                dst = raw[:, c, :].rearrange("p (k f) -> p k f", k=KD if c < 2 else 2)
                src = (ffn1_w_gu[0].rearrange("(k p) f -> p k f", p=P)[:, :, c * FF:c * FF + 256] if c < 2 else
                       ffn1_w_down[0].rearrange("(i j p) f -> i p j f", p=P, j=2)[0])
                sp.dma_start(dst[:, ks, :], src[:, ks, :]).then_inc(signal or raw_in[c], 16)

            def load_gb(l):
                for a, w in enumerate((ln_g, ln_b)):
                    sp.dma_start(gb[:, a, :], w[l // 3, l % 3:l % 3 + 1, :].to_broadcast([P, D])).then_inc(gb_in, 16)

            def ffn_loads(f):
                base = FFN_BASE[f]
                load_ffn(f, 0, base)
                with sp.Fori(0, NFI // 2) as p:
                    load_ffn(f, 1, base + 3, p)
                    load_ffn(f, 2, base + 6, p)

            sp.dma_start(ident[:, :], identity).then_inc(ident_in, 16)
            load_first(0, slice(0, KD // 2), half_in)
            sp.dma_start(x_nat[:, 0, :], x[0, 0:P, :]).then_inc(x_in[0], 16)
            load_first(0, slice(KD // 2, KD), raw_in[0])
            sp.dma_start(x_nat[:, 1, :], x[0, P:2 * P, :]).then_inc(x_in[1], 16)
            load_first(1)
            for w, at, n in ((ln_g, G_COL, 48), (ln_b, B_COL, 48)):
                sp.dma_start(prow[at:at + n, :], w.rearrange("a b (k p) -> (a b k) p", p=P)).then_inc(rows_in, 16)
            sp.dma_start(prow[QN_COL:QN_COL + 6, :], b_q_norm.rearrange("a (k p) -> (a k) p", p=P)).then_inc(rows_in, 16)
            sp.dma_start(prow[KVN_COL:KVN_COL + 2, :], b_kv_norm.rearrange("a (k p) -> (a k) p", p=P)).then_inc(rows_in, 16)
            load_first(2)
            with sp.Fori(0, NFI // 2) as p:
                load_ffn(0, 1, 3, p)
                load_ffn(0, 2, 6, p)
            sp.wait_ge(cols_ready, 1)
            load_gb(0)
            sp.dma_start(window_s[:, :], window).then_inc(const_in, 16)
            sp.dma_start(causal_s[:, :], causal).then_inc(const_in, 16)
            sp.dma_start(rope_s[:, :, :, :], rope_tab.rearrange("(t p) a c -> p t a c", p=P)).then_inc(const_in, 16)
            sp.dma_start(nsink[:, :], a_sinks.to_broadcast([P, HEADS])).then_inc(const_in, 16)
            for n in range(A0, FFN1):
                load(n)
            sp.wait_ge(s_psum, 3 * QUADS)
            load_gb(A_LN)
            for f in (1, 2):
                ffn_loads(f)
                sp.wait_ge(x_ready, NT * FFN_LN[f])
                load_gb(FFN_LN[f])
            for n in range(B0, FFN3):
                load(n)
            sp.wait_ge(s_psum, 6 * QUADS)
            load_gb(B_LN)
            ffn_loads(3)
            sp.wait_ge(x_ready, NT * (B_LN + 1))
            load_gb(FFN_LN[3])
            for t in range(NT):
                for a in range(2):
                    sp.wait_ge((out_pool, out_dve)[t], a + 1)
                    half = slice(a * 512, (a + 1) * 512)
                    sp.dma_start(out[0, t * P:(t + 1) * P, half], r[:, t, half]).then_inc(out_done, 16)
            sp.wait_ge(out_done, 16 * 2 * NT)

        @block.gpsimd
        def _(pool):
            for a, eps in enumerate((LN_EPS, 4 * LN_EPS, RMS_EPS)):
                e = nc.gpsimd.memset(eps_col[:, a:a + 1], eps)
            e.then_inc(eps_ready, 1)
            pool.wait_ge(const_in, 16 * 4)
            for h in range(HEADS):
                slope = 2.0 ** (-8.0 * (h + 1) / HEADS) / WIN_SCALE
                a = nc.gpsimd.tensor_scalar(alibi[:, h, :], window_s[:, :], slope, None, ALU.mult)
            a.then_inc(alibi_ready, 1)
            nc.gpsimd.tensor_scalar(nsink[:, :], nsink[:, :], -1.0, None, ALU.mult).then_inc(sink_neg, 1)

            def rebuild_x(l):
                u = T_LN[l] + 2
                pool.wait_ge(thi_ready, u)
                pool.wait_ge(tlo_ready, u - 1)
                nc.gpsimd.tensor_tensor(xT_lo[:, 4:8, 0:P], xf[:, 1, :, :], xT_hi[:, 4:8, 0:P],
                                        ALU.subtract).then_inc(tlo_ready, 1)
                pool.wait_ge(tlo_ready, u)
                pool.wait_ge(gb_in, 32 * (l + 1))
                for t in range(NT):
                    pool.wait_ge(xhat_ready, 2 * (NT * l + t + 1))
                    nc.gpsimd.tensor_tensor(x_nat[:, t, :], r[:, t, :], gb[:, 0, :], ALU.mult).then_inc(pool_step, 1)
                    pool.wait_ge(pool_step, NT * l + t + 1)
                    nc.gpsimd.tensor_tensor(x_nat[:, t, :], x_nat[:, t, :], gb[:, 1, :], ALU.add).then_inc(x_ready, 1)

            for l in range(B_LN):
                rebuild_x(l)
            pool.wait_ge(x_ready, NT * B_LN)
            pool.wait_ge(kr_first, 1)
            src = khB[NOPE:QW, 0:1, :].to_broadcast([ROPE, HEADS - 1, S])
            nc.gpsimd.tensor_copy(khB[NOPE:QW, 1:HEADS, :], src).then_inc(kr_all, 1)
            pool.wait_ge(kr_all, 1)
            rebuild_x(B_LN)
            pool.wait_ge(gb_in, 32 * LNS)
            pool.wait_ge(x_ready, NT * (B_LN + 1))
            for a in range(2):
                half = slice(a * 512, (a + 1) * 512)
                pool.wait_ge(xhat_ready, 2 * NT * (LNS - 1) + a + 1)
                nc.gpsimd.tensor_tensor(r[:, 0, half], r[:, 0, half], gb[:, 0, half], ALU.mult).then_inc(fin_pool, 1)
                pool.wait_ge(fin_pool, a + 1)
                nc.gpsimd.tensor_tensor(r[:, 0, half], r[:, 0, half], gb[:, 1, half], ALU.add).then_inc(out_pool, 1)

        @block.tensor
        def _(pe):
            def mm3(dst, a_hi, a_lo, b_hi, b_lo, first, last):
                pe.matmul(dst, a_hi, b_hi, start=first, stop=False)
                pe.matmul(dst, a_hi, b_lo, start=False, stop=False)
                return pe.matmul(dst, a_lo, b_hi, start=False, stop=last)

            def weights(sl, a, n):
                return hi[:, sl, a:a + n], lo[:, sl, a:a + n]

            def transpose_unit(src, t, q):
                for k in range(4):
                    tr = pe.transpose(W[:, LN_BANKS[2 * t + q], k * P:(k + 1) * P],
                                      src[:, t, (4 * q + k) * P:(4 * q + k + 1) * P], ident[:, :])
                tr.then_inc(tr_ready, 1)

            def transpose_outputs(q):
                for t in range(NT):
                    for k in range(4):
                        tr = pe.transpose(W[:, O_BANKS[NT * q + t], k * P:(k + 1) * P],
                                          r[:, t, (4 * q + k) * P:(4 * q + k + 1) * P], ident[:, :])
                    tr.then_inc(tr_ready, 1)

            def transpose_pairs(src, tiles, banks, waits):
                for t in range(NT):
                    waits(t)
                    for k in range(tiles):
                        tr = pe.transpose(W[:, banks[k // 2], (k % 2) * S + t * P:(k % 2) * S + (t + 1) * P],
                                          src(t, k), ident[:, :])
                        if t == NT - 1 and k % 2:
                            tr.then_inc(tr_ready, 1)

            def after_ln(l, t, units=range(2)):
                for q in units if l in T_LN else ():
                    pe.wait_ge(xhat_ready, 2 * (NT * l + t) + q + 1)
                    transpose_unit(r, t, q)

            def unit_wait(units, t, k):
                if k % 4 == 0:
                    pe.wait_ge(tlo_ready, units + 2 * t + k // 4 + 1)

            def natural_part(f, half, t, units):
                n = FFN_BASE[f] + half
                if n:
                    pe.wait_ge(lo_done, n + 1)
                for k in range(KD):
                    if n == 0 and k == 0:
                        pe.wait_ge(half_lo, 1)
                    if n == 0 and k == KD // 2:
                        pe.wait_ge(lo_done, 1)
                    if half == 0:
                        unit_wait(units, t, k)
                    wh, wl = weights(n % SPLIT_SLOTS, k * 256, 256)
                    mm = mm3(W[:, t, half * S:(half + 1) * S], xT_hi[:, k, t * P:(t + 1) * P], xT_lo[:, k, t * P:(t + 1) * P],
                             wh, wl, k == 0, k == KD - 1)
                if half:
                    mm.then_inc(gu_ready, 1)

            def transpose_hidden(f):
                for t in range(NT):
                    pe.wait_ge(hf_ready, NFT * f + t + 1)
                    for j in range(2):
                        tr = pe.transpose(W[:, 2, j * S + t * P:j * S + (t + 1) * P], hf[:, t, j * P:(j + 1) * P], ident[:, :])
                tr.then_inc(hidden_tr, 1)

            def gate_up(f, t, sl, n, tp=0, np_=0):
                pe.wait_ge(hf_ready, NFT * f + t - 1 + tp)
                for half in range(2):
                    pe.wait_ge(lo_done, n + half + 1 + np_)
                    for k in range(KD):
                        wh, wl = weights(sl[half], k * 256 + (t % 2) * P, P)
                        mm = mm3(W[:, t % 2, half * S:(half + 1) * S], wh, wl, xT_hi[:, k, :], xT_lo[:, k, :],
                                 k == 0, k == KD - 1)
                mm.then_inc(gu_ready, 1)

            def down(t, sl, tt, first, last, halves=range(2)):
                for c in halves:
                    wh, wl = weights(sl, (t % 2) * D + c * 512, 512)
                    mm = mm3(W[:, 4 + 2 * tt + c, :], h_hi[:, t % HRING, tt * P:(tt + 1) * P],
                             h_lo[:, t % HRING, tt * P:(tt + 1) * P], wh, wl, first, last)
                return mm

            def down_both(f, t, sl, n, first, tp=0, np_=0):
                pe.wait_ge(hlo_ready, NFT * f + t + 1 + tp)
                pe.wait_ge(lo_done, n + 1 + np_)
                for tt in range(NT):
                    mm = down(t, sl, tt, first, False)
                mm.then_inc(d_done, 1)

            def ffn(f, units, before=None):
                base = FFN_BASE[f]

                def step(i, p=None):
                    n = base + 3 * i
                    tp, np_ = (0, 0) if p is None else (4 * p, 6 * p)
                    s0 = [(n + c) % SPLIT_SLOTS for c in range(3)]
                    gate_up(f, 2 * i, s0, n, tp, np_)
                    if i > 1 and i < NFI - 1:
                        down_both(f, 2 * i - 1, (n - 1) % SPLIT_SLOTS, n - 1, False, tp, np_)
                    if i == 1:
                        transpose_hidden(f)
                    gate_up(f, 2 * i + 1, s0, n, tp, np_)
                    if i == 1:
                        for t in range(2):
                            down_both(f, t, (n - 1) % SPLIT_SLOTS, n - 1, t == 0)
                    if 2 * i < NFT - LAST:
                        down_both(f, 2 * i, s0[2], n + 2, False, tp, np_)

                if f == 0:
                    pe.wait_ge(ident_in, 16)
                    for t in range(NT):
                        pe.wait_ge(x_in[t], 16)
                        for q in range(2):
                            transpose_unit(x_nat, t, q)
                natural_part(f, 0, 0, units)
                if f == 0:
                    pe.wait_ge(rows_in, 64)
                    pe.transpose(W[:, 7, 0:N_COL], prow[0:N_COL, :], ident[0:N_COL, 0:N_COL]).then_inc(cols_tr, 1)
                else:
                    after_ln(before, 1)
                for half, t in ((0, 1), (1, 0), (1, 1)) if f == 0 else ((1, 0), (0, 1), (1, 1)):
                    natural_part(f, half, t, units)
                step(1)
                with pe.Fori(0, NFI // 2 - 2) as p:
                    step(2, p)
                    step(3, p)
                for i in range(NFI - 3, NFI):
                    step(i)
                for tt in range(NT):
                    for half in range(2):
                        for t in range(NFT - LAST, NFT):
                            m = base + 3 * (t // 2) + 2
                            if tt == 0 and half == 0:
                                pe.wait_ge(hlo_ready, NFT * f + t + 1)
                                pe.wait_ge(lo_done, m + 1)
                            mm = down(t, m % SPLIT_SLOTS, tt, False, t == NFT - 1, [half])
                            if tt and half and t >= NFT - 3 and t < NFT - 1:
                                after_ln(FFN_LN[f], 0, [t - NFT + 3])
                        mm.then_inc(y_ready, 1)

            def two_tiles(at, kt, ah, al, bank):
                for j in range(2):
                    for k in range(kt):
                        wh, wl = at(j, k)
                        mm = mm3(W[:, bank, j * S:(j + 1) * S], wh, wl, ah[:, k, :], al[:, k, :], k == 0, k == kt - 1)
                return mm

            def plain_tiles(n):
                return lambda j, k: weights(n % SPLIT_SLOTS, k * 256 + j * P, P)

            def natural(n, width, kt, ah, al, bank, tiles=range(NT), wait=None):
                for t in tiles:
                    for k in range(kt):
                        if wait is not None:
                            wait(k)
                        wh, wl = weights(n % SPLIT_SLOTS, k * width, width)
                        mm = mm3(W[:, bank, t * width:(t + 1) * width], ah[:, k, t * P:(t + 1) * P],
                                 al[:, k, t * P:(t + 1) * P], wh, wl, k == 0, k == kt - 1)
                return mm

            def scores(step, kh, head, rows):
                a = step % 2
                for j in range(4):
                    mm = pe.matmul(W[:, 4 + j // 2, (j % 2) * S:(j % 2 + 1) * S], qh[0:rows, a, j, P:S],
                                   kh[0:rows, head(j), :], start=True, stop=True)
                    if j % 2:
                        mm.then_inc(s_psum, 1)
                for j in range(4):
                    mm = pe.matmul(W[:, 6, j * P:(j + 1) * P], qh[0:rows, a, j, 0:P],
                                   kh[0:rows, head(j), 0:P], start=True, stop=True)
                mm.then_inc(s_psum, 1)

            def transpose_p(step, rotated=0):
                if step % QUADS:
                    pe.wait_ge(pt_dve, step)
                    pe.wait_ge(pt_act, 2 * step)
                transpose_upper(step)
                transpose_lower(step, rotated)

            def transpose_upper(step):
                pe.wait_ge(p_ready, 2 * step + 1)
                for j in range(4):
                    for kb in range(2):
                        tr = pe.transpose(W[:, 2 + j // 2, (j % 2) * S + kb * P:(j % 2) * S + (kb + 1) * P],
                                          sc[:, j, P + kb * P:P + (kb + 1) * P], ident[:, :])
                    if j % 2:
                        tr.then_inc(pt_psum, 1)

            def transpose_lower(step, rotated=0):
                pe.wait_ge(p_ready, 2 * step + 2)
                if rotated:
                    pe.wait_ge(qr_act, rotated)
                    pe.wait_ge(qr_dve, rotated)
                for j in range(4):
                    tr = pe.transpose(W[:, p_bank(step), j * P:(j + 1) * P], sc[:, j, 0:P], ident[:, :])
                tr.then_inc(pt_psum, 1)

            def attend(step, v, col):
                pe.wait_ge(pt_dve, step + 1)
                pe.wait_ge(pt_act, 2 * step + 2)
                if step % QUADS:
                    pe.wait_ge(o_out, step)
                for j in range(4):
                    vj = v[:, :, col(j):col(j) + DH]
                    pe.matmul(W[:, 1, 256 + j * DH:256 + (j + 1) * DH], pT[:, 2 * j, :], vj[:, 0, :], start=True, stop=False)
                    pe.matmul(W[:, 1, 256 + j * DH:256 + (j + 1) * DH], pT[:, 2 * j + 1, :], vj[:, 1, :], start=False, stop=True)
                    mm = pe.matmul(W[:, 1, j * DH:(j + 1) * DH], pT[:, 8 + j, :], vj[:, 0, :], start=True, stop=True)
                mm.then_inc(o_psum, 1)

            def last_quad(l, base, units, first_step, attend_last):
                def part(c, t, halves=range(2)):
                    n = base + c
                    pe.wait_ge(lo_done, n + 1)
                    pe.wait_ge(tlo_ready, units + NT * (c // 2) + t + 1)
                    for k in range(2):
                        for half in halves:
                            wh, wl = weights(n % SPLIT_SLOTS, k * D + half * 512, 512)
                            mm = mm3(W[:, 4 + 2 * t + half, :], xT_hi[:, 2 * c + k, t * P:(t + 1) * P],
                                     xT_lo[:, 2 * c + k, t * P:(t + 1) * P], wh, wl,
                                     c == 0 and k == 0, c == O_CHUNKS - 1 and k == 1)
                    return mm

                last = first_step + QUADS - 1
                pe.wait_ge(o_out, last)
                pe.wait_ge(s_masked, last + 1)
                transpose_outputs(0)
                transpose_upper(last)
                part(0, 0)
                transpose_lower(last)
                part(0, 1).then_inc(wo_done, 1)
                attend_last()
                part(1, 0, [0])
                pe.wait_ge(o_out, last + 1)
                transpose_outputs(1)
                part(1, 0, [1])
                for t in range(NT):
                    for half in range(2):
                        for c in range(2 - t, O_CHUNKS):
                            mm = part(c, t, [half])
                            if t and half and c < 3:
                                after_ln(l, 0, [c - 1])
                        mm.then_inc(y_ready, 1)

            def mixer_a():
                for t in range(NT):
                    pe.wait_ge(lo_done, A0 + 2)
                    mm = natural(A0 + 1, 256, KD, xT_hi, xT_lo, 1, [t], lambda k: unit_wait(T_LN[0], t, k))
                    if t == 0:
                        after_ln(0, 1)
                mm.then_inc(v_psum, 1)
                pe.wait_ge(lo_done, A0 + 1)
                two_tiles(plain_tiles(A0), KD, xT_hi, xT_lo, 7).then_inc(k_psum, 1)

                def project_q(c):
                    if c:
                        pe.wait_ge(q_lower, c)
                        pe.wait_ge(q_upper, c)
                    n = A0 + 2 + c
                    pe.wait_ge(lo_done, n + 1)
                    two_tiles(plain_tiles(n), KD, xT_hi, xT_lo, 0).then_inc(q_psum, 1)

                def score(c):
                    pe.wait_ge(q_lower, c + 1)
                    pe.wait_ge(q_upper, c + 1)
                    if c:
                        pe.wait_ge(s_masked, c)
                    else:
                        pe.wait_ge(k_lower, 1)
                        pe.wait_ge(k_upper, 1)
                    scores(c, khA, lambda j: c, DH)

                project_q(0)
                score(0)
                for c in range(QUADS - 1):
                    project_q(c + 1)
                    transpose_p(c)
                    score(c + 1)
                    if c == 0:
                        pe.wait_ge(v_out0, 1)
                    attend(c, vA, lambda j: c * DH)
                last_quad(A_LN, AO, T_AO, 0, lambda: attend(QUADS - 1, vA, lambda j: (QUADS - 1) * DH))

            def mixer_b():
                kt_q, kt_kv = QLORA // P, KVLORA // P
                for t in range(NT):
                    for c in range(2):
                        if t == 0 and c == 1:
                            after_ln(3, 1)
                        pe.wait_ge(lo_done, B0 + c + 1)
                        mm = natural(B0 + c, 256, KD, xT_hi, xT_lo, NAT_BANK[NAT_ORDER[c]], [t],
                                     lambda k: unit_wait(T_LN[3], t, k))
                        if t == NT - 1:
                            mm.then_inc(nat_psum, 1)
                for c in range(2, 5):
                    part = NAT_ORDER[c]
                    pe.wait_ge(lo_done, B0 + c + 1)
                    if part == "kr":
                        for k in range(KD):
                            wh, wl = weights((B0 + c) % SPLIT_SLOTS, k * ROPE, ROPE)
                            mm = mm3(W[0:ROPE, 3, 0:S], wh, wl, xT_hi[:, k, :], xT_lo[:, k, :], k == 0, k == KD - 1)
                    else:
                        mm = natural(B0 + c, 256, KD, xT_hi, xT_lo, NAT_BANK[part])
                    mm.then_inc(nat_psum, 1)
                    if c == 2:
                        transpose_pairs(lambda t, k: c_nat[:, t, QLORA + k * P:QLORA + (k + 1) * P], kt_kv, CKV_BANKS,
                                        lambda t: pe.wait_ge(c_norm, t + 1))
                pe.wait_ge(kr_out, 1)
                for t in range(NT):
                    tr = pe.transpose(W[:, 3, S + t * ROPE:S + (t + 1) * ROPE], kr_T[:, t * P:(t + 1) * P], ident[0:ROPE, 0:ROPE])
                tr.then_inc(krn_psum, 1)
                pe.wait_ge(tlo_ready, T_CKV + 1)
                for u in range(2):
                    n, sl = BU + u, (BU + u) % SPLIT_SLOTS
                    pe.wait_ge(lo_done, n + 1)

                    def head_cols(ring, k, h, part, count):
                        at = k * D + part * 8 * DH + h * DH
                        return ring[:, sl, at:at + count * DH]

                    for b in range(2):
                        if u:
                            pe.wait_ge(k_lower, 1 + b + 1)
                            pe.wait_ge(k_upper, 1 + b + 1)
                        else:
                            pe.wait_ge(nat_out, b + 1)
                        mm = two_tiles(lambda j, k: (head_cols(hi, k, 4 * b + 2 * j, 0, 2), head_cols(lo, k, 4 * b + 2 * j, 0, 2)),
                                       kt_kv, h_hi, h_lo, b)
                        mm.then_inc(k_psum, 1)
                    for t in range(NT):
                        if u:
                            pe.wait_ge((v_out0, v_out1)[t], 2 - t)
                        else:
                            pe.wait_ge(nat_out, (3, 4)[t])
                        for k in range(kt_kv):
                            mm = mm3(W[:, 6 + t, :], h_hi[:, k, t * P:(t + 1) * P], h_lo[:, k, t * P:(t + 1) * P],
                                     head_cols(hi, k, 0, 1, 8), head_cols(lo, k, 0, 1, 8), k == 0, k == kt_kv - 1)
                        mm.then_inc(v_psum, 1)
                    if u == 0:
                        pe.wait_ge(kr_rotated, 1)
                        for t in range(NT):
                            tr = pe.transpose(W[0:ROPE, 3, t * P:(t + 1) * P], kr_nat[:, t, :], ident[:, :])
                        tr.then_inc(krt_psum, 1)
                        transpose_pairs(lambda t, k: c_nat[:, t, k * P:(k + 1) * P], kt_q, CQ_BANKS,
                                        lambda t: pe.wait_ge(c_norm, NT + t + 1))

                def project_q(c):
                    if c == 0:
                        pe.wait_ge(tlo_ready, T_CQ + 3)
                        pe.wait_ge(v_out1, 2)
                    else:
                        pe.wait_ge(pt_act, 2 * (QUADS + c - 1))
                    if c % 2 == 0:
                        s0 = (BQ + 2 * c) % SPLIT_SLOTS
                        assert s0 + 4 <= SPLIT_SLOTS
                        pe.wait_ge(lo_done, BQ + 2 * c + 4)
                        for t in range(NT):
                            for k in range(kt_q):
                                wh, wl = (ring[:, s0:s0 + 4, k * 2 * QW + 2 * NOPE:(k + 1) * 2 * QW] for ring in (hi, lo))
                                mm = mm3(W[:, 7, t * S:(t + 1) * S], xT_hi[:, k, t * P:(t + 1) * P],
                                         xT_lo[:, k, t * P:(t + 1) * P], wh, wl, k == 0, k == kt_q - 1)
                        mm.then_inc(qr_psum, 1)
                    if c == 0:
                        pe.wait_ge(k_lower, 4)
                        pe.wait_ge(k_upper, 4)
                    else:
                        pe.wait_ge(q_lower, QUADS + c)
                        pe.wait_ge(q_upper, QUADS + c)
                    for j in range(2):
                        for k in range(kt_q):
                            wh, wl = weights((BQ + 2 * c + j) % SPLIT_SLOTS, k * 2 * QW, 2 * NOPE)
                            mm = mm3(W[:, 0, j * S:(j + 1) * S], wh, wl, xT_hi[:, k, :], xT_lo[:, k, :], k == 0, k == kt_q - 1)
                    mm.then_inc(q_psum, 1)
                    pe.wait_ge(qr_ready, c // 2 + 1)
                    h = 4 * (c % 2)
                    for t in range(NT):
                        tr = pe.transpose(W[:, 7, S + t * P:S + (t + 1) * P],
                                          qr_nat[:, t, h:h + 4, :].rearrange("p h d -> p (h d)"), ident[:, :])
                    tr.then_inc(qrt_psum, 1)

                def score(c):
                    pe.wait_ge(q_lower, QUADS + c + 1)
                    pe.wait_ge(q_upper, QUADS + c + 1)
                    pe.wait_ge(qr_act, c + 1)
                    pe.wait_ge(qr_dve, c + 1)
                    if c:
                        pe.wait_ge(s_masked, QUADS + c)
                    else:
                        pe.wait_ge(k_lower, 5)
                        pe.wait_ge(k_upper, 5)
                        pe.wait_ge(kr_all, 1)
                    scores(QUADS + c, khB, lambda j: 4 * c + j, QW)

                project_q(0)
                score(0)
                for c in range(QUADS - 1):
                    project_q(c + 1)
                    transpose_p(QUADS + c, c + 2)
                    score(c + 1)
                    if c == 0:
                        pe.wait_ge(v_out0, 3)
                    attend(QUADS + c, vB, lambda j: (4 * c + j) * DH)
                last_quad(B_LN, BO, T_BO, QUADS, lambda: attend(2 * QUADS - 1, vB, lambda j: (4 * QUADS - 4 + j) * DH))

            ffn(0, T_X)
            mixer_a()
            ffn(1, T_LN[1], A_LN)
            ffn(2, T_LN[2], 2)
            mixer_b()
            ffn(3, T_LN[4], B_LN)

        @block.scalar
        def _(act):
            nxt = [0]

            def round_chunk(n, p=None, free=None):
                more = 0 if p is None else 2 * p
                act.wait_ge(raw_in[n % RAW_SLOTS], 16 * (n // RAW_SLOTS + 1) + 16 * more)
                if n >= SPLIT_SLOTS:
                    who, value = consumed(n - SPLIT_SLOTS)
                    act.wait_ge(who, value if p is None else value + 4 * p)
                for src, dst in zip(parts(n, (raw, n % RAW_SLOTS)), parts(n, (hi, n % SPLIT_SLOTS))):
                    op = nc.scalar.copy(dst, src)
                op.then_inc(hi_done, 1)

            def rounds_to(n):
                while nxt[0] <= min(n, CHUNKS - 1):
                    round_chunk(nxt[0])
                    nxt[0] += 1

            def hidden(f, t, tp=0):
                act.wait_ge(gu_ready, NFT * f + t + 1 + tp)
                nc.scalar.activation(sil[:, t % 2, :], W[:, t % 2, 0:S], ACT.Silu).then_inc(sil_ready, 1)
                act.wait_ge(hf_ready, NFT * f + t + 1 + tp)
                if t >= HRING:
                    act.wait_ge(d_done, D_DONE * f + t - HRING + 1 + tp)
                nc.scalar.copy(h_hi[:, t % HRING, :], hf[:, t % 2, :]).then_inc(hhi_ready, 1)

            def hidden_natural(f, t):
                act.wait_ge(gu_ready, NFT * f + t + 1)
                nc.scalar.activation(sil[:, t, :], W[:, t, 0:S], ACT.Silu).then_inc(sil_ready, 1)

            def ffn(f):
                base = FFN_BASE[f]

                def step(i, p=None):
                    n, tp = base + 3 * i, 0 if p is None else 4 * p
                    if i == 0:
                        hidden_natural(f, 0)
                    for c in range(3):
                        if n + LOOKAHEAD + c < min(base + FFN_CHUNKS + 2, CHUNKS):
                            round_chunk(n + LOOKAHEAD + c, p)
                        if i == 0 and c == 1:
                            hidden_natural(f, 1)
                        if i == 1 and c == 0:
                            act.wait_ge(hidden_tr, f + 1)
                            nc.scalar.copy(h_hi[:, 0:2, :], W[:, 2, :].rearrange("p (j n) -> p j n", j=2)).then_inc(hhi_ready, 2)
                        if i and c != 1:
                            hidden(f, 2 * i + c // 2, tp)

                load_table(ACT.Silu)
                step(0)
                step(1)
                with act.Fori(0, NFI // 2 - 1) as p:
                    step(2, p)
                    step(3, p)
                step(NFI - 1)
                nxt[0] = base + FFN_CHUNKS + 2

            def load_table(func):
                nc.scalar.activation(warm[:, :], eps_col[:, 0:1], func)

            def square_root(e, v, at, eps):
                nc.scalar.activation(inv_s[:, at], v, ACT.Sqrt, bias=eps_col[:, eps:eps + 1]).then_inc(isq_act, 1)

            def layer_norm(l):
                load_table(ACT.Sqrt)

                def root(t):
                    act.wait_ge(ln_step, 4 * (NT * l + t) + 4)
                    square_root(ISQ_LN[l] + t, mv[:, t, 1:2], slice(t, t + 1), 1 if l in FFN_LN else 0)

                def affine(t, q):
                    act.wait_ge(tr_ready, T_LN[l] + 2 * t + q + 1)
                    if t:
                        act.wait_ge(tlo_ready, T_LN[l] + 1)
                    for k in range(4):
                        c = l * KD + 4 * q + k
                        op = nc.scalar.activation(xf[:, q, k, :], W[:, LN_BANKS[2 * t + q], k * P:(k + 1) * P], ACT.Identity,
                                                  bias=cols[:, B_COL + c:B_COL + c + 1], scale=cols[:, G_COL + c:G_COL + c + 1])
                    op.then_inc(xf_ready, 1)

                def round_unit(t, q):
                    if t and q:
                        act.wait_ge(xf_last, LN_SEQ[l] + 1)
                    else:
                        act.wait_ge(xf_ready, 3 * LN_SEQ[l] + 2 * t + q + 1)
                    nc.scalar.copy(xT_hi[:, 4 * q:4 * q + 4, t * P:(t + 1) * P], xf[:, q, :, :]).then_inc(thi_ready, 1)

                root(0)
                if l not in T_LN:
                    root(1)
                    return
                affine(0, 0)
                round_unit(0, 0)
                affine(0, 1)
                if l in FFN_LN:
                    root(1)
                round_unit(0, 1)
                if l not in FFN_LN:
                    root(1)
                rounds_to(NEXT[l] + 2)
                affine(1, 0)
                round_unit(1, 0)
                round_unit(1, 1)

            def units_plain(t0, banks, units):
                for u in units:
                    t, q = divmod(u, 2)
                    act.wait_ge(tr_ready, t0 + u + 1)
                    nc.scalar.copy(xT_hi[:, 4 * q:4 * q + 4, t * P:(t + 1) * P],
                                   W[:, banks[u], :].rearrange("p (k n) -> p k n", k=4)).then_inc(thi_ready, 1)

            def pairs_scaled(t0, n, banks, dst, col):
                for p in range(n):
                    act.wait_ge(tr_ready, t0 + p + 1)
                    for k in range(2):
                        c = col + 2 * p + k
                        op = nc.scalar.mul(dst[:, 2 * p + k, :], W[:, banks[p], k * S:(k + 1) * S], cols[:, c:c + 1])
                    op.then_inc(thi_ready, 1)

            def lower_heads(dst, bank, done):
                nc.scalar.copy(dst, W[0:DH, bank, :].rearrange("p (j n) -> p j n", j=2)).then_inc(done, 1)

            def exps(step, scale, sinks, between=None):
                act.wait_ge(negm_ready, step + 1)
                for t in (1, 0):
                    if t == 0 and between:
                        between()
                    for j in range(4):
                        s = sc[:, j, P:3 * P] if t else sc[:, j, 0:P]
                        op = nc.scalar.activation(s, s, ACT.Exp, bias=negm[:, t, j:j + 1], scale=scale,
                                                  accum_out=rsum[:, t, j:j + 1])
                    op.then_inc(p_ready, 1)
                if sinks:
                    act.wait_ge(es_arg, step + 1)
                    nc.scalar.activation(esink[:, :, :], esink[:, :, :], ACT.Exp).then_inc(es_ready, 1)

            def copy_pt(step):
                if step:
                    act.wait_ge(o_psum, step)
                for b, (bank, at) in enumerate(((3, 4), (p_bank(step), 8))):
                    act.wait_ge(pt_psum, 3 * step + 2 + b)
                    nc.scalar.copy(pT[:, at:at + 4, :], W[:, bank, :].rearrange("p (i n) -> p i n", i=4)).then_inc(pt_act, 1)

            def output_units(t0, q):
                for t in range(NT):
                    u = NT * q + t
                    act.wait_ge(tr_ready, t0 + u + 1)
                    nc.scalar.copy(xT_hi[:, 4 * q:4 * q + 4, t * P:(t + 1) * P],
                                   W[:, O_BANKS[u], :].rearrange("p (k n) -> p k n", k=4)).then_inc(thi_ready, 1)

            def last_quad(t0, base, step):
                copy_pt(step)
                rounds_to(base + LOOKAHEAD)
                output_units(t0, 1)
                for c in range(1, O_CHUNKS - 1):
                    rounds_to(base + c + LOOKAHEAD)

            def mixer_a():
                rounds_to(A0 + LOOKAHEAD)
                act.wait_ge(k_psum, 1)
                lower_heads(khA[0:DH, 0:KV_HEADS:2, :], 7, k_lower)
                rounds_to(A0 + 1 + LOOKAHEAD)
                for c in range(QUADS):
                    act.wait_ge(q_psum, c + 1)
                    if c == 0:
                        act.wait_ge(x_ready, NT * A_LN)
                    if c >= 2:
                        act.wait_ge(s_psum, 3 * (c - 1))
                    lower_heads(qh[0:DH, c % 2, 0:4:2, :], 0, q_lower)
                    if c:
                        copy_pt(c - 1)
                    else:
                        load_table(ACT.Exp)
                    rounds_to(A0 + 2 + c + LOOKAHEAD)
                    exps(c, WIN_SCALE, True, (lambda: output_units(T_AO, 0)) if c == QUADS - 1 else None)
                last_quad(T_AO, AO, QUADS - 1)

            def mixer_b():
                rounds_to(B0 + LOOKAHEAD)
                rounds_to(B0 + 1 + LOOKAHEAD)

                def squares(a, first, width, after):
                    act.wait_ge(nat_out, after)
                    for t in range(NT):
                        op = nc.scalar.activation(junk[:, t, 0:width], c_nat[:, t, first:first + width], ACT.Square,
                                                  scale=float(width) ** -0.5, accum_out=msq[:, a, t:t + 1])
                    op.then_inc(msq_ready, 1)
                    act.wait_ge(msq_ready, a + 1)
                    square_root(ISQ_RMS[a], msq[:, a, :], slice(0, NT), 2)

                squares(0, QLORA, KVLORA, 1)
                rounds_to(B0 + 2 + LOOKAHEAD)
                pairs_scaled(T_CKV, 1, CKV_BANKS, h_hi, KVN_COL)
                rounds_to(B0 + 4 + LOOKAHEAD)
                act.wait_ge(nat_psum, 4)
                act.wait_ge(x_ready, NT * B_LN)
                nc.scalar.copy(kr_T, W[0:ROPE, 3, 0:S]).then_inc(kr_out, 1)
                squares(1, 0, QLORA, 4)
                for u in range(2):
                    rounds_to(BU + u + LOOKAHEAD)
                    for b in range(2):
                        act.wait_ge(k_psum, 1 + 2 * u + b + 1)
                        h = 8 * u + 4 * b
                        lower_heads(khB[0:DH, h:h + 4:2, :], b, k_lower)
                    act.wait_ge(v_psum, 1 + 2 * u + 1)
                    nc.scalar.copy(vB[:, 0, u * 512:(u + 1) * 512], W[:, 6, :]).then_inc(v_out0, 1)
                    if u == 0:
                        pairs_scaled(T_CQ, 3, CQ_BANKS, xT_hi, QN_COL)
                        act.wait_ge(krt_psum, 1)
                        nc.scalar.copy(khB[NOPE:QW, 0, :], W[0:ROPE, 3, 0:S]).then_inc(kr_first, 1)
                rounds_to(BQ + 2 + LOOKAHEAD)
                for c in range(QUADS):
                    act.wait_ge(q_psum, QUADS + c + 1)
                    if c == 0:
                        act.wait_ge(x_ready, NT * B_LN)
                    if c >= 2:
                        act.wait_ge(s_psum, 3 * (QUADS + c - 1))
                    lower_heads(qh[0:DH, c % 2, 0:4:2, :], 0, q_lower)
                    act.wait_ge(qrt_psum, c + 1)
                    for j in range(2):
                        op = nc.scalar.copy(qh[NOPE:QW, c % 2, j, :], W[j * ROPE:(j + 1) * ROPE, 7, S:2 * S])
                    op.then_inc(qr_act, 1)
                    if c:
                        copy_pt(QUADS + c - 1)
                    if c == 0:
                        load_table(ACT.Exp)
                    rounds_to(BQ + 7 + c)
                    exps(QUADS + c, MLA_SCALE, False, (lambda: output_units(T_BO, 0)) if c == QUADS - 1 else None)
                last_quad(T_BO, BO, 2 * QUADS - 1)

            act.wait_ge(eps_ready, 1)
            load_table(ACT.Silu)
            act.wait_ge(half_in, 16)
            nc.scalar.copy(hi[:, 0, 0:CH // 2], raw[:, 0, 0:CH // 2]).then_inc(half_hi, 1)
            units_plain(T_X, LN_BANKS, range(0, 2))
            act.wait_ge(raw_in[0], 16)
            nc.scalar.copy(hi[:, 0, CH // 2:CH], raw[:, 0, CH // 2:CH]).then_inc(hi_done, 1)
            nxt[0] = 1
            units_plain(T_X, LN_BANKS, range(2, 4))
            rounds_to(LOOKAHEAD - 1)
            act.wait_ge(cols_tr, 1)
            nc.scalar.copy(cols[:, :], W[:, 7, 0:N_COL]).then_inc(cols_ready, 1)
            ffn(0)
            act.wait_ge(cols_ready, 1)
            layer_norm(0)
            mixer_a()
            layer_norm(A_LN)
            ffn(1)
            layer_norm(2)
            ffn(2)
            layer_norm(3)
            mixer_b()
            layer_norm(B_LN)
            ffn(3)
            layer_norm(LNS - 1)

        @block.vector
        def _(dve):
            nxt = [0]

            def rest_of_chunk(n, p=None):
                dve.wait_ge(hi_done, n + 1 if p is None else n + 1 + 6 * p)
                sl = n % SPLIT_SLOTS
                for src, top, dst in zip(parts(n, (raw, n % RAW_SLOTS)), parts(n, (hi, sl)), parts(n, (lo, sl))):
                    op = nc.vector.tensor_tensor(dst, src, top, ALU.subtract)
                op.then_inc(lo_done, 1)

            def rests_to(n):
                while nxt[0] <= min(n, CHUNKS - 1):
                    rest_of_chunk(nxt[0])
                    nxt[0] += 1

            def hidden(f, t, tp=0):
                dve.wait_ge(sil_ready, NFT * f + t + 1 + tp)
                nc.vector.tensor_tensor(hf[:, t % 2, :], sil[:, t % 2, :], W[:, t % 2, S:2 * S], ALU.mult).then_inc(hf_ready, 1)

            def hidden_rest(f, t, tp=0):
                dve.wait_ge(hhi_ready, NFT * f + t + 1 + tp)
                nc.vector.tensor_tensor(h_lo[:, t % HRING, :], hf[:, t % 2, :], h_hi[:, t % HRING, :], ALU.subtract).then_inc(hlo_ready, 1)

            def ffn(f):
                base = FFN_BASE[f]

                def step(i, p=None):
                    n, tp = base + 3 * i + LOOKAHEAD, 0 if p is None else 4 * p
                    if i == 0:
                        hidden(f, 0)
                        rest_of_chunk(n)
                        rest_of_chunk(n + 1)
                        hidden(f, 1)
                        rest_of_chunk(n + 2)
                        return
                    if n < CHUNKS:
                        rest_of_chunk(n, p)
                    if i == 1:
                        dve.wait_ge(hhi_ready, NFT * f + 2)
                        nc.vector.tensor_tensor(h_lo[:, 0:2, :], W[:, 2, :].rearrange("p (j n) -> p j n", j=2),
                                                h_hi[:, 0:2, :], ALU.subtract).then_inc(hlo_ready, 2)
                    hidden(f, 2 * i, tp)
                    if n < CHUNKS:
                        rest_of_chunk(n + 1, p)
                    hidden_rest(f, 2 * i, tp)
                    if i < NFI - 1:
                        rest_of_chunk(n + 2, p)
                    hidden(f, 2 * i + 1, tp)
                    hidden_rest(f, 2 * i + 1, tp)

                step(0)
                step(1)
                with dve.Fori(0, NFI // 2 - 1) as p:
                    step(2, p)
                    step(3, p)
                step(NFI - 1)
                nxt[0] = base + FFN_CHUNKS + 2

            def inverse_sqrt(e, v, eps, at, meanwhile=None):
                nc.vector.tensor_scalar(inv_v[:, at], v, eps, None, ALU.add).then_inc(isq_dve, 1)
                if meanwhile:
                    meanwhile()
                dve.wait_ge(isq_act, e + 1)
                nc.vector.reciprocal(inv_e[:, at], inv_s[:, at]).then_inc(isq_dve, 1)
                dve.wait_ge(isq_dve, 4 * e + 2)
                for t in range(at.start, at.stop):
                    op = nc.vector.scalar_tensor_tensor(out=inv_t[:, t:t + 1], in0=inv_e[:, t:t + 1], scalar=inv_v[:, t:t + 1],
                                                        in1=inv_e[:, t:t + 1], op0=ALU.mult, op1=ALU.mult)
                op.then_inc(isq_dve, 1)
                dve.wait_ge(isq_dve, 4 * e + 3)
                nc.vector.tensor_scalar(inv_t[:, at], inv_t[:, at], -0.5, 1.5, ALU.mult, ALU.add).then_inc(isq_dve, 1)
                dve.wait_ge(isq_dve, 4 * e + 4)
                nc.vector.tensor_tensor(rstd[:, at], inv_e[:, at], inv_t[:, at], ALU.mult).then_inc(rstd_ready, 1)
                dve.wait_ge(rstd_ready, e + 1)

            def layer_norm(l, ffn_before):
                two = 2.0 if ffn_before else 1.0
                for t in range(NT):
                    s0 = 4 * (NT * l + t)
                    if l:
                        dve.wait_ge(x_ready, NT * (l - 1) + t + 1)
                    else:
                        dve.wait_ge(x_in[t], 16)
                    for a in range(2):
                        half = slice(a * 512, (a + 1) * 512)
                        dve.wait_ge(y_ready, 2 * (NT * l + t) + a + 1)
                        nc.vector.scalar_tensor_tensor(out=r[:, t, half], in0=x_nat[:, t, half], scalar=two * ALPHA,
                                                       in1=W[:, 4 + 2 * t + a, :], op0=ALU.mult, op1=ALU.add).then_inc(ln_step, 1)
                        dve.wait_ge(ln_step, s0 + a + 1)
                        op = nc.vector.bn_stats(bn[:, t, a, :], r[:, t, half])
                    op.then_inc(ln_step, 1)
                    if t and l in T_LN:
                        rest_of_unit(l, 0)
                    dve.wait_ge(ln_step, s0 + 3)
                    nc.vector.bn_aggr(mv[:, t, :], bn[:, t, :, :].rearrange("p a s -> p (a s)")).then_inc(ln_step, 1)
                    dve.wait_ge(ln_step, s0 + 4)
                    if l == LNS - 1 and t:
                        result(mv[:, t, 0:1], two * two * LN_EPS)
                        return
                    inverse_sqrt(ISQ_LN[l] + t, mv[:, t, 1:2], two * two * LN_EPS, slice(t, t + 1))
                    for a in range(2):
                        half = slice(a * 512, (a + 1) * 512)
                        nc.vector.tensor_scalar(r[:, t, half], r[:, t, half], mv[:, t, 0:1], rstd[:, t:t + 1],
                                                ALU.subtract, ALU.mult).then_inc(xhat_ready, 1)
                if l in T_LN:
                    rests_to(NEXT[l] + 2)
                    dve.wait_ge(tr_ready, T_LN[l] + 4)
                    dve.wait_ge(tlo_ready, T_LN[l] + 2)
                    for k in range(4):
                        c = l * KD + 4 + k
                        op = nc.vector.tensor_scalar(xf[:, 1, k, :], W[:, LN_BANKS[3], k * P:(k + 1) * P],
                                                     cols[:, G_COL + c:G_COL + c + 1], cols[:, B_COL + c:B_COL + c + 1],
                                                     ALU.mult, ALU.add)
                    op.then_inc(xf_last, 1)
                    rest_of_unit(l, 2)
                    rest_of_unit(l, 3)

            def result(mean, eps):
                def centre():
                    dve.wait_ge(gb_in, 32 * LNS)
                    for a in range(2):
                        half = slice(a * 512, (a + 1) * 512)
                        nc.vector.scalar_tensor_tensor(out=r[:, 1, half], in0=r[:, 1, half], scalar=mean, in1=gb[:, 0, half],
                                                       op0=ALU.subtract, op1=ALU.mult).then_inc(fin_step, 1)

                inverse_sqrt(ISQ_LN[LNS - 1] + 1, mv[:, 1, 1:2], eps, slice(1, 2), centre)
                for a in range(2):
                    half = slice(a * 512, (a + 1) * 512)
                    dve.wait_ge(fin_step, a + 1)
                    nc.vector.scalar_tensor_tensor(out=r[:, 1, half], in0=r[:, 1, half], scalar=rstd[:, 1:2], in1=gb[:, 1, half],
                                                   op0=ALU.mult, op1=ALU.add).then_inc(out_dve, 1)

            def rest_of_unit(l, u):
                t, q = divmod(u, 2)
                dve.wait_ge(thi_ready, T_LN[l] + u + 1)
                at = xT_lo[:, 4 * q:4 * q + 4, t * P:(t + 1) * P]
                nc.vector.tensor_tensor(at, xf[:, q, :, :], xT_hi[:, 4 * q:4 * q + 4, t * P:(t + 1) * P],
                                        ALU.subtract).then_inc(tlo_ready, 1)

            def units_plain(t0, banks, units):
                for u in units:
                    t, q = divmod(u, 2)
                    dve.wait_ge(thi_ready, t0 + u + 1)
                    nc.vector.tensor_tensor(xT_lo[:, 4 * q:4 * q + 4, t * P:(t + 1) * P],
                                            W[:, banks[u], :].rearrange("p (k n) -> p k n", k=4),
                                            xT_hi[:, 4 * q:4 * q + 4, t * P:(t + 1) * P], ALU.subtract).then_inc(tlo_ready, 1)

            def pairs_scaled(t0, n, banks, dst, src, col):
                for p in range(n):
                    dve.wait_ge(thi_ready, t0 + p + 1)
                    for k in range(2):
                        c = col + 2 * p + k
                        op = nc.vector.scalar_tensor_tensor(out=dst[:, 2 * p + k, :], in0=W[:, banks[p], k * S:(k + 1) * S],
                                                            scalar=cols[:, c:c + 1], in1=src[:, 2 * p + k, :],
                                                            op0=ALU.mult, op1=ALU.subtract)
                    op.then_inc(tlo_ready, 1)

            def upper_heads(dst, bank, done):
                nc.vector.tensor_copy(dst, W[DH:P, bank, :].rearrange("p (j n) -> p j n", j=2)).then_inc(done, 1)

            def maxima(step, bias):
                for t in (1, 0):
                    for j in range(4):
                        if t and j % 2 == 0:
                            dve.wait_ge(s_psum, 3 * step + j // 2 + 1)
                        if t == 0 and j == 0:
                            dve.wait_ge(s_psum, 3 * step + 3)
                        if t:
                            dst, src, b = sc[:, j, P:3 * P], W[:, 4 + j // 2, (j % 2) * S:(j % 2 + 1) * S], bias(j)
                        else:
                            dst, src, b = sc[:, j, 0:P], W[:, 6, j * P:(j + 1) * P], bias(j)[:, P:2 * P]
                        op = nc.vector.tensor_tensor_reduce(out=dst, in0=src, in1=b, scale=1.0, scalar=NEG, op0=ALU.add,
                                                            op1=ALU.max, accum_out=smax[:, t, j:j + 1])
                op.then_inc(s_masked, 1)

            def copy_pt(step):
                dve.wait_ge(pt_psum, 3 * step + 1)
                nc.vector.tensor_copy(pT[:, 0:4, :], W[:, 2, :].rearrange("p (i n) -> p i n", i=4)).then_inc(pt_dve, 1)

            def normalise(step, c):
                dve.wait_ge(o_psum, step + 1)
                dve.wait_ge(den_step, DEN[step])
                if c == 0:
                    dve.wait_ge(x_ready, NT * (A_LN if step == 0 else B_LN))
                nc.vector.tensor_tensor(
                    r[:, :, c * 4 * DH:(c + 1) * 4 * DH].rearrange("p t (j d) -> p t j d", j=4),
                    W[:, 1, :].rearrange("p (t j d) -> p t j d", t=NT, j=4),
                    rden[:, :, :].unsqueeze(3).to_broadcast([P, NT, 4, DH]), ALU.mult).then_inc(o_out, 1)

            def output_units(t0, q):
                for t in range(NT):
                    u = NT * q + t
                    dve.wait_ge(thi_ready, t0 + u + 1)
                    nc.vector.tensor_tensor(xT_lo[:, 4 * q:4 * q + 4, t * P:(t + 1) * P],
                                            W[:, O_BANKS[u], :].rearrange("p (k n) -> p k n", k=4),
                                            xT_hi[:, 4 * q:4 * q + 4, t * P:(t + 1) * P], ALU.subtract).then_inc(tlo_ready, 1)

            def last_quad(t0, base, finish):
                output_units(t0, 0)
                rests_to(base - 1 + LOOKAHEAD)
                finish()
                rests_to(base + LOOKAHEAD)
                output_units(t0, 1)
                for c in range(1, O_CHUNKS - 1):
                    rests_to(base + c + LOOKAHEAD)

            def mixer_a():
                rests_to(A0 + LOOKAHEAD)
                dve.wait_ge(v_psum, 1)
                nc.vector.tensor_copy(vA[:, :, :], W[:, 1, :].rearrange("p (t d) -> p t d", t=NT)).then_inc(v_out0, 1)
                dve.wait_ge(k_psum, 1)
                upper_heads(khA[0:DH, 1:KV_HEADS:2, :], 7, k_upper)
                rests_to(A0 + 1 + LOOKAHEAD)
                dve.wait_ge(alibi_ready, 1)
                dve.wait_ge(sink_neg, 1)

                def denominators(c):
                    dve.wait_ge(es_ready, c + 1)
                    if c:
                        dve.wait_ge(o_out, c)
                    nc.vector.tensor_tensor(rden[:, :, :], rsum[:, :, :], esink[:, :, :], ALU.add).then_inc(den_step, 1)
                    dve.wait_ge(den_step, 2 * c + 1)
                    nc.vector.reciprocal(rden[:, :, :], rden[:, :, :]).then_inc(den_step, 1)
                    copy_pt(c)

                for c in range(QUADS):
                    dve.wait_ge(q_psum, c + 1)
                    if c == 0:
                        dve.wait_ge(x_ready, NT * A_LN)
                    if c >= 2:
                        dve.wait_ge(s_psum, 3 * (c - 1))
                    upper_heads(qh[0:DH, c % 2, 1:4:2, :], 0, q_upper)
                    if c:
                        denominators(c - 1)
                    maxima(c, lambda j: alibi[:, 4 * c + j, :])
                    dve.wait_ge(s_masked, c + 1)
                    sinks = nsink[:, 4 * c:4 * c + 4].unsqueeze(1).to_broadcast([P, NT, 4])
                    nc.vector.scalar_tensor_tensor(out=negm[:, :, :], in0=smax[:, :, :], scalar=-WIN_SCALE, in1=sinks,
                                                   op0=ALU.mult, op1=ALU.min).then_inc(negm_ready, 1)
                    dve.wait_ge(negm_ready, c + 1)
                    nc.vector.tensor_tensor(esink[:, :, :], negm[:, :, :], sinks, ALU.subtract).then_inc(es_arg, 1)
                    if c:
                        normalise(c - 1, c - 1)
                    if c + 1 < QUADS:
                        rests_to(A0 + 2 + c + LOOKAHEAD)

                def finish():
                    denominators(QUADS - 1)
                    normalise(QUADS - 1, QUADS - 1)

                last_quad(T_AO, AO, finish)

            def rotate(x1, x2, o1, o2, shape, start):
                heads = shape[1]
                ta = rope_t[:, 0, :, 0:heads, :]
                tb = rope_t[:, 1, :, 0:heads, :]
                cos, sin = (rope_s[:, :, a:a + 1, :].to_broadcast([P, NT, heads, HR]) for a in range(2))
                for o, (fa, fb, op) in ((o1, (cos, sin, ALU.subtract)), (o2, (sin, cos, ALU.add))):
                    nc.vector.tensor_tensor(ta, x1, fa, ALU.mult)
                    nc.vector.tensor_tensor(tb, x2, fb, ALU.mult).then_inc(rope_step, 1)
                    start += 1
                    dve.wait_ge(rope_step, start)
                    last = nc.vector.tensor_tensor(o, ta, tb, op)
                    if o is o1:
                        last.then_inc(rope_step, 1)
                        start += 1
                        dve.wait_ge(rope_step, start)
                return last

            def mixer_b():
                rests_to(B0 + LOOKAHEAD)

                def nat_copy(c):
                    part = NAT_ORDER[c]
                    at = QLORA if part == "ckv" else 256 * int(part[2])
                    dve.wait_ge(nat_psum, c + 1)
                    nc.vector.tensor_copy(c_nat[:, :, at:at + 256],
                                          W[:, NAT_BANK[part], :].rearrange("p (t d) -> p t d", t=NT)).then_inc(nat_out, 1)

                def rms(a, first, width):
                    dve.wait_ge(msq_ready, a + 1)
                    inverse_sqrt(ISQ_RMS[a], msq[:, a, :], RMS_EPS, slice(0, NT))
                    for t in range(NT):
                        nc.vector.tensor_scalar(c_nat[:, t, first:first + width], c_nat[:, t, first:first + width],
                                                rstd[:, t:t + 1], None, ALU.mult).then_inc(c_norm, 1)

                nat_copy(0)
                rms(0, QLORA, KVLORA)
                nat_copy(1)
                rests_to(B0 + 1 + LOOKAHEAD)
                nat_copy(2)
                pairs_scaled(T_CKV, 1, CKV_BANKS, h_lo, h_hi, KVN_COL)
                rests_to(B0 + 2 + LOOKAHEAD)
                rests_to(B0 + 4 + LOOKAHEAD)
                nat_copy(4)
                dve.wait_ge(krn_psum, 1)
                dve.wait_ge(x_ready, NT * B_LN)
                ps = W[:, 3, S:S + NT * ROPE].rearrange("p (t a c) -> p t a c", t=NT, a=2)
                rotate(ps[:, :, 0:1, :], ps[:, :, 1:2, :], kr_nat[:, :, 0:HR].unsqueeze(2), kr_nat[:, :, HR:ROPE].unsqueeze(2),
                       [NT, 1], 0).then_inc(kr_rotated, 1)
                rms(1, 0, QLORA)
                for u in range(2):
                    rests_to(BU + u + LOOKAHEAD)
                    for b in range(2):
                        dve.wait_ge(k_psum, 1 + 2 * u + b + 1)
                        h = 8 * u + 4 * b
                        upper_heads(khB[0:DH, h + 1:h + 4:2, :], b, k_upper)
                    dve.wait_ge(v_psum, 1 + 2 * u + 2)
                    nc.vector.tensor_copy(vB[:, 1, u * 512:(u + 1) * 512], W[:, 7, :]).then_inc(v_out1, 1)
                    if u == 0:
                        pairs_scaled(T_CQ, 3, CQ_BANKS, xT_lo, xT_hi, QN_COL)
                rests_to(BQ + 2 + LOOKAHEAD)

                def denominators(c):
                    copy_pt(QUADS + c)
                    dve.wait_ge(p_ready, 2 * (QUADS + c) + 2)
                    dve.wait_ge(o_out, QUADS + c)
                    nc.vector.reciprocal(rden[:, :, :], rsum[:, :, :]).then_inc(den_step, 1)

                for c in range(QUADS):
                    if c % 2 == 0:
                        dve.wait_ge(qr_psum, c // 2 + 1)
                        if c:
                            dve.wait_ge(qrt_psum, c)
                        ps = W[:, 7, :].rearrange("p (t h a c) -> p t h a c", t=NT, h=8, a=2)
                        rotate(ps[:, :, :, 0, :], ps[:, :, :, 1, :], qr_nat[:, :, :, 0:HR], qr_nat[:, :, :, HR:ROPE],
                               [NT, 8], 3 * (c // 2 + 1)).then_inc(qr_ready, 1)
                    dve.wait_ge(q_psum, QUADS + c + 1)
                    if c == 0:
                        dve.wait_ge(x_ready, NT * B_LN)
                    if c >= 2:
                        dve.wait_ge(s_psum, 3 * (QUADS + c - 1))
                    upper_heads(qh[0:DH, c % 2, 1:4:2, :], 0, q_upper)
                    dve.wait_ge(qrt_psum, c + 1)
                    for j in range(2, 4):
                        op = nc.vector.tensor_copy(qh[NOPE:QW, c % 2, j, :], W[j * ROPE:(j + 1) * ROPE, 7, S:2 * S])
                    op.then_inc(qr_dve, 1)
                    if c:
                        denominators(c - 1)
                    maxima(QUADS + c, lambda j: causal_s[:, :])
                    dve.wait_ge(s_masked, QUADS + c + 1)
                    nc.vector.tensor_scalar(negm[:, :, :], smax[:, :, :], -MLA_SCALE, None, ALU.mult).then_inc(negm_ready, 1)
                    if c:
                        normalise(QUADS + c - 1, c - 1)
                    if c + 1 < QUADS:
                        rests_to(BQ + 7 + c)

                def finish():
                    denominators(QUADS - 1)
                    normalise(2 * QUADS - 1, QUADS - 1)

                last_quad(T_BO, BO, finish)

            dve.wait_ge(half_hi, 1)
            nc.vector.tensor_tensor(lo[:, 0, 0:CH // 2], raw[:, 0, 0:CH // 2], hi[:, 0, 0:CH // 2],
                                    ALU.subtract).then_inc(half_lo, 1)
            units_plain(T_X, LN_BANKS, range(0, 2))
            dve.wait_ge(hi_done, 1)
            nc.vector.tensor_tensor(lo[:, 0, CH // 2:CH], raw[:, 0, CH // 2:CH], hi[:, 0, CH // 2:CH],
                                    ALU.subtract).then_inc(lo_done, 1)
            nxt[0] = 1
            units_plain(T_X, LN_BANKS, range(2, 4))
            rests_to(LOOKAHEAD - 1)
            ffn(0)
            layer_norm(0, True)
            mixer_a()
            layer_norm(A_LN, False)
            ffn(1)
            layer_norm(2, True)
            ffn(2)
            layer_norm(3, True)
            mixer_b()
            layer_norm(B_LN, False)
            ffn(3)
            layer_norm(LNS - 1, True)


def p_bank(step):
    return 0 if step % QUADS == QUADS - 1 else 7


DEN = [2 * (s + 1) for s in range(QUADS)] + [2 * QUADS + s + 1 for s in range(QUADS)]
ISQ_LN = [2 * l if l < B_LN else 2 * l + 2 for l in range(LNS)]
ISQ_RMS = [2 * B_LN, 2 * B_LN + 1]
NEXT = {0: A0, A_LN: FFN1, 2: FFN2, 3: B0, B_LN: FFN3}
LN_SEQ = {l: i for i, l in enumerate(sorted(T_LN))}

_INS = ["x", "ffn1_w_gu", "ffn1_w_down", "ffn2_w_gu", "ffn2_w_down", "ln_g", "ln_b",
        "a_w_in", "a_sinks", "a_w_o", "b_w_in", "b_q_norm", "b_w_uq", "b_kv_norm", "b_w_ukv", "b_w_o"]


def shape_constants():
    q = np.arange(P)[:, None]
    k = np.arange(2 * P)[None, :]
    dist = q + P - k
    window = np.where((dist >= 0) & (dist < P), -dist, NEG).astype(np.float32)
    causal = np.where(dist >= 0, 0.0, NEG).astype(np.float32)
    inv = np.float32(10000.0) ** (-np.arange(0, ROPE, 2, dtype=np.float32) / np.float32(ROPE))
    ang = np.arange(S, dtype=np.float32)[:, None] * inv[None, :].astype(np.float32)
    table = np.stack([np.cos(ang), np.sin(ang)], axis=1).astype(np.float32)
    return {"identity": np.eye(P, dtype=np.float32), "window": window, "causal": causal, "rope_tab": table}


def kernel(**inputs):
    import concourse.bacc as _bacc
    from concourse.bass_utils import run_bass_kernel_spmd as _run

    nc = _bacc.Bacc("TRN2", target_bir_lowering=False, num_devices=1)
    arrays, args = {}, []
    given = {name: np.ascontiguousarray(inputs[name]) for name in _INS}
    for name, a in {**given, **shape_constants()}.items():
        arrays[f"in_{name}_dram"] = a
        args.append(nc.dram_tensor(f"in_{name}_dram", a.shape, mybir.dt.from_np(a.dtype), kind="ExternalInput").ap())
    args.append(nc.dram_tensor("out_0_dram", (1, S, D), F32, kind="ExternalOutput").ap())
    trunk_kernel(nc, *args)
    r = _run(nc, [arrays], core_ids=[0])
    return r.results[0]["out_0_dram"]
```
